# Optimizing a Trainium2 kernel written in Bass

```python
import math
import jax
import jax.numpy as jnp
from jax import lax
import numpy as np

D_MODEL = 1024
BATCH = 1
SEQ = 512
DEPTH = 2

N_META = 16
S5_WIDTH = 512
S5_GROUP = 16
S5_GROUPS = S5_WIDTH // S5_GROUP
S5_STATE = 64
DT_MIN = 1e-3
DT_MAX = 1e-1
LRU_WIDTH = 512
LRU_HEADS = 8
LRU_HEAD_DIM = LRU_WIDTH // LRU_HEADS
CONV_WIDTH = 4
LRU_C = 8.0
N_BRANCH = 2
D_IN = S5_WIDTH + 2 * LRU_WIDTH + N_BRANCH * D_MODEL
DENSE_FF = 3 * D_MODEL
N_EXPERTS = 8
TOP_K = 2
EXPERT_FF = 3 * D_MODEL // 2
MOE_BLOCK = 256
N_DENSE = (DEPTH + 1) // 2
N_MOE = DEPTH // 2
EPS = 1e-6

kernel_name = "hybrid_s5_rglru_gated_moe_trunk"

def rmsnorm(x, g):
    x32 = x.astype(jnp.float32)
    y = x32 * lax.rsqrt(jnp.mean(x32 * x32, axis=-1, keepdims=True) + EPS)
    return (y * g.astype(jnp.float32)).astype(x.dtype)

def _complex_linear_combine(left, right):
    a1r, a1i, b1r, b1i = left
    a2r, a2i, b2r, b2i = right
    return (a2r * a1r - a2i * a1i,
            a2r * a1i + a2i * a1r,
            a2r * b1r - a2i * b1i + b2r,
            a2r * b1i + a2i * b1r + b2i)

def _real_linear_combine(left, right):
    a1, b1 = left
    a2, b2 = right
    return (a1 * a2, a2 * b1 + b2)

def s5_branch(u, lam_re, lam_im, log_dt, b_re, b_im, c_re, c_im, d_skip, w_glu, b_glu):
    f32 = jnp.float32
    bsz, t, _ = u.shape
    u32 = u.astype(f32)
    ug = u32.reshape(bsz, t, S5_GROUPS, S5_GROUP)
    lr = lam_re.astype(f32)
    li = lam_im.astype(f32)
    dt = jnp.exp(log_dt.astype(f32))[:, None]
    mag = jnp.exp(lr * dt)
    ab_re = mag * jnp.cos(li * dt)
    ab_im = mag * jnp.sin(li * dt)
    den = lr * lr + li * li
    num_re = ab_re - 1.0
    coef_re = (num_re * lr + ab_im * li) / den
    coef_im = (ab_im * lr - num_re * li) / den
    br = b_re.astype(f32)
    bi = b_im.astype(f32)
    bb_re = coef_re[..., None] * br - coef_im[..., None] * bi
    bb_im = coef_re[..., None] * bi + coef_im[..., None] * br
    bu_re = jnp.einsum('btgh,gph->btgp', ug, bb_re)
    bu_im = jnp.einsum('btgh,gph->btgp', ug, bb_im)
    a_re = jnp.broadcast_to(ab_re, bu_re.shape)
    a_im = jnp.broadcast_to(ab_im, bu_re.shape)
    _, _, s_re, s_im = lax.associative_scan(
        _complex_linear_combine, (a_re, a_im, bu_re, bu_im), axis=1)
    y = (jnp.einsum('btgp,ghp->btgh', s_re, c_re.astype(f32))
         - jnp.einsum('btgp,ghp->btgh', s_im, c_im.astype(f32)))
    y = y.reshape(bsz, t, S5_WIDTH) + d_skip.astype(f32) * u32
    y = jax.nn.gelu(y).astype(u.dtype)
    return y * jax.nn.sigmoid(y @ w_glu + b_glu)

def rglru_branch(xb, gate_in, conv_w, conv_b, w_r, b_r, w_i, b_i, lam):
    f32 = jnp.float32
    bsz, t, c = xb.shape
    xc = lax.conv_general_dilated(
        xb, conv_w[:, None, :], window_strides=(1,), padding=[(CONV_WIDTH - 1, 0)],
        dimension_numbers=('NWC', 'WIO', 'NWC'), feature_group_count=c) + conv_b
    x32 = xc.astype(f32)
    xh = x32.reshape(bsz, t, LRU_HEADS, LRU_HEAD_DIM)
    r = jax.nn.sigmoid(jnp.einsum('btnh,nhk->btnk', xh, w_r.astype(f32)).reshape(bsz, t, c)
                       + b_r.astype(f32))
    i = jax.nn.sigmoid(jnp.einsum('btnh,nhk->btnk', xh, w_i.astype(f32)).reshape(bsz, t, c)
                       + b_i.astype(f32))
    log_a = -LRU_C * r * jax.nn.softplus(-lam.astype(f32))
    a = jnp.exp(log_a)
    mult = jnp.sqrt(-jnp.expm1(2.0 * log_a))
    b = mult * (i * x32)
    _, h = lax.associative_scan(_real_linear_combine, (a, b), axis=1)
    return (h * jax.nn.gelu(gate_in.astype(f32))).astype(xb.dtype)

def swiglu(h, w_gate, w_up, w_down):
    return (jax.nn.silu(h @ w_gate) * (h @ w_up)) @ w_down

def moe_swiglu(x2d, router_w, router_b, w_gate, w_up, w_down):
    n, d = x2d.shape
    logits = (x2d @ router_w).astype(jnp.float32) + router_b.astype(jnp.float32)
    top_val, top_idx = lax.top_k(logits, TOP_K)
    gates = jax.nn.softmax(top_val, axis=-1)
    nk = n * TOP_K
    flat_e = top_idx.reshape(nk)
    flat_tok = jnp.arange(nk, dtype=jnp.int32) // TOP_K
    flat_g = gates.reshape(nk)
    order = jnp.argsort(flat_e, stable=True)
    sorted_e = flat_e[order]
    counts = jnp.bincount(flat_e, length=N_EXPERTS)
    padded = ((counts + MOE_BLOCK - 1) // MOE_BLOCK) * MOE_BLOCK
    cum_pad = jnp.cumsum(padded)
    pad_start = cum_pad - padded
    start = jnp.cumsum(counts) - counts
    rank = jnp.arange(nk, dtype=jnp.int32) - start[sorted_e]
    dest = pad_start[sorted_e] + rank
    n_blocks = -(-nk // MOE_BLOCK) + N_EXPERTS
    n_slots = n_blocks * MOE_BLOCK
    slot_tok = jnp.full((n_slots,), n, dtype=jnp.int32).at[dest].set(flat_tok[order])
    slot_gate = jnp.zeros((n_slots,), jnp.float32).at[dest].set(flat_g[order])
    block_start = jnp.arange(n_blocks, dtype=jnp.int32) * MOE_BLOCK
    block_expert = jnp.minimum(jnp.searchsorted(cum_pad, block_start, side='right'),
                               N_EXPERTS - 1).astype(jnp.int32)
    x_pad = jnp.concatenate([x2d, jnp.zeros((1, d), x2d.dtype)], axis=0)
    xs = x_pad[slot_tok].reshape(n_blocks, MOE_BLOCK, d)

    def expert_block(args):
        xb, e = args
        return swiglu(xb, w_gate[e], w_up[e], w_down[e])

    ys = lax.map(expert_block, (xs, block_expert)).reshape(n_slots, d)
    ys = ys * slot_gate[:, None].astype(ys.dtype)
    out = jnp.zeros((n + 1, d), ys.dtype).at[slot_tok].add(ys)
    return out[:n]

def setup_inputs(seed: int = 0) -> dict:
    key = jax.random.key(seed)
    ks = iter(jax.random.split(key, 48))
    f32 = jnp.float32

    def nrm(shape, scale):
        return jax.random.normal(next(ks), shape, f32) * scale

    x = nrm((BATCH, SEQ, D_MODEL), 1.0)
    meta_tokens = nrm((N_META, D_MODEL), 1.0)
    mix_norm = 1.0 + nrm((DEPTH, D_MODEL), 0.01)
    w_in = nrm((DEPTH, D_MODEL, D_IN), D_MODEL ** -0.5)
    merge_bias = nrm((DEPTH, N_BRANCH * D_MODEL), 0.01)
    n_idx = jnp.arange(S5_STATE, dtype=f32)
    s5_lambda_re = -0.5 + nrm((DEPTH, S5_GROUPS, S5_STATE), 0.01)
    s5_lambda_im = math.pi * n_idx + nrm((DEPTH, S5_GROUPS, S5_STATE), 0.01)
    s5_log_dt = jax.random.uniform(next(ks), (DEPTH, S5_GROUPS), f32,
                                   math.log(DT_MIN), math.log(DT_MAX))
    s5_b_re = nrm((DEPTH, S5_GROUPS, S5_STATE, S5_GROUP), (2 * S5_GROUP) ** -0.5)
    s5_b_im = nrm((DEPTH, S5_GROUPS, S5_STATE, S5_GROUP), (2 * S5_GROUP) ** -0.5)
    s5_c_re = nrm((DEPTH, S5_GROUPS, S5_GROUP, S5_STATE), (2 * S5_STATE) ** -0.5)
    s5_c_im = nrm((DEPTH, S5_GROUPS, S5_GROUP, S5_STATE), (2 * S5_STATE) ** -0.5)
    s5_d = nrm((DEPTH, S5_WIDTH), 1.0)
    s5_w_glu = nrm((DEPTH, S5_WIDTH, S5_WIDTH), S5_WIDTH ** -0.5)
    s5_b_glu = nrm((DEPTH, S5_WIDTH), 0.01)
    s5_w_proj = nrm((DEPTH, S5_WIDTH, D_MODEL), S5_WIDTH ** -0.5)
    lru_conv_w = nrm((DEPTH, CONV_WIDTH, LRU_WIDTH), CONV_WIDTH ** -0.5)
    lru_conv_b = nrm((DEPTH, LRU_WIDTH), 0.01)
    lru_w_rgate = nrm((DEPTH, LRU_HEADS, LRU_HEAD_DIM, LRU_HEAD_DIM), LRU_HEAD_DIM ** -0.5)
    lru_b_rgate = nrm((DEPTH, LRU_WIDTH), 0.01)
    lru_w_igate = nrm((DEPTH, LRU_HEADS, LRU_HEAD_DIM, LRU_HEAD_DIM), LRU_HEAD_DIM ** -0.5)
    lru_b_igate = nrm((DEPTH, LRU_WIDTH), 0.01)
    a_c = jax.random.uniform(next(ks), (DEPTH, LRU_WIDTH), f32, 0.9, 0.999)
    s = a_c ** (1.0 / LRU_C)
    lru_lambda = jnp.log(s) - jnp.log1p(-s)
    lru_w_proj = nrm((DEPTH, LRU_WIDTH, D_MODEL), LRU_WIDTH ** -0.5)
    w_out = nrm((DEPTH, D_MODEL, D_MODEL), D_MODEL ** -0.5)
    ffn_norm = 1.0 + nrm((DEPTH, D_MODEL), 0.01)
    dense_w_gate = nrm((N_DENSE, D_MODEL, DENSE_FF), D_MODEL ** -0.5)
    dense_w_up = nrm((N_DENSE, D_MODEL, DENSE_FF), D_MODEL ** -0.5)
    dense_w_down = nrm((N_DENSE, DENSE_FF, D_MODEL), DENSE_FF ** -0.5)
    router_w = nrm((N_MOE, D_MODEL, N_EXPERTS), D_MODEL ** -0.5)
    router_b = nrm((N_MOE, N_EXPERTS), 0.01)
    moe_w_gate = nrm((N_MOE, N_EXPERTS, D_MODEL, EXPERT_FF), D_MODEL ** -0.5)
    moe_w_up = nrm((N_MOE, N_EXPERTS, D_MODEL, EXPERT_FF), D_MODEL ** -0.5)
    moe_w_down = nrm((N_MOE, N_EXPERTS, EXPERT_FF, D_MODEL), EXPERT_FF ** -0.5)
    final_norm = 1.0 + nrm((D_MODEL,), 0.01)
    return {
        "x": x, "meta_tokens": meta_tokens, "mix_norm": mix_norm, "w_in": w_in,
        "merge_bias": merge_bias, "s5_lambda_re": s5_lambda_re, "s5_lambda_im": s5_lambda_im,
        "s5_log_dt": s5_log_dt, "s5_b_re": s5_b_re, "s5_b_im": s5_b_im,
        "s5_c_re": s5_c_re, "s5_c_im": s5_c_im, "s5_d": s5_d, "s5_w_glu": s5_w_glu,
        "s5_b_glu": s5_b_glu, "s5_w_proj": s5_w_proj, "lru_conv_w": lru_conv_w,
        "lru_conv_b": lru_conv_b, "lru_w_rgate": lru_w_rgate, "lru_b_rgate": lru_b_rgate,
        "lru_w_igate": lru_w_igate, "lru_b_igate": lru_b_igate, "lru_lambda": lru_lambda,
        "lru_w_proj": lru_w_proj, "w_out": w_out, "ffn_norm": ffn_norm,
        "dense_w_gate": dense_w_gate, "dense_w_up": dense_w_up, "dense_w_down": dense_w_down,
        "router_w": router_w, "router_b": router_b, "moe_w_gate": moe_w_gate,
        "moe_w_up": moe_w_up, "moe_w_down": moe_w_down, "final_norm": final_norm,
    }

def reference(x, meta_tokens, mix_norm, w_in, merge_bias, s5_lambda_re, s5_lambda_im,
              s5_log_dt, s5_b_re, s5_b_im, s5_c_re, s5_c_im, s5_d, s5_w_glu, s5_b_glu,
              s5_w_proj, lru_conv_w, lru_conv_b, lru_w_rgate, lru_b_rgate, lru_w_igate,
              lru_b_igate, lru_lambda, lru_w_proj, w_out, ffn_norm, dense_w_gate,
              dense_w_up, dense_w_down, router_w, router_b, moe_w_gate, moe_w_up,
              moe_w_down, final_norm):
    bsz = x.shape[0]
    meta = jnp.broadcast_to(meta_tokens[None].astype(x.dtype), (bsz, N_META, D_MODEL))
    hs = jnp.concatenate([meta, x], axis=1)
    t = hs.shape[1]
    o_x = S5_WIDTH
    o_g = S5_WIDTH + LRU_WIDTH
    o_m = S5_WIDTH + 2 * LRU_WIDTH
    for layer in range(DEPTH):
        hn = rmsnorm(hs, mix_norm[layer])
        z = hn @ w_in[layer]
        u_s5 = z[..., :o_x]
        x_lru = z[..., o_x:o_g]
        g_lru = z[..., o_g:o_m]
        gates = jax.nn.sigmoid(z[..., o_m:] + merge_bias[layer]).reshape(
            bsz, t, N_BRANCH, D_MODEL)
        y_a = s5_branch(u_s5, s5_lambda_re[layer], s5_lambda_im[layer], s5_log_dt[layer],
                        s5_b_re[layer], s5_b_im[layer], s5_c_re[layer], s5_c_im[layer],
                        s5_d[layer], s5_w_glu[layer], s5_b_glu[layer]) @ s5_w_proj[layer]
        y_b = rglru_branch(x_lru, g_lru, lru_conv_w[layer], lru_conv_b[layer],
                           lru_w_rgate[layer], lru_b_rgate[layer], lru_w_igate[layer],
                           lru_b_igate[layer], lru_lambda[layer]) @ lru_w_proj[layer]
        y = gates[:, :, 0, :] * y_a + gates[:, :, 1, :] * y_b
        hs = hs + y @ w_out[layer]
        hn = rmsnorm(hs, ffn_norm[layer])
        j = layer // 2
        if layer % 2 == 0:
            hs = hs + swiglu(hn, dense_w_gate[j], dense_w_up[j], dense_w_down[j])
        else:
            f = moe_swiglu(hn.reshape(bsz * t, D_MODEL), router_w[j], router_b[j],
                           moe_w_gate[j], moe_w_up[j], moe_w_down[j])
            hs = hs + f.reshape(bsz, t, D_MODEL)
    return rmsnorm(hs[:, N_META:], final_norm)


_drawn_inputs = setup_inputs


def setup_inputs(seed=0):
    import zlib

    import numpy as np

    out = dict(_drawn_inputs(seed))
    spreads = {}
    factors = {'mix_norm': 4.663,
     'merge_bias': 8.0,
     's5_lambda_re': 64.0,
     's5_b_re': 3.217,
     's5_b_im': 2.943,
     's5_c_re': 2.945,
     's5_b_glu': 64.0,
     'lru_b_rgate': 25.92,
     'lru_b_igate': 8.0,
     'router_b': 25.608,
     'final_norm': 32.335,
     's5_c_im': 3.688,
     'lru_conv_b': 3.188,
     'ffn_norm': 8.0}
    for name, (base, spread) in spreads.items():
        noise = np.random.default_rng([zlib.crc32(name.encode()), seed]).standard_normal(out[name].shape)
        drawn = base * np.exp(spread * noise) if base else spread * noise
        out[name] = jnp.asarray(drawn.astype(out[name].dtype))
    for name, factor in factors.items():
        out[name] = (out[name] * factor).astype(out[name].dtype)
    return out
```

```python
from contextlib import ExitStack

import concourse.bass as bass
from concourse import mybir

F32 = mybir.dt.float32
F32R = mybir.dt.float32r
ALU = mybir.AluOpType
ACT = mybir.ActivationFunctionType
AX_X = mybir.AxisListType.X

P = 128
D = 1024
DK = D // P
META = 16
T = 512 + META
TH = T // 2
LAYERS = 2
W5 = 512
MT = W5 // P
GROUPS, GC, GS = 32, 16, 64
L = P // GC
NC = T // L
GB = 4
NB = GROUPS // GB
PADW = (2 * L - 1) * GC
SP2 = LAYERS * GROUPS
FF = 1536
FT = FF // P
EXPERTS = 8
TOK = 88
TB = T // TOK
EPS = 1e-6
LRU_C = 8.0

UNIT = 8 * P
RING = 3
U_IN = 28
U_GLU = 2
U_MIX = U_IN + U_GLU + 8 + 8
U_FF = 3 * FT
STEP = 6
UNITS = LAYERS * U_MIX + (2 + EXPERTS) * U_FF
ACC_MIX, ACC_FF = 28, 16

COLS, _at = {}, 0
for _name, _n in (("mix_norm", 8), ("ffn_norm", 8), ("merge_bias", 16), ("conv_w", 16), ("conv_b", 4),
                  ("b_r", 4), ("b_i", 4), ("lam", 4), ("b_glu", 4), ("s5_d", 32), ("final_norm", 4)):
    COLS[_name] = (_at, _n)
    _at += LAYERS * _n
NCOL = _at


def build(nc, xT, W, cols_d, s5p, s5m, wg, rw, rb, out, hs_d, u_d, y_d, g_d):
    ctx = ExitStack()
    with ctx:
        cursor = [16512]

        def region(nbytes):
            start = cursor[0]
            cursor[0] += (nbytes + 31) // 32 * 32
            return start

        def place(name, shape, dt=F32, at=None):
            n = 4
            for s in shape[1:]:
                n *= s
            if at is None:
                start = region(n)
            else:
                start = at[0]
                at[0] += (n + 31) // 32 * 32
                assert at[0] <= at[1], name
            return nc.alloc_sbuf_tensor_at(name, shape, dt, offset=start)

        def shared(nbytes):
            start = region(nbytes)
            return lambda: [start, start + nbytes]

        def sem(name):
            return ctx.enter_context(nc.semaphore(name))

        H = shared(4 * 2 * DK * T)
        h = H()
        hs = place("hs", [P, DK, T], at=h)
        hn = place("hn", [P, DK, T], at=h)
        gates = place("gates", [P, 2 * DK, T], at=H())
        xh = place("xh", [P, DK, T], F32R)
        xl = place("xl", [P, DK, T], F32R)
        raw = [place(f"raw{i}", [P, UNIT]) for i in range(RING)]
        wh = [place(f"wh{i}", [P, UNIT], F32R) for i in range(RING)]
        wl = [place(f"wl{i}", [P, UNIT], F32R) for i in range(RING)]
        FFR = shared(4 * 2 * FT * T)
        f = FFR()
        fh = place("fh", [P, FT, T], F32R, at=f)
        fl = place("fl", [P, FT, T], F32R, at=f)
        f = FFR()
        y1h = place("y1h", [P, MT, T], F32R, at=f)
        y1l = place("y1l", [P, MT, T], F32R, at=f)
        y2h = place("y2h", [P, MT, T], F32R, at=f)
        y2l = place("y2l", [P, MT, T], F32R, at=f)
        ybh = place("ybh", [P, MT, T], F32R, at=f)
        ybl = place("ybl", [P, MT, T], F32R, at=f)
        start = FFR()[0]
        f = [start, start + 4 * 4 * MT * T]
        m1 = place("m1", [P, GB, P], at=f)
        m1y = place("m1y", [P, GB, P], at=f)
        m2 = place("m2", [P, GB, P], at=f)
        m2y = place("m2y", [P, GB, P], at=f)
        m3 = place("m3", [P, GB, P], at=f)
        m1t = place("m1t", [P, GB, PADW], at=f)
        cosT = place("cosT", [P, GB, NC], at=f)
        sinT = place("sinT", [P, GB, NC], at=f)
        decay = place("decay", [P, GB, NC], at=f)
        rot = place("rot", [P, GB, NC], at=f)
        rot2 = place("rot2", [P, GB, NC], at=f)
        turned = place("turned", [P, GB, NC], at=f)
        cr = place("cr", [P, GB, NC], at=f)
        sr = place("sr", [P, GB, NC], at=f)
        pbuf = place("pbuf", [P, 2, 4, GB * GC], at=f)
        b2s = place("b2s", [P, GB, GC], at=f)
        bx = place("bx", [P, GB, GC], at=f)
        by = place("by", [P, GB, GC], at=f)
        c1 = place("c1", [P, GB, GC], at=f)
        c2 = place("c2", [P, GB, GC], at=f)
        pt1 = place("pt1", [P, GB * P], at=f)
        pt2 = place("pt2", [P, GB * P], at=f)
        dt1 = place("dt1", [P, GB * P], at=f)
        LR = shared(4 * (14 * T + T + 3 + 8))
        f = LR()
        xc = place("xc", [P, MT, T], at=f)
        gg = place("gg", [P, MT, T], at=f)
        ra = place("ra", [P, 2, T], at=f)
        ii = place("ii", [P, 2, T], at=f)
        th = place("th", [P, 2, T], at=f)
        xpad = place("xpad", [P, T + 3], at=f)
        uperm = place("uperm", [P, MT, L, NC], at=[LR()[0] + 4 * 8 * T, LR()[1]])
        f = LR()
        gt = place("gt", [P, 2, T], at=f)
        ft = place("ft", [P, 2, T], at=f)
        gbc = place("gbc", [P, EXPERTS, T], at=f)
        f = LR()
        pp = {n: place("p_" + n, [P, SP2], at=f) for n in
              ("lr", "li", "ldt", "dt", "ang", "k", "red", "red2", "sin", "cos", "mag", "num", "den",
               "rden", "t1", "t2", "t3")}
        tri = place("tri", [P, EXPERTS, EXPERTS], at=f)

        UU = shared(4 * GROUPS * NC)
        uu = place("uu", [P, GROUPS, NC], at=UU())
        yt = place("yt", [P, MT, L, NC], at=UU())
        ys = place("ys", [P, 2, GB, NC])
        rs = place("rs", [P, T], at=[LR()[0] + 4 * 8 * T, LR()[1]])
        cols = place("cols", [P, NCOL])
        apr = place("apr", [P, L + 1, SP2])
        api = place("api", [P, L + 1, SP2])
        sqr = place("sqr", [P, 7, SP2])
        sqi = place("sqi", [P, 7, SP2])
        mag8 = place("mag8", [P, SP2])
        cfr = place("cfr", [P, SP2])
        cfi = place("cfi", [P, SP2])
        sp8 = place("sp8", [P, LAYERS * MT])
        sp8n = place("sp8n", [P, LAYERS * MT])
        spt = [place(f"spt{i}", [P, LAYERS * MT]) for i in range(4)]
        sgn = place("sgn", [P, 2])
        ones = place("ones", [P, P])
        ident = place("ident", [P, P])
        gw = place("gw", [P, 2, MT, LRU_WB])
        rws = place("rws", [P, DK, EXPERTS])
        rbs = place("rbs", [P, EXPERTS])
        lg = place("lg", [P, TB, EXPERTS])
        cmp1 = place("cmp1", [P, TB, EXPERTS, EXPERTS], at=[UU()[0], UU()[1]])
        cmp2 = place("cmp2", [P, TB, EXPERTS, EXPERTS], at=[UU()[0] + 4 * TB * 64, UU()[1]])
        rank = place("rank", [P, TB, EXPERTS])
        gate = place("gate", [P, TB, EXPERTS])
        gtmp = place("gtmp", [P, TB, EXPERTS])
        v1, v2, ex, g1, g2 = (place(n, [P, TB]) for n in ("v1", "v2", "ex", "g1", "g2"))
        gT = place("gT", [EXPERTS, T], at=LR())
        assert cursor[0] <= nc.sbuf_usable_end

        acc = ctx.enter_context(nc.psum_tensor("acc", [P, 2, 2, 512], F32))
        side = ctx.enter_context(nc.psum_tensor("side", [P, 4, 512], F32))

        raw_landed = [sem(f"raw_landed{i}") for i in range(RING)]
        hi_ready = [sem(f"hi_ready{i}") for i in range(RING)]
        lo_ready = [sem(f"lo_ready{i}") for i in range(RING)]
        unit_done = [sem(f"unit_done{i}") for i in range(RING)]
        acc_free = [sem(f"acc_free{i}") for i in range(2)]
        x_landed, small_landed = sem("x_landed"), sem("small_landed")
        const_ready = sem("const_ready")
        hs_ready, sq_ready, ss_ready, rms_ready = sem("hs_ready"), sem("sq_ready"), sem("ss_ready"), sem("rms_ready")
        hn_ready, xh_ready, xl_ready = sem("hn_ready"), sem("xh_ready"), sem("xl_ready")
        hs_saved, hs_back = sem("hs_saved"), sem("hs_back")
        prep_act, prep_dve, prep_pool = sem("prep_act"), sem("prep_dve"), sem("prep_pool")
        up_ready, u_out, u_in = sem("up_ready"), sem("u_out"), sem("u_in")
        xp_ready, xc_ready, gg_ready = sem("xp_ready"), sem("xc_ready"), sem("gg_ready")
        gm_done, ri_ready = sem("gm_done"), sem("ri_ready")
        lru_a, lru_t, lru_m, lru_r = sem("lru_a"), sem("lru_t"), sem("lru_m"), sem("lru_r")
        yb_ready, ybh_ready, ybl_ready = sem("yb_ready"), sem("ybh_ready"), sem("ybl_ready")
        gates_ready = sem("gates_ready")
        pb_landed = [sem("pb_landed0"), sem("pb_landed1")]
        wg_landed = sem("wg_landed")
        m1t_ready, tab_ready, c_ready = sem("m1t_ready"), sem("tab_ready"), sem("c_ready")
        p1_done, p2_done, p3_done = sem("p1_done"), sem("p2_done"), sem("p3_done")
        m_act, m_dve, m2_ready, rot_ready = sem("m_act"), sem("m_dve"), sem("m2_ready"), sem("rot_ready")
        ys_ready, y_out, y_in = sem("ys_ready"), [sem("y_out0"), sem("y_out1")], sem("y_in")
        y1_ready, y1h_ready, y1l_ready = sem("y1_ready"), sem("y1h_ready"), sem("y1l_ready")
        sg_ready, y2_ready, y2h_ready, y2l_ready = sem("sg_ready"), sem("y2_ready"), sem("y2h_ready"), sem("y2l_ready")
        mg_ready = sem("mg_ready")
        g_ready, f_ready, fh_ready, fl_ready = sem("g_ready"), sem("f_ready"), sem("fh_ready"), sem("fl_ready")
        lg_done, gate_ready, gT_done, gT_ready, g_out, g_in, ex_ready, d_ready = (
            sem(n) for n in ("lg_done", "gate_ready", "gT_done", "gT_ready", "g_out", "g_in", "ex_ready", "d_ready"))
        out_done = sem("out_done")
        act_chain, dve_chain, pool_chain = sem("act_chain"), sem("dve_chain"), sem("pool_chain")

        block = ctx.enter_context(nc.Block())

        def col(name, layer, tile):
            at, n = COLS[name]
            return cols[:, at + layer * n + tile:at + layer * n + tile + 1]

        def use(u, more=0):
            return u % RING, u // RING + more

        def halves(x):
            return x.rearrange("p (b c) -> p b c", b=2)

        def perm(x):
            return x.rearrange("p j c -> p c j")

        def chunked(x):
            return x.rearrange("p (c j) -> p c j", j=L)

        mix_u = [0, U_MIX + 2 * U_FF]
        mix_acc = [0, ACC_MIX + 2 * ACC_FF]
        ff_u = [U_MIX, 2 * U_MIX + 2 * U_FF]
        ff_acc = [ACC_MIX, 2 * ACC_MIX + 2 * ACC_FF]
        ff_e0 = [0, 2]
        ff_n = [2, EXPERTS]
        hs_at_norm = [0, 8, 24, 32, 96]

        def slot_of(k):
            return divmod(k - 4, 3) if k >= 4 else (None, None)

        KIND = [("u", m) for m in range(MT)]
        for m in range(MT):
            KIND += [("x", m), ("g", m)]
        KIND += [("gate", q) for q in range(2 * DK)]

        @block.sync
        def _(sp):
            sp.dma_start(cols[:, :], cols_d).then_inc(small_landed, 16)
            for m in range(DK):
                sp.dma_start(hs[:, m, :], xT[:, m, :]).then_inc(x_landed, 16)
            for u in range(RING):
                sp.dma_start(raw[u][:, :], W[u, :, :]).then_inc(raw_landed[u], 16)
            with sp.Fori(1, UNITS // RING) as it:
                for s in range(RING):
                    sp.wait_ge(lo_ready[s], it)
                    sp.dma_start(raw[s][:, :], W[it * RING + s, :, :]).then_inc(raw_landed[s], 16)
            for u in range(UNITS // RING * RING, UNITS):
                s, n = use(u)
                sp.wait_ge(lo_ready[s], n)
                sp.dma_start(raw[s][:, :], W[u, :, :]).then_inc(raw_landed[s], 16)
            for m in range(DK):
                sp.wait_ge(hn_ready, 4 * DK + m + 1)
                sp.dma_start(out[:, m, :], hn[:, m, :]).then_inc(out_done, 16)
            sp.wait_ge(out_done, 16 * DK)

        @block.gpsimd
        def _(pool):
            g = nc.gpsimd
            chain = [0]

            def link(ins):
                chain[0] += 1
                ins.then_inc(pool_chain, 1)
                pool.wait_ge(pool_chain, chain[0])

            def tt(out, a, b, op):
                link(g.tensor_tensor(out, a, b, op))

            for n, i in (("lr", 0), ("li", 1), ("ldt", 2)):
                pool.dma_start(pp[n][:, :], s5p[:, i, :]).then_inc(prep_pool, 16)
            g.memset(ones[:, :], 1.0).then_inc(const_ready, 1)
            link(g.memset(ident[:, :], 0.0))
            g.affine_select(out=ident[:, :], in_=ident[:, :], compare_op=ALU.not_equal, fill=1.0, base=0,
                            pattern=[[-1, P]], channel_multiplier=1).then_inc(const_ready, 1)
            pool.wait_ge(const_ready, 2)
            link(g.memset(apr[:, 0, :], 1.0))
            link(g.memset(api[:, 0, :], 0.0))
            g.memset(xpad[:, 0:3], 0.0).then_inc(const_ready, 1)
            pool.dma_start(rws[:, :, :], rw).then_inc(prep_pool, 16)
            pool.dma_start(rbs[:, :], rb).then_inc(prep_pool, 16)
            pool.wait_ge(prep_act, 4)
            t1, t2 = pp["t1"][:, :], pp["t2"][:, :]
            c, s = pp["cos"][:, :], pp["sin"][:, :]
            tt(apr[:, 1, :], pp["mag"][:, :], c, ALU.mult)
            tt(api[:, 1, :], pp["mag"][:, :], s, ALU.mult)

            def product(outr, outi, ar, ai, br, bi, x1=t1, x2=t2):
                tt(x1, ar, br, ALU.mult)
                tt(x2, ai, bi, ALU.mult)
                tt(x1, x1, x2, ALU.subtract)
                tt(x2, ar, bi, ALU.mult)
                tt(outi, ai, br, ALU.mult)
                tt(outi, outi, x2, ALU.add)
                link(g.tensor_copy(outr, x1))

            pool.wait_ge(prep_dve, 2)
            link(g.tensor_scalar(pp["num"][:, :], apr[:, 1, :], 1.0, 0.0, ALU.subtract, ALU.add))
            num, lr, li = pp["num"][:, :], pp["lr"][:, :], pp["li"][:, :]
            tt(t1, num, lr, ALU.mult)
            tt(t2, api[:, 1, :], li, ALU.mult)
            tt(t1, t1, t2, ALU.add)
            tt(cfr[:, :], t1, pp["rden"][:, :], ALU.mult)
            tt(t1, api[:, 1, :], lr, ALU.mult)
            tt(t2, num, li, ALU.mult)
            tt(t1, t1, t2, ALU.subtract)
            tt(cfi[:, :], t1, pp["rden"][:, :], ALU.mult)
            for k in range(2, L + 1):
                product(apr[:, k, :], api[:, k, :], apr[:, k - 1, :], api[:, k - 1, :], apr[:, 1, :], api[:, 1, :])
            ur, ui = sqr[:, 0, :], sqi[:, 0, :]
            product(ur, ui, c, s, c, s)
            t3 = pp["t3"][:, :]
            n = 2
            while n < L:
                tt(t1, ur, ur, ALU.mult)
                tt(t2, ui, ui, ALU.mult)
                tt(t3, ur, ui, ALU.mult)
                tt(ur, t1, t2, ALU.subtract)
                tt(ui, t3, t3, ALU.add)
                n *= 2
            tt(t1, ur, ur, ALU.mult)
            tt(t2, ui, ui, ALU.mult)
            tt(t1, t1, t2, ALU.add)
            link(g.tensor_scalar(t1, t1, -0.5, 1.5, ALU.mult, ALU.add))
            tt(ur, ur, t1, ALU.mult)
            tt(ui, ui, t1, ALU.mult)
            for k in range(1, 7):
                ar, ai = sqr[:, k - 1, :], sqi[:, k - 1, :]
                tt(t1, ar, ar, ALU.mult)
                tt(t2, ai, ai, ALU.mult)
                tt(t3, ar, ai, ALU.mult)
                tt(sqr[:, k, :], t1, t2, ALU.subtract)
                tt(sqi[:, k, :], t3, t3, ALU.add)

            for l in range(LAYERS):
                if l:
                    pool.wait_ge(hs_ready, hs_at_norm[2])
                for r in range(2):
                    pool.dma_start(gw[:, r, :, :], wg[l, :, r, :, :]).then_inc(wg_landed, 16)
                for b in range(2):
                    pool.dma_start(pbuf[:, b, :, :], s5m[l, b, :, :, :]).then_inc(pb_landed[b], 16)
                link(g.memset(m1t[:, :, L * GC:PADW], 0.0))
                link(g.memset(cosT[:, :, 0:1], 1.0))
                link(g.memset(sinT[:, :, 0:1], 0.0))
                link(g.memset(decay[:, :, 0:1], 0.0))
                for b in range(NB):
                    done = l * NB + b
                    gs = slice(l * GROUPS + b * GB, l * GROUPS + (b + 1) * GB)
                    v = lambda x: x.rearrange("p (g h) -> p g h", g=GB)
                    b1, braw, craw1, craw2 = (v(pbuf[:, b % 2, i, :]) for i in range(4))
                    wide = [P, GB, GC]
                    cb = lambda x: x[:, gs].unsqueeze(2).to_broadcast(wide)
                    pool.wait_ge(pb_landed[b % 2], 16 * (l * NB // 2 + b // 2 + 1))
                    if done:
                        pool.wait_ge(p1_done, done)
                        pool.wait_ge(m2_ready, done)
                    link(g.tensor_scalar(b2s[:, :, :], braw, sgn[:, 0:1], 0.0, ALU.mult, ALU.add))
                    link(g.tensor_scalar(c1[:, :, :], craw1, sgn[:, 1:2], 0.0, ALU.mult, ALU.add))
                    g.tensor_scalar(c2[:, :, :], craw2, -1.0, 0.0, ALU.mult, ALU.add).then_inc(c_ready, 1)
                    x1, x2 = v(pt1[:, 0:GB * GC]), v(pt2[:, 0:GB * GC])
                    tt(x1, cb(cfr), b1, ALU.mult)
                    tt(x2, cb(cfi), b2s[:, :, :], ALU.mult)
                    tt(bx[:, :, :], x1, x2, ALU.add)
                    tt(x1, cb(cfr), b2s[:, :, :], ALU.mult)
                    tt(x2, cb(cfi), b1, ALU.mult)
                    tt(by[:, :, :], x1, x2, ALU.subtract)
                    pool.wait_ge(c_ready, done + 1)
                    if b + 2 < NB:
                        pool.dma_start(pbuf[:, b % 2, :, :], s5m[l, b + 2, :, :, :]).then_inc(pb_landed[b % 2], 16)
                    for j in range(L):
                        ab = lambda x: x[:, L - 1 - j, gs].unsqueeze(2).to_broadcast(wide)
                        y1, y2 = (v(x[:, j * 64:j * 64 + 64]) for x in (pt1, pt2))
                        g.tensor_tensor(y1, ab(apr), bx[:, :, :], ALU.mult)
                        last = g.tensor_tensor(y2, ab(api), by[:, :, :], ALU.mult)
                    link(last)
                    w4 = lambda x: x[:, :].rearrange("p (j g h) -> p g j h", g=GB, h=GC)
                    g.tensor_tensor(m1t[:, :, 0:L * GC].rearrange("p g (j h) -> p g j h", h=GC), w4(pt1), w4(pt2),
                                    ALU.add).then_inc(m1t_ready, 1)
                    if done:
                        pool.wait_ge(rot_ready, done)
                    pool.wait_ge(m1t_ready, done + 1)
                    col1 = lambda x: x[:, gs].unsqueeze(2).to_broadcast([P, GB, NC - 1])
                    link(g.tensor_copy(decay[:, :, 1:NC], col1(mag8)))
                    link(g.tensor_copy(cosT[:, :, 1:2], sqr[:, 0, gs].unsqueeze(2)))
                    link(g.tensor_copy(sinT[:, :, 1:2], sqi[:, 0, gs].unsqueeze(2)))
                    k = 1
                    for i in range(1, 7):
                        k *= 2
                        n = min(k, NC - k)
                        br = sqr[:, i, gs].unsqueeze(2).to_broadcast([P, GB, n])
                        bi = sqi[:, i, gs].unsqueeze(2).to_broadcast([P, GB, n])
                        z1, z2, z3, z4 = (x[:, o:o + GB * n].rearrange("p (g c) -> p g c", g=GB)
                                          for x in (pt1, pt2) for o in (0, 256))
                        g.tensor_tensor(z1, cosT[:, :, 0:n], br, ALU.mult)
                        g.tensor_tensor(z3, sinT[:, :, 0:n], bi, ALU.mult)
                        g.tensor_tensor(z2, cosT[:, :, 0:n], bi, ALU.mult)
                        tt(z4, sinT[:, :, 0:n], br, ALU.mult)
                        g.tensor_tensor(cosT[:, :, k:k + n], z1, z3, ALU.subtract)
                        last = g.tensor_tensor(sinT[:, :, k:k + n], z2, z4, ALU.add)
                        if i < 6:
                            link(last)
                    last.then_inc(tab_ready, 1)
                    pool.wait_ge(tab_ready, done + 1)
            pool.wait_ge(xl_ready, 5 * DK)
            link(g.memset(tri[:, :, :], 1.0))
            g.affine_select(out=tri[:, :, :], in_=tri[:, :, :], compare_op=ALU.is_gt, fill=0.0, base=0,
                            pattern=[[1, EXPERTS], [-1, EXPERTS]], channel_multiplier=0).then_inc(const_ready, 1)

        @block.scalar
        def _(act):
            a = nc.scalar
            chain = [0]

            def link(ins):
                chain[0] += 1
                ins.then_inc(act_chain, 1)
                act.wait_ge(act_chain, chain[0])

            def split_hi(u, more=0):
                if isinstance(u, int) and isinstance(more, int) and u + RING * more >= UNITS:
                    return
                s, n = use(u, more)
                act.wait_ge(raw_landed[s], n * 16 + 16)
                if u >= RING:
                    act.wait_ge(unit_done[s], n)
                a.activation(wh[s][:, :], raw[s][:, :], ACT.Copy).then_inc(hi_ready[s], 1)

            def arrived(u, more=0):
                s, n = use(u, more)
                act.wait_ge(unit_done[s], n + 1)

            def norm(i):
                for m in range(DK):
                    if i == 0:
                        act.wait_ge(x_landed, 16 * DK)
                    else:
                        act.wait_ge(hs_ready, hs_at_norm[i] - DK + m + 1)
                    a.activation(hn[:, m, :], hs[:, m, :], ACT.Square).then_inc(sq_ready, 1)
                act.wait_ge(ss_ready, i + 1)
                link(a.activation(halves(rs[:, :]), side[:, 0:2, 0:TH], ACT.Copy, scale=1.0 / D))
                a.activation(rs[:, :], rs[:, :], ACT.Sqrt, bias=EPS).then_inc(rms_ready, 1)
                if i == 4:
                    return
                for m in range(DK):
                    act.wait_ge(hn_ready, i * DK + m + 1)
                    a.activation(xh[:, m, :], hn[:, m, :], ACT.Copy).then_inc(xh_ready, 1)

            def lru_pair(l, q):
                n = l * 2 + q
                act.wait_ge(ri_ready, 4 * n + 4)
                act.wait_ge(prep_dve, 4)
                if n:
                    act.wait_ge(yb_ready, 2 * n)
                for i in range(2):
                    t = l * MT + 2 * q + i
                    a.activation(th[:, i, :], ra[:, i, :], ACT.Tanh, scale=sp8[:, t:t + 1]).then_inc(lru_t, 1)
                act.wait_ge(lru_t, 2 * n + 2)
                for i in range(2):
                    t = l * MT + 2 * q + i
                    a.activation(ra[:, i, :], ra[:, i, :], ACT.Exp, scale=sp8n[:, t:t + 1]).then_inc(lru_a, 1)
                act.wait_ge(lru_m, n + 1)
                a.activation(th[:, :, :], th[:, :, :], ACT.Sqrt).then_inc(lru_r, 1)

            def lru_out(l, q):
                for t in (2 * q, 2 * q + 1):
                    act.wait_ge(yb_ready, l * MT + t + 1)
                    a.activation(ybh[:, t, :], gg[:, t, :], ACT.Copy).then_inc(ybh_ready, 1)

            def gate_sigmoid(l, q):
                t, r = q // 2, q % 2
                act.wait_ge(gm_done, l * 8 + q + 1)
                act.wait_ge(u_out, 64 * (l + 1))
                dst = (ra, ii)[r]
                if t >= 2:
                    act.wait_ge(yb_ready, l * MT + 2)
                a.activation(halves(dst[:, t % 2, :]), side[:, 2:4, 0:TH], ACT.Sigmoid,
                             bias=col(("b_r", "b_i")[r], l, t)).then_inc(ri_ready, 1)

            def mixer(l):
                u0, a0 = mix_u[l], mix_acc[l]
                for k in range(U_IN):
                    split_hi(u0 + k + 2)
                    kind, m = KIND[k]
                    arrived(u0 + k)
                    src = acc[:, k % 2, :, 0:TH]
                    if kind == "u":
                        if l and m == 0:
                            act.wait_ge(hs_ready, hs_at_norm[2])
                        a.activation(uperm[:, m, :, :].rearrange("p j (b c) -> p b c j", b=2),
                                     src.rearrange("p b (c j) -> p b c j", j=L), ACT.Copy).then_inc(acc_free[k % 2], 1)
                        act.wait_ge(acc_free[k % 2], a0 + k // 2 + 1)
                        act.dma_start(u_d[8 * m:8 * m + 8].rearrange("g h j c -> (g h) (j c)"),
                                      uperm[:, m, :, :].rearrange("p j c -> p (j c)")).then_inc(u_out, 16)
                    elif kind == "x":
                        if m or l:
                            act.wait_ge(xc_ready, l * MT + m)
                        if m == 0:
                            act.wait_ge(const_ready, 3)
                        a.activation(halves(xpad[:, 3:3 + T]), src, ACT.Copy).then_inc(acc_free[k % 2], 1)
                    elif kind == "g":
                        a.activation(halves(gg[:, m, :]), src, ACT.Gelu_apprx_tanh).then_inc(acc_free[k % 2], 1)
                    else:
                        if m == 0:
                            act.wait_ge(xl_ready, xl_at_norm(2 * l) + DK)
                            if l:
                                act.wait_ge(hs_saved, 16)
                        a.activation(halves(gates[:, m, :]), src, ACT.Sigmoid,
                                     bias=col("merge_bias", l, m)).then_inc(acc_free[k % 2], 1)
                    if k == 4:
                        act.wait_ge(u_out, 64 * (l + 1))
                        for j in range(L):
                            act.dma_start(uu[j * GC:(j + 1) * GC, :, :],
                                          u_d[:, :, j, :].rearrange("g h c -> h g c")).then_inc(u_in, 16)
                    b, part = slot_of(k)
                    if b is None:
                        continue
                    n = l * NB + b
                    if part == 0:
                        act.wait_ge(p1_done, n + 1)
                        mt = side[:, 0, :].rearrange("p (g s) -> p g s", g=GB)
                        a.activation(m1[:, :, :], mt, ACT.Copy)
                        a.activation(m1y[:, :, 0:GS], mt[:, :, GS:P], ACT.Copy)
                        a.activation(m1y[:, :, GS:P], mt[:, :, 0:GS], ACT.Copy, scale=-1.0).then_inc(m_act, 1)
                        if 1 <= b <= MT:
                            gate_sigmoid(l, 2 * b - 1)
                        if b in (2, 4):
                            lru_pair(l, b // 2 - 1)
                    elif part == 1 and b in (2, 4):
                        lru_out(l, b // 2 - 1)
                    elif part == 2:
                        act.wait_ge(p3_done, n + 1)
                        if n >= 2:
                            act.wait_ge(y_out[b % 2], 16 * L * (n // 2))
                        a.activation(ys[:, b % 2, :, :],
                                     side[:, 0, 0:GB * NC].rearrange("p (g c) -> p g c", g=GB),
                                     ACT.Copy).then_inc(ys_ready, 1)
                        act.wait_ge(ys_ready, n + 1)
                        for j in range(L):
                            act.dma_start(y_d[b * GB:(b + 1) * GB, :, j, :].rearrange("g h c -> h g c"),
                                          ys[j * GC:(j + 1) * GC, b % 2, :, :]).then_inc(y_out[b % 2], 16)
                        if b < MT:
                            gate_sigmoid(l, 2 * b)
                for i in range(2):
                    act.wait_ge(y_out[i], 16 * L * NB // 2 * (l + 1))
                act.dma_start(yt[:, :, :, :].rearrange("p m j c -> p m (j c)"),
                              y_d.rearrange("(m q) h j c -> (q h) m (j c)", m=MT)).then_inc(y_in, 16)
                act.wait_ge(y_in, 16 * (l + 1))
                for m in range(MT):
                    a.activation(yt[:, m, :, :], yt[:, m, :, :], ACT.Gelu_apprx_tanh).then_inc(y1_ready, 1)
                for m in range(MT):
                    act.wait_ge(y1_ready, l * MT + m + 1)
                    a.activation(chunked(y1h[:, m, :]), perm(yt[:, m, :, :]), ACT.Copy).then_inc(y1h_ready, 1)
                a1 = a0 + U_IN // 2
                for v in range(U_GLU):
                    u = u0 + U_IN + v
                    split_hi(u + 2)
                    arrived(u)
                    for i in range(2):
                        n = l * MT + 2 * v + i
                        if n >= 2:
                            act.wait_ge(y2_ready, n - 1)
                        if v == 0 and i == 0:
                            act.wait_ge(ybl_ready, (l + 1) * MT)
                        a.activation(halves(gt[:, i, :]), acc[:, i, :, 0:TH], ACT.Sigmoid,
                                     bias=col("b_glu", l, 2 * v + i)).then_inc(acc_free[i], 1)
                    for i in range(2):
                        act.wait_ge(y2_ready, l * MT + 2 * v + i + 1)
                        a.activation(y2h[:, 2 * v + i, :], ft[:, i, :], ACT.Copy).then_inc(y2h_ready, 1)
                for m in range(DK):
                    u = u0 + U_IN + U_GLU + m
                    split_hi(u + 2)
                    act.wait_ge(mg_ready, l * DK + m + 1)
                    a.activation(xh[:, m, :], ft[:, 0, :], ACT.Copy).then_inc(xh_ready, 1)
                for m in range(DK):
                    act.dma_start(hs[:, m, :], (hs_d if l else xT)[:, m, :]).then_inc(hs_back, 16)
                for m in range(DK):
                    split_hi(u0 + U_MIX - DK + m + 2)

            def expert(l, u0, e, e_all):
                with act.Fori(0, 2 * FT // STEP) as it:
                    more = e * (U_FF // RING) + it * (STEP // RING)
                    for i in range(STEP // 2):
                        m = it * (STEP // 2) + i
                        u = u0 + 2 * i
                        split_hi(u + 2, more)
                        arrived(u, more)
                        a.activation(halves(gt[:, 0, :]), acc[:, 0, :, 0:TH], ACT.Silu).then_inc(acc_free[0], 1)
                        split_hi(u + 3, more)
                        act.wait_ge(f_ready, e_all * FT + m + 1)
                        a.activation(fh[:, m, :], ft[:, 0, :], ACT.Copy).then_inc(fh_ready, 1)

            def down(u0, e, last):
                more = e * (U_FF // RING)
                for j in range(FT):
                    if not (last and j >= FT - 2):
                        split_hi(u0 + 2 * FT + j + 2, more)

            act.wait_ge(prep_pool, 16 * 5)
            link(a.activation(pp["dt"][:, :], pp["ldt"][:, :], ACT.Exp))
            a.activation(pp["t1"][:, :], pp["dt"][:, :], ACT.Copy).then_inc(prep_act, 1)
            act.wait_ge(prep_dve, 1)
            link(a.activation(pp["mag"][:, :], pp["num"][:, :], ACT.Exp))
            a.activation(mag8[:, :], pp["num"][:, :], ACT.Exp, scale=float(L)).then_inc(prep_act, 1)
            a.activation(pp["sin"][:, :], pp["red"][:, :], ACT.Sin).then_inc(prep_act, 1)
            a.activation(pp["cos"][:, :], pp["red2"][:, :], ACT.Sin).then_inc(prep_act, 1)
            act.wait_ge(prep_dve, 3)
            a.activation(spt[1][:, :], spt[0][:, :], ACT.Exp, scale=-1.0).then_inc(prep_act, 1)
            split_hi(0)
            split_hi(1)
            norm(0)
            mixer(0)
            norm(1)
            for l in range(LAYERS):
                if l:
                    for m in range(DK):
                        act.wait_ge(hs_ready, hs_at_norm[2] - DK + m + 1)
                    act.dma_start(hs_d, hs[:, :, :]).then_inc(hs_saved, 16)
                    norm(2)
                    mixer(1)
                    norm(3)
                    act.wait_ge(d_ready, 1)
                    a.activation(ex[0:TOK, :], v2[0:TOK, :], ACT.Exp).then_inc(ex_ready, 1)
                    act.wait_ge(gT_done, 1)
                    for i in range(2):
                        link(a.activation(gT[:, i * TH:(i + 1) * TH], side[0:EXPERTS, 1 + i, 0:TH], ACT.Copy))
                    act.dma_start(g_d, gT[:, :]).then_inc(g_out, 16)
                    act.wait_ge(g_out, 16)
                    act.wait_ge(mg_ready, 2 * DK)
                    act.dma_start(gbc[:, :, :], g_d.partition_broadcast(P)).then_inc(g_in, 16)
                with act.Fori(0, ff_n[l] - 1) as e:
                    expert(l, ff_u[l], e, e + ff_e0[l])
                    down(ff_u[l], e, False)
                e = ff_n[l] - 1
                expert(l, ff_u[l], e, e + ff_e0[l])
                down(ff_u[l], e, l == LAYERS - 1)
            norm(4)

        @block.vector
        def _(dve):
            v = nc.vector
            chain = [0]

            def link(ins):
                chain[0] += 1
                ins.then_inc(dve_chain, 1)
                dve.wait_ge(dve_chain, chain[0])

            def tt(out, a, b, op):
                return v.tensor_tensor(out, a, b, op)

            def split_lo(u, more=0):
                if isinstance(u, int) and isinstance(more, int) and u + RING * more >= UNITS:
                    return
                s, n = use(u, more)
                dve.wait_ge(hi_ready[s], n + 1)
                tt(wl[s][:, :], raw[s][:, :], wh[s][:, :].bitcast(F32), ALU.subtract).then_inc(lo_ready[s], 1)

            def arrived(u, more=0):
                s, n = use(u, more)
                dve.wait_ge(unit_done[s], n + 1)

            def norm(i):
                name, layer = (("mix_norm", 0), ("ffn_norm", 0), ("mix_norm", 1), ("ffn_norm", 1), ("final_norm", 0))[i]
                dve.wait_ge(rms_ready, i + 1)
                link(v.reciprocal(rs[:, :], rs[:, :]))

                def lower(m):
                    dve.wait_ge(xh_ready, xh_at_norm(i) + m + 1)
                    tt(xl[:, m, :], hn[:, m, :], xh[:, m, :].bitcast(F32), ALU.subtract).then_inc(xl_ready, 1)

                for m in range(DK):
                    if i < 4:
                        g = col(name, layer, m)
                    else:
                        at = COLS["final_norm"][0]
                        g = cols[:, at + m:at + m + 1]
                    v.scalar_tensor_tensor(out=hn[:, m, :], in0=hs[:, m, :], scalar=g, in1=rs[:, :],
                                           op0=ALU.mult, op1=ALU.mult).then_inc(hn_ready, 1)
                    if m and i < 4:
                        lower(m - 1)
                if i < 4:
                    lower(DK - 1)

            def conv(l, m):
                n = l * MT + m
                w = lambda k: col("conv_w", l, 4 * k + m)
                if n == 0:
                    dve.wait_ge(c_ready, 1)
                dve.wait_ge(acc_free[0], mix_acc[l] + 2 + m + 1)
                link(v.tensor_scalar(xc[:, m, :], xpad[:, 0:T], w(0), col("conv_b", l, m), ALU.mult, ALU.add))
                for k in range(1, 4):
                    last = v.scalar_tensor_tensor(out=xc[:, m, :], in0=xpad[:, k:k + T], scalar=w(k),
                                                  in1=xc[:, m, :], op0=ALU.mult, op1=ALU.add)
                    if k < 3:
                        link(last)
                last.then_inc(xc_ready, 1)

            def lru_pair(l, q):
                n = l * 2 + q
                dve.wait_ge(lru_a, 2 * n + 2)
                dve.wait_ge(xc_ready, l * MT + 2 * q + 2)
                pair = slice(2 * q, 2 * q + 2)
                link(tt(ii[:, :, :], ii[:, :, :], xc[:, pair, :], ALU.mult))
                link(tt(xc[:, pair, :], ra[:, :, :], ra[:, :, :], ALU.mult))
                v.scalar_tensor_tensor(out=th[:, :, :].rearrange("p a b -> p (a b)"),
                                       in0=xc[:, pair, :].rearrange("p a b -> p (a b)"), scalar=1.0,
                                       in1=th[:, :, :].rearrange("p a b -> p (a b)"),
                                       op0=ALU.add, op1=ALU.mult).then_inc(lru_m, 1)

            def lru_scan(l, q):
                n = l * 2 + q
                dve.wait_ge(lru_r, n + 1)
                pair = slice(2 * q, 2 * q + 2)
                link(tt(ii[:, :, :], ii[:, :, :], th[:, :, :], ALU.mult))
                v.tensor_tensor_scan(th[:, 0, :], ra[:, 0, :], ii[:, 0, :], 0.0, ALU.mult, ALU.add)
                link(v.tensor_tensor_scan(th[:, 1, :], ra[:, 1, :], ii[:, 1, :], 0.0, ALU.mult, ALU.add))
                k = 4 + 2 * (2 * q + 1) + 1
                dve.wait_ge(acc_free[1], mix_acc[l] + k // 2 + 1)
                for i in range(2):
                    tt(gg[:, 2 * q + i, :], gg[:, 2 * q + i, :], th[:, i, :], ALU.mult).then_inc(yb_ready, 1)

            def lru_out(l, q):
                for t in (2 * q, 2 * q + 1):
                    dve.wait_ge(ybh_ready, l * MT + t + 1)
                    tt(ybl[:, t, :], gg[:, t, :], ybh[:, t, :].bitcast(F32), ALU.subtract).then_inc(ybl_ready, 1)

            def mixer(l):
                u0, a0 = mix_u[l], mix_acc[l]
                v.memset(cr[:, :, 0:1], 0.0)
                link(v.memset(sr[:, :, 0:1], 0.0))
                for k in range(U_IN):
                    split_lo(u0 + k + 2)
                    b, part = slot_of(k)
                    if b is None:
                        continue
                    n = l * NB + b
                    if part == 0:
                        dve.wait_ge(p1_done, n + 1)
                        for i in range(GB):
                            at = COLS["s5_d"][0] + l * GROUPS + b * GB + i
                            last = v.scalar_tensor_tensor(out=m3[:, i, :], in0=ident[:, :], scalar=cols[:, at:at + 1],
                                                          in1=side[:, 1, i * P:(i + 1) * P], op0=ALU.mult, op1=ALU.add)
                        last.then_inc(m_dve, 1)
                        dve.wait_ge(c_ready, n + 1)
                        if n:
                            dve.wait_ge(p3_done, n)
                        gs = slice(l * GROUPS + b * GB, l * GROUPS + (b + 1) * GB)
                        w4 = [P, GB, L, GC]
                        ab = lambda x: x[:, 1:L + 1, gs].rearrange("p j g -> p g j").unsqueeze(3).to_broadcast(w4)
                        cb = lambda x: x[:, :, :].unsqueeze(2).to_broadcast(w4)
                        q4 = lambda x: x[:, :, :].rearrange("p g (j h) -> p g j h", h=GC)
                        d4 = dt1[:, :].rearrange("p (g j h) -> p g j h", g=GB, h=GC)
                        tt(d4, ab(apr), cb(c1), ALU.mult)
                        link(tt(q4(m2), ab(api), cb(c2), ALU.mult))
                        link(tt(q4(m2), q4(m2), d4, ALU.add))
                        tt(d4, ab(apr), cb(c2), ALU.mult)
                        link(tt(q4(m2y), ab(api), cb(c1), ALU.mult))
                        tt(q4(m2y), d4, q4(m2y), ALU.subtract).then_inc(m2_ready, 1)
                        if b in (2, 4):
                            lru_pair(l, b // 2 - 1)
                    elif part == 1:
                        dve.wait_ge(p2_done, n + 1)
                        dve.wait_ge(tab_ready, n + 1)
                        w3 = lambda bank: side[:, bank, 0:GB * NC].rearrange("p (g c) -> p g c", g=GB)
                        tt(rot[:, :, :], w3(2), cosT[:, :, :], ALU.mult)
                        link(tt(rot2[:, :, :], w3(3), sinT[:, :, :], ALU.mult))
                        link(tt(rot[:, :, :], rot[:, :, :], rot2[:, :, :], ALU.add))
                        flat = lambda x: x[:, :, :].rearrange("p g c -> p (g c)")
                        link(v.tensor_tensor_scan(flat(turned), flat(decay), flat(rot), 0.0, ALU.mult, ALU.add))
                        tt(cr[:, :, 1:NC], turned[:, :, 0:NC - 1], cosT[:, :, 0:NC - 1], ALU.mult)
                        tt(sr[:, :, 1:NC], turned[:, :, 0:NC - 1], sinT[:, :, 0:NC - 1], ALU.mult).then_inc(rot_ready, 1)
                        if b in (2, 4):
                            lru_scan(l, b // 2 - 1)
                            lru_out(l, b // 2 - 1)
                    kind, m = KIND[k]
                    if kind == "x":
                        conv(l, m)
                for m in range(MT):
                    dve.wait_ge(y1h_ready, l * MT + m + 1)
                    tt(chunked(y1l[:, m, :]), perm(yt[:, m, :, :]), chunked(y1h[:, m, :].bitcast(F32)),
                       ALU.subtract).then_inc(y1l_ready, 1)
                a1 = a0 + U_IN // 2
                for g in range(U_GLU):
                    split_lo(u0 + U_IN + g + 2)
                    for i in range(2):
                        m = 2 * g + i
                        dve.wait_ge(acc_free[i], a1 + g + 1)
                        if m >= 2:
                            dve.wait_ge(y2l_ready, l * MT + m - 1)
                        tt(chunked(ft[:, i, :]), chunked(gt[:, i, :]), perm(yt[:, m, :, :]), ALU.mult).then_inc(y2_ready, 1)
                    for i in range(2):
                        m = 2 * g + i
                        dve.wait_ge(y2h_ready, l * MT + m + 1)
                        tt(y2l[:, m, :], ft[:, i, :], y2h[:, m, :].bitcast(F32), ALU.subtract).then_inc(y2l_ready, 1)
                for m in range(DK):
                    u = u0 + U_IN + U_GLU + m
                    split_lo(u + 2)
                    arrived(u)
                    if m == 0:
                        dve.wait_ge(acc_free[0], a0 + 14)
                        dve.wait_ge(acc_free[1], a0 + 14)
                        dve.wait_ge(y2l_ready, (l + 1) * MT)
                    else:
                        dve.wait_ge(xl_ready, xh_at_mix(l) + m)
                    tt(halves(ft[:, 0, :]), acc[:, 0, :, 0:TH], halves(gates[:, m, :]), ALU.mult).then_inc(acc_free[0], 1)
                    tt(halves(ft[:, 1, :]), acc[:, 1, :, 0:TH], halves(gates[:, DK + m, :]), ALU.mult).then_inc(acc_free[1], 1)
                    dve.wait_ge(acc_free[0], a0 + 16 + m + 1)
                    dve.wait_ge(acc_free[1], a0 + 16 + m + 1)
                    tt(ft[:, 0, :], ft[:, 0, :], ft[:, 1, :], ALU.add).then_inc(mg_ready, 1)
                    dve.wait_ge(xh_ready, xh_at_mix(l) + m + 1)
                    tt(xl[:, m, :], ft[:, 0, :], xh[:, m, :].bitcast(F32), ALU.subtract).then_inc(xl_ready, 1)
                for m in range(DK):
                    u = u0 + U_MIX - DK + m
                    split_lo(u + 2)
                    arrived(u)
                    dve.wait_ge(hs_back, 16 * DK * (l + 1))
                    v.tensor_tensor(halves(hs[:, m, :]), halves(hs[:, m, :]), acc[:, m % 2, :, 0:TH],
                                    ALU.add).then_inc(hs_ready, 1)
                    dve.wait_ge(hs_ready, hs_at_norm[2 * l + 1] - DK + m + 1)
                    v.nop().then_inc(acc_free[m % 2], 1)

            def expert(l, u0, e, e_all):
                with dve.Fori(0, 2 * FT // STEP) as it:
                    more = e * (U_FF // RING) + it * (STEP // RING)
                    for i in range(STEP // 2):
                        m = it * (STEP // 2) + i
                        u = u0 + 2 * i
                        split_lo(u + 2, more)
                        split_lo(u + 3, more)
                        arrived(u + 1, more)
                        uses = e * ACC_FF + it * (STEP // 2) + (i + ff_acc[l] + 1)
                        dve.wait_ge(acc_free[0], uses)
                        tt(halves(ft[:, 0, :]), halves(gt[:, 0, :]), acc[:, 1, :, 0:TH], ALU.mult).then_inc(acc_free[1], 1)
                        dve.wait_ge(acc_free[1], uses)
                        if l:
                            tt(ft[:, 0, :], ft[:, 0, :], gbc[:, e, :], ALU.mult).then_inc(f_ready, 1)
                        else:
                            v.nop().then_inc(f_ready, 1)
                        dve.wait_ge(fh_ready, e_all * FT + m + 1)
                        tt(fl[:, m, :], ft[:, 0, :], fh[:, m, :].bitcast(F32), ALU.subtract).then_inc(fl_ready, 1)
                        dve.wait_ge(fl_ready, e_all * FT + m + 1)

            def down(l, u0, e, e_all, last):
                more = e * (U_FF // RING)
                for j in range(FT):
                    u = u0 + 2 * FT + j
                    if not (last and j >= FT - 2):
                        split_lo(u + 2, more)
                    if j % 3 == 0:
                        continue
                    m = 2 * (j // 3) + (j % 3 - 1)
                    arrived(u, more)
                    seen = hs_at_norm[2 * l + 1] + e * DK
                    if m == 0:
                        dve.wait_ge(hs_ready, seen)
                    v.tensor_tensor(halves(hs[:, m, :]), halves(hs[:, m, :]), acc[:, m % 2, :, 0:TH],
                                    ALU.add).then_inc(hs_ready, 1)
                    dve.wait_ge(hs_ready, seen + m + 1)
                    v.nop().then_inc(acc_free[m % 2], 1)

            v.memset(sgn[0:GS, 0:1], -1.0)
            v.memset(sgn[GS:P, 0:1], 1.0)
            v.memset(sgn[0:GS, 1:2], 1.0)
            link(v.memset(sgn[GS:P, 1:2], -1.0))
            dve.wait_ge(small_landed, 16)
            dve.wait_ge(prep_act, 1)
            ang, kk, red, red2 = (pp[n][:, :] for n in ("ang", "k", "red", "red2"))
            ROUND = 12582912.0
            C1, C2, C3 = 6.28125, 0.0019350051879882812, 3.019916e-07
            link(tt(ang, pp["li"][:, :], pp["dt"][:, :], ALU.mult))
            link(v.tensor_scalar(kk, ang, 0.15915494309189535, ROUND, ALU.mult, ALU.add))
            link(v.tensor_scalar(kk, kk, ROUND, 0.0, ALU.subtract, ALU.add))
            for c in (C1, C2, C3):
                link(v.scalar_tensor_tensor(out=ang, in0=kk, scalar=-c, in1=ang, op0=ALU.mult, op1=ALU.add))
            link(v.tensor_scalar(red, ang, 3.1415925, -3.1415925, ALU.min, ALU.max))
            link(v.tensor_scalar(kk, ang, 1.5707963267948966, -6.283185307179586, ALU.is_gt, ALU.mult))
            link(v.scalar_tensor_tensor(out=red2, in0=ang, scalar=1.5707963267948966, in1=kk, op0=ALU.add, op1=ALU.add))
            link(v.tensor_scalar(red2, red2, 3.1415925, -3.1415925, ALU.min, ALU.max))
            tt(pp["num"][:, :], pp["lr"][:, :], pp["dt"][:, :], ALU.mult).then_inc(prep_dve, 1)
            link(tt(pp["den"][:, :], pp["lr"][:, :], pp["lr"][:, :], ALU.mult))
            link(tt(pp["t3"][:, :], pp["li"][:, :], pp["li"][:, :], ALU.mult))
            link(tt(pp["den"][:, :], pp["den"][:, :], pp["t3"][:, :], ALU.add))
            v.reciprocal(pp["rden"][:, :], pp["den"][:, :]).then_inc(prep_dve, 1)
            at, n = COLS["lam"]
            lam = cols[:, at:at + LAYERS * n]
            s0, s1, s2, s3 = (x[:, :] for x in spt)
            link(v.tensor_scalar(s2, lam, -1.0, 0.0, ALU.mult, ALU.add))
            tt(s0, lam, s2, ALU.max).then_inc(prep_dve, 1)
            link(v.tensor_scalar(s3, s2, 0.0, 0.0, ALU.max, ALU.add))
            dve.wait_ge(prep_act, 5)
            link(v.tensor_scalar(s0, s1, 2.0, 0.0, ALU.add, ALU.add))
            link(v.reciprocal(s0, s0))
            link(tt(s1, s1, s0, ALU.mult))
            link(tt(s0, s1, s1, ALU.mult))
            link(v.tensor_scalar(s2, s0, 2.0 / 17, 2.0 / 15, ALU.mult, ALU.add))
            for d in (13, 11, 9, 7, 5, 3, 1):
                link(tt(s2, s2, s0, ALU.mult))
                link(v.tensor_scalar(s2, s2, 1.0, 2.0 / d, ALU.mult, ALU.add))
            link(tt(s2, s2, s1, ALU.mult))
            link(tt(s2, s2, s3, ALU.add))
            link(v.tensor_scalar(sp8[:, :], s2, LRU_C, 0.0, ALU.mult, ALU.add))
            v.tensor_scalar(sp8n[:, :], s2, -LRU_C, 0.0, ALU.mult, ALU.add).then_inc(prep_dve, 1)
            split_lo(0)
            split_lo(1)
            norm(0)
            mixer(0)
            norm(1)
            for l in range(LAYERS):
                if l:
                    norm(2)
                    mixer(1)
                    norm(3)
                    k = slice(0, TOK)
                    dve.wait_ge(lg_done, 1)
                    dve.wait_ge(const_ready, 4)
                    w3, w4 = [TOK, TB, EXPERTS], [TOK, TB, EXPERTS, EXPERTS]
                    link(tt(lg[k, :, :], side[k, 0, 0:TB * EXPERTS].rearrange("p (t e) -> p t e", t=TB),
                            rbs[k, :].unsqueeze(1).to_broadcast(w3), ALU.add))
                    mine = lg[k, :, :].unsqueeze(3).to_broadcast(w4)
                    other = lg[k, :, :].unsqueeze(2).to_broadcast(w4)
                    tt(cmp1[k], other, mine, ALU.is_gt)
                    link(tt(cmp2[k], other, mine, ALU.is_equal))
                    link(tt(cmp2[k], cmp2[k], tri[k].unsqueeze(1).to_broadcast(w4), ALU.mult))
                    link(tt(cmp1[k], cmp1[k], cmp2[k], ALU.add))
                    link(v.reduce_sum(rank[k], cmp1[k], AX_X))
                    v.reduce_max(v1[k], lg[k], AX_X)
                    link(v.tensor_scalar(gtmp[k], rank[k], 0.0, -1e30, ALU.is_equal, ALU.mult))
                    link(tt(gtmp[k], gtmp[k], lg[k], ALU.add))
                    link(v.reduce_max(v2[k], gtmp[k], AX_X))
                    tt(v2[k], v2[k], v1[k], ALU.subtract).then_inc(d_ready, 1)
                    dve.wait_ge(ex_ready, 1)
                    link(v.tensor_scalar(g1[k], ex[k], 1.0, 0.0, ALU.add, ALU.add))
                    link(v.reciprocal(g1[k], g1[k]))
                    link(tt(g2[k], g1[k], ex[k], ALU.mult))
                    v.tensor_scalar(gate[k], rank[k], 0.0, 0.0, ALU.is_equal, ALU.add)
                    link(v.tensor_scalar(gtmp[k], rank[k], 1.0, 0.0, ALU.is_equal, ALU.add))
                    tt(gate[k], gate[k], g1[k].unsqueeze(2).to_broadcast(w3), ALU.mult)
                    link(tt(gtmp[k], gtmp[k], g2[k].unsqueeze(2).to_broadcast(w3), ALU.mult))
                    tt(gate[k], gate[k], gtmp[k], ALU.add).then_inc(gate_ready, 1)
                    dve.wait_ge(g_in, 16)
                with dve.Fori(0, ff_n[l] - 1) as e:
                    expert(l, ff_u[l], e, e + ff_e0[l])
                    down(l, ff_u[l], e, e + ff_e0[l], False)
                e = ff_n[l] - 1
                expert(l, ff_u[l], e, e + ff_e0[l])
                down(l, ff_u[l], e, e + ff_e0[l], l == LAYERS - 1)
            norm(4)

        @block.tensor
        def _(pe):
            mm = nc.tensor.matmul

            def free(s, n):
                if not isinstance(n, int) or n > 0:
                    pe.wait_ge(acc_free[s], n)

            def unit(u, jobs, more=0):
                s, n = use(u, more)
                pe.wait_ge(lo_ready[s], n + 1)
                for k, a, hi, lo, first, last in jobs:
                    w_hi, w_lo = (x[s][:, k * P:(k + 1) * P] for x in (wh, wl))
                    parts = [(w_hi, hi), (w_hi, lo), (w_lo, hi)]
                    for i, (w, x) in enumerate(parts):
                        for b in range(2):
                            ins = mm(acc[:, a, b, 0:TH], w, x[:, b * TH:(b + 1) * TH],
                                     start=first and i == 0, stop=last and i == 2)
                ins.then_inc(unit_done[s], 1)

            def norm(i):
                if i == 0:
                    pe.wait_ge(const_ready, 1)
                for m in range(DK):
                    pe.wait_ge(sq_ready, i * DK + m + 1)
                    for b in range(2):
                        ins = mm(side[:, b, 0:TH], ones[:, :], hn[:, m, b * TH:(b + 1) * TH],
                                 start=m == 0, stop=m == DK - 1)
                ins.then_inc(ss_ready, 1)

            def full(xs, m):
                return [(k, xs[0][:, k, :], xs[1][:, k, :]) for k in range(DK)]

            def gate_mm(l, q):
                t, r = q // 2, q % 2
                pe.wait_ge(xc_ready, l * MT + t + 1)
                pe.wait_ge(wg_landed, 32 * (l + 1))
                if l * 8 + q:
                    pe.wait_ge(ri_ready, l * 8 + q)
                pe.wait_ge(rot_ready, l * NB + q // 2 + 1)
                for hd in range(2):
                    rows = slice(hd * 64, hd * 64 + 64)
                    for b in range(2):
                        ins = mm(side[rows, 2 + b, 0:TH], gw[rows, r, t, :], xc[rows, t, b * TH:(b + 1) * TH],
                                 start=True, stop=True)
                ins.then_inc(gm_done, 1)

            def mixer(l):
                u0, a0 = mix_u[l], mix_acc[l]
                for k in range(U_IN):
                    if k == 0:
                        pe.wait_ge(xl_ready, xl_at_norm(2 * l) + DK)
                    free(k % 2, a0 + k // 2)
                    unit(u0 + k, [(j, k % 2, xh[:, j, :], xl[:, j, :], j == 0, j == DK - 1) for j in range(DK)])
                    b, part = slot_of(k)
                    if b is None:
                        continue
                    n = l * NB + b
                    if part == 0:
                        pe.wait_ge(const_ready, 2)
                        pe.wait_ge(m1t_ready, n + 1)
                        pe.wait_ge(c_ready, n + 1)
                        if n:
                            pe.wait_ge(ys_ready, n)
                            pe.wait_ge(m_dve, n)
                        for i in range(GB):
                            nc.tensor.transpose(side[:, 0, i * P:(i + 1) * P], m1t[:, i, 0:P], ident[:, :])
                        for i in range(GB):
                            for j in range(L):
                                at = (L - 1 - j) * GC
                                ins = mm(side[:, 1, i * P + j * GC:i * P + (j + 1) * GC], m1t[:, i, at:at + P],
                                         c1[:, i, :], start=True, stop=True)
                        ins.then_inc(p1_done, 1)
                        if 1 <= b <= MT:
                            gate_mm(l, 2 * b - 1)
                    elif part == 1:
                        pe.wait_ge(m_act, n + 1)
                        pe.wait_ge(m_dve, n + 1)
                        pe.wait_ge(u_in, 16 * L * (l + 1))
                        if b:
                            pe.wait_ge(ri_ready, l * 8 + min(2 * b, 8))
                        for i in range(GB):
                            c = slice(i * NC, (i + 1) * NC)
                            mm(side[:, 2, c], m1[:, i, :], uu[:, b * GB + i, :], start=True, stop=True)
                            ins = mm(side[:, 3, c], m1y[:, i, :], uu[:, b * GB + i, :], start=True, stop=True)
                        ins.then_inc(p2_done, 1)
                    else:
                        pe.wait_ge(rot_ready, n + 1)
                        pe.wait_ge(m2_ready, n + 1)
                        for i in range(GB):
                            c = slice(i * NC, (i + 1) * NC)
                            mm(side[:, 0, c], m3[:, i, :], uu[:, b * GB + i, :], start=True, stop=False)
                            mm(side[:, 0, c], m2[:, i, :], cr[:, i, :], start=False, stop=False)
                            ins = mm(side[:, 0, c], m2y[:, i, :], sr[:, i, :], start=False, stop=True)
                        ins.then_inc(p3_done, 1)
                        if b < MT:
                            gate_mm(l, 2 * b)
                a1 = a0 + U_IN // 2
                pe.wait_ge(y1l_ready, (l + 1) * MT)
                for g in range(U_GLU):
                    free(0, a1 + g)
                    free(1, a1 + g)
                    unit(u0 + U_IN + g, [(4 * i + k, i, y1h[:, k, :], y1l[:, k, :], k == 0, k == MT - 1)
                                         for i in range(2) for k in range(MT)])
                pe.wait_ge(y2l_ready, (l + 1) * MT)
                pe.wait_ge(ybl_ready, (l + 1) * MT)
                for m in range(DK):
                    free(0, a0 + 16 + m)
                    free(1, a0 + 16 + m)
                    unit(u0 + U_IN + U_GLU + m,
                         [(k, 0, y2h[:, k, :], y2l[:, k, :], k == 0, k == MT - 1) for k in range(MT)]
                         + [(MT + k, 1, ybh[:, k, :], ybl[:, k, :], k == 0, k == MT - 1) for k in range(MT)])
                pe.wait_ge(xl_ready, xl_mix_end(l))
                for m in range(DK):
                    free(m % 2, a0 + 24 + m // 2)
                    unit(u0 + U_MIX - DK + m,
                         [(k, m % 2, xh[:, k, :], xl[:, k, :], k == 0, k == DK - 1) for k in range(DK)])

            def expert(l, u0, e, e_all):
                with pe.Fori(0, 2 * FT // STEP) as it:
                    more = e * (U_FF // RING) + it * (STEP // RING)
                    for i in range(STEP):
                        free(i % 2, e * ACC_FF + it * (STEP // 2) + (i // 2 + ff_acc[l]))
                        unit(u0 + i, [(k, i % 2, xh[:, k, :], xl[:, k, :], k == 0, k == DK - 1) for k in range(DK)], more)

            def down(l, u0, e, e_all):
                more = e * (U_FF // RING)
                for q in range(FT // 3):
                    tiles = [(2 * q + i, k) for i in range(2) for k in range(FT)]
                    for j in range(3):
                        jobs = []
                        for p, (m, k) in enumerate(tiles[8 * j:8 * j + 8]):
                            jobs.append((p, m % 2, fh[:, k, :], fl[:, k, :], k == 0, k == FT - 1))
                        pe.wait_ge(fl_ready, e_all * FT + (8 if q == 0 and j == 0 else FT))
                        for m, k in tiles[8 * j:8 * j + 8]:
                            if k == 0:
                                free(m % 2, e * ACC_FF + (ff_acc[l] + FT + q))
                        unit(u0 + 2 * FT + 3 * q + j, jobs, more)

            norm(0)
            mixer(0)
            norm(1)
            for l in range(LAYERS):
                if l:
                    norm(2)
                    mixer(1)
                    norm(3)
                    pe.wait_ge(hn_ready, 4 * DK)
                    pe.wait_ge(rms_ready, 4)
                    pe.wait_ge(prep_pool, 16 * 5)
                    for t in range(TB):
                        for k in range(DK):
                            ins = mm(side[0:TOK, 0, t * EXPERTS:(t + 1) * EXPERTS], hn[:, k, t * TOK:(t + 1) * TOK],
                                     rws[:, k, :], start=k == 0, stop=k == DK - 1)
                    ins.then_inc(lg_done, 1)
                    pe.wait_ge(gate_ready, 1)
                    for t in range(TB):
                        at = t % 3 * TOK
                        ins = mm(side[0:EXPERTS, 1 + t // 3, at:at + TOK], gate[0:TOK, t, :], ident[0:TOK, 0:TOK],
                                 start=True, stop=True)
                    ins.then_inc(gT_done, 1)
                pe.wait_ge(xl_ready, xl_at_norm(2 * l + 1) + DK)
                with pe.Fori(0, ff_n[l] - 1) as e:
                    expert(l, ff_u[l], e, e + ff_e0[l])
                    down(l, ff_u[l], e, e + ff_e0[l])
                e = ff_n[l] - 1
                expert(l, ff_u[l], e, e + ff_e0[l])
                down(l, ff_u[l], e, e + ff_e0[l])
            norm(4)


LRU_WB = 64


def xh_at_norm(i):
    return DK * (0, 2, 3, 5)[i]


def xl_at_norm(i):
    return xh_at_norm(i)


def xh_at_mix(l):
    return DK * (1, 4)[l]


def xl_mix_end(l):
    return xh_at_mix(l) + DK


def layout(inputs):
    import numpy as np

    a = {k: np.asarray(v) for k, v in inputs.items()}
    arrays = {}
    x = np.concatenate([a["meta_tokens"], a["x"][0]], axis=0)
    tiles = lambda v: np.moveaxis(v.reshape(-1, P, *v.shape[1:]), 0, 1)
    arrays["xT"] = tiles(x.T)

    W = np.empty((UNITS, P, UNIT), np.float32)
    at = [0]

    def put(w):
        n = w.shape[0] // 8
        W[at[0]:at[0] + n] = np.moveaxis(w.reshape(n, 8, P, P), 1, 2).reshape(n, P, UNIT)
        at[0] += n

    def cut(w):
        k, m = w.shape
        return w.reshape(k // P, P, m // P, P).transpose(2, 0, 1, 3)

    def ffn(gate, up, down):
        g, u = cut(gate), cut(up)
        put(np.stack([g, u], axis=1).reshape(-1, P, P))
        put(cut(down).reshape(-1, P, P))

    for l in range(LAYERS):
        w = cut(a["w_in"][l])
        order = list(range(MT))
        for m in range(MT):
            order += [MT + m, 2 * MT + m]
        order += list(range(3 * MT, U_IN))
        put(w[order].reshape(-1, P, P))
        put(cut(a["s5_w_glu"][l]).reshape(-1, P, P))
        put(np.stack([cut(a["s5_w_proj"][l]), cut(a["lru_w_proj"][l])], axis=1).reshape(-1, P, P))
        put(cut(a["w_out"][l]).reshape(-1, P, P))
        if l == 0:
            for h in range(2):
                c = slice(h * FF, (h + 1) * FF)
                ffn(a["dense_w_gate"][0][:, c], a["dense_w_up"][0][:, c], a["dense_w_down"][0][c])
        else:
            for e in range(EXPERTS):
                ffn(a["moe_w_gate"][0, e], a["moe_w_up"][0, e], a["moe_w_down"][0, e])
    assert at[0] == UNITS
    arrays["W"] = W

    cols = np.empty((P, NCOL), np.float32)
    for name, key in (("mix_norm", "mix_norm"), ("ffn_norm", "ffn_norm"), ("merge_bias", "merge_bias"),
                      ("conv_w", "lru_conv_w"), ("conv_b", "lru_conv_b"), ("b_r", "lru_b_rgate"),
                      ("b_i", "lru_b_igate"), ("lam", "lru_lambda"), ("b_glu", "s5_b_glu"),
                      ("final_norm", "final_norm")):
        c, n = COLS[name]
        cols[:, c:c + LAYERS * n] = a[key].reshape(-1, P).T
    c, n = COLS["s5_d"]
    cols[:, c:c + LAYERS * n] = np.tile(a["s5_d"].reshape(SP2, GC).T, (L, 1))
    arrays["cols"] = cols

    lam = [np.tile(a[k].reshape(SP2, GS).T, (2, 1)) for k in ("s5_lambda_re", "s5_lambda_im")]
    dt = np.broadcast_to(a["s5_log_dt"].reshape(1, SP2), (P, SP2))
    arrays["s5p"] = np.stack([*lam, dt], axis=1)
    br, bi = (a[k].transpose(0, 2, 1, 3) for k in ("s5_b_re", "s5_b_im"))
    cr, ci = (a[k].transpose(0, 3, 1, 2) for k in ("s5_c_re", "s5_c_im"))
    both = [np.concatenate(p, axis=1) for p in ((br, bi), (bi, br), (cr, ci), (ci, cr))]
    m = np.stack(both, axis=2).reshape(LAYERS, P, 4, NB, GB * GC)
    arrays["s5m"] = m.transpose(0, 3, 1, 2, 4)

    wr, wi = (a[k].reshape(LAYERS, MT, P, LRU_WB).transpose(0, 2, 1, 3) for k in ("lru_w_rgate", "lru_w_igate"))
    arrays["wg"] = np.stack([wr, wi], axis=2)
    arrays["rw"] = tiles(a["router_w"][0])
    arrays["rb"] = np.broadcast_to(a["router_b"], (P, EXPERTS))
    return {"in_" + k: np.ascontiguousarray(v) for k, v in arrays.items()}


def kernel(**inputs):
    import numpy as np
    from concourse import bacc
    from concourse.bass_utils import run_bass_kernel_spmd

    arrays = layout(inputs)
    nc = bacc.Bacc("TRN2", target_bir_lowering=False, num_devices=1)
    args = [nc.dram_tensor(k, v.shape, F32, kind="ExternalInput").ap() for k, v in arrays.items()]
    out = nc.dram_tensor("out_0", (P, DK, T), F32, kind="ExternalOutput").ap()
    scratch = [nc.dram_tensor(n, s, F32).ap() for n, s in
               (("hs_d", (P, DK, T)), ("u_d", (GROUPS, GC, L, NC)), ("y_d", (GROUPS, GC, L, NC)),
                ("g_d", (EXPERTS, T)))]
    build(nc, *args, out, *scratch)
    r = run_bass_kernel_spmd(nc, [arrays], core_ids=[0]).results[0]["out_0"]
    return np.ascontiguousarray(np.moveaxis(r, 1, 0).reshape(D, T).T[None, META:])
```

```python
from contextlib import ExitStack

import concourse.bass as bass
from concourse import mybir

F32 = mybir.dt.float32
F32R = mybir.dt.float32r
ALU = mybir.AluOpType
ACT = mybir.ActivationFunctionType
AX_X = mybir.AxisListType.X

P = 128
D = 1024
DK = D // P
META = 16
T = 512 + META
TH = T // 2
LAYERS = 2
W5 = 512
MT = W5 // P
GROUPS, GC, GS = 32, 16, 64
L = P // GC
NC = T // L
GB = 4
NB = GROUPS // GB
PADW = (2 * L - 1) * GC
SP2 = LAYERS * GROUPS
FF = 1536
FT = FF // P
EXPERTS = 8
TOK = 88
TB = T // TOK
S = 216
SH = S // 2
WIDTHS = (128, 160, 192, S)
QMAX = -(-T // S) - 1
EXTRA = 2 * T // S
SLOTS = (EXPERTS + EXTRA) * S
ZROWS = 8
U32 = mybir.dt.uint32
EPS = 1e-6
LRU_C = 8.0

UNIT = 8 * P
RING = 3
U_IN = 28
U_GLU = 2
U_MIX = U_IN + U_GLU + 8 + 8
U_FF = 3 * FT
STEP = 6
BODY = 6
SLOT3 = 3
UNITS = LAYERS * U_MIX + (2 + EXPERTS) * U_FF
ACC_MIX, ACC_FF = 28, 16

COLS, _at = {}, 0
for _name, _n in (("mix_norm", 8), ("ffn_norm", 8), ("merge_bias", 16), ("conv_w", 16), ("conv_b", 4),
                  ("b_r", 4), ("b_i", 4), ("lam", 4), ("b_glu", 4), ("s5_d", 32)):
    COLS[_name] = (_at, _n)
    _at += LAYERS * _n
NCOL = _at


def build(nc, xT, W, cols_d, s5p, s5m, wg, rw, rb, fg, out, hs_d, u_d, y_d, xg_d, yg_d):
    ctx = ExitStack()
    with ctx:
        cursor = [16512]

        def region(nbytes):
            start = cursor[0]
            cursor[0] += (nbytes + 31) // 32 * 32
            return start

        def place(name, shape, dt=F32, at=None):
            n = 4
            for s in shape[1:]:
                n *= s
            if at is None:
                start = region(n)
            else:
                start = at[0]
                at[0] += (n + 31) // 32 * 32
                assert at[0] <= at[1], name
            return nc.alloc_sbuf_tensor_at(name, shape, dt, offset=start)

        def shared(nbytes):
            start = region(nbytes)
            return lambda: [start, start + nbytes]

        def sem(name):
            return ctx.enter_context(nc.semaphore(name))

        H = shared(4 * 2 * DK * T)
        h = H()
        hs = place("hs", [P, DK, T], at=h)
        hn = place("hn", [P, DK, T], at=h)
        gates = place("gates", [P, 2 * DK, T], at=H())
        xh_at = cursor[0]
        xh = place("xh", [P, DK, T], F32R)
        xl = place("xl", [P, DK, T], F32R)
        raw = [place(f"raw{i}", [P, UNIT]) for i in range(RING)]
        wh = [place(f"wh{i}", [P, UNIT], F32R) for i in range(RING)]
        wl = [place(f"wl{i}", [P, UNIT], F32R) for i in range(RING)]
        FFR = shared(4 * 2 * FT * T)
        f = FFR()
        fh = place("fh", [P, FT, T], F32R, at=f)
        fl = place("fl", [P, FT, T], F32R, at=f)
        f = FFR()
        y1h = place("y1h", [P, MT, T], F32R, at=f)
        y1l = place("y1l", [P, MT, T], F32R, at=f)
        y2h = place("y2h", [P, MT, T], F32R, at=f)
        y2l = place("y2l", [P, MT, T], F32R, at=f)
        ybh = place("ybh", [P, MT, T], F32R, at=f)
        ybl = place("ybl", [P, MT, T], F32R, at=f)
        start = FFR()[0]
        f = [start, start + 4 * 4 * MT * T]
        m1 = place("m1", [P, GB, P], at=f)
        m1y = place("m1y", [P, GB, P], at=f)
        m2 = place("m2", [P, GB, P], at=f)
        m2y = place("m2y", [P, GB, P], at=f)
        m3 = place("m3", [P, GB, P], at=f)
        m1t = place("m1t", [P, GB, PADW], at=f)
        cosT = place("cosT", [P, GB, NC], at=f)
        sinT = place("sinT", [P, GB, NC], at=f)
        decay = place("decay", [P, GB, NC], at=f)
        rot = place("rot", [P, GB, NC], at=f)
        rot2 = place("rot2", [P, GB, NC], at=f)
        turned = place("turned", [P, GB, NC], at=f)
        cr = place("cr", [P, GB, NC], at=f)
        sr = place("sr", [P, GB, NC], at=f)
        pbuf = place("pbuf", [P, 2, 4, GB * GC], at=f)
        b2s = place("b2s", [P, GB, GC], at=f)
        bx = place("bx", [P, GB, GC], at=f)
        by = place("by", [P, GB, GC], at=f)
        c1 = place("c1", [P, GB, GC], at=f)
        c2 = place("c2", [P, GB, GC], at=f)
        pt1 = place("pt1", [P, GB * P], at=f)
        pt2 = place("pt2", [P, GB * P], at=f)
        dt1 = place("dt1", [P, GB * P], at=f)
        LR = shared(4 * (14 * T + T + 3 + 8))
        f = LR()
        xc = place("xc", [P, MT, T], at=f)
        gg = place("gg", [P, MT, T], at=f)
        ra = place("ra", [P, 2, T], at=f)
        ii = place("ii", [P, 2, T], at=f)
        th = place("th", [P, 2, T], at=f)
        xpad = place("xpad", [P, T + 3], at=f)
        uperm = place("uperm", [P, MT, L, NC], at=[LR()[0] + 4 * 8 * T, LR()[1]])
        f = LR()
        gt = place("gt", [P, 2, T], at=f)
        ft = place("ft", [P, 2, T], at=f)
        f = [LR()[0] + 4 * 12 * T, LR()[1]]
        zero = place("zero", [P, D], at=f)
        f = LR()
        pp = {n: place("p_" + n, [P, SP2], at=f) for n in
              ("lr", "li", "ldt", "dt", "ang", "k", "red", "red2", "sin", "cos", "mag", "num", "den",
               "rden", "t1", "t2", "t3")}

        UU = shared(4 * GROUPS * NC)
        uu = place("uu", [P, GROUPS, NC], at=UU())
        yt = place("yt", [P, MT, L, NC], at=UU())
        ys = place("ys", [P, 2, GB, NC])
        rs = place("rs", [P, T], at=[LR()[0] + 4 * 8 * T, LR()[1]])
        cols = place("cols", [P, NCOL])
        apr = place("apr", [P, L + 1, SP2])
        api = place("api", [P, L + 1, SP2])
        sqr = place("sqr", [P, 7, SP2])
        sqi = place("sqi", [P, 7, SP2])
        mag8 = place("mag8", [P, SP2])
        cfr = place("cfr", [P, SP2])
        cfi = place("cfi", [P, SP2])
        sp8 = place("sp8", [P, LAYERS * MT])
        sp8n = place("sp8n", [P, LAYERS * MT])
        spt = [place(f"spt{i}", [P, LAYERS * MT]) for i in range(4)]
        sgn = place("sgn", [P, 2])
        warm = place("warm", [P, 1])
        ones = place("ones", [P, P])
        ident = place("ident", [P, P])
        gw = place("gw", [P, 2, MT, LRU_WB])
        rws = place("rws", [P, DK, EXPERTS])
        rbs = place("rbs", [P, EXPERTS])
        lg = place("lg", [P, TB, EXPERTS])
        cmp1 = place("cmp1", [P, TB, EXPERTS, EXPERTS], at=[UU()[0], UU()[1]])
        cmp2 = place("cmp2", [P, TB, EXPERTS, EXPERTS], at=[UU()[0] + 4 * TB * 64, UU()[1]])
        rank = place("rank", [P, TB, EXPERTS])
        gate = place("gate", [P, TB, EXPERTS])
        gtmp = place("gtmp", [P, TB, EXPERTS])
        v1, v2, ex, g1, g2 = (place(n, [P, TB]) for n in ("v1", "v2", "ex", "g1", "g2"))
        idx = place("idx", [P, 2, TB], U32)
        tab = place("tab", [P, EXTRA + 1 + EXPERTS], U32)
        ssq = place("ssq", [P, TB])

        f = [xh_at, xh_at + 4 * 2 * DK * T]
        hn_tok = place("hn_tok", [TOK, TB, D], at=f)
        f = [xh_at, xh_at + 4 * 2 * DK * T]
        xg = place("xg", [P, DK, 2, S], F32R, at=f)
        f = FFR()
        fg2 = place("fg2", [P, FT, 2, S], F32R, at=f)
        hs_tok = place("hs_tok", [TOK, TB, D], at=f)
        gmb = place("gmb", [TOK, D], at=f)
        f = LR()
        tri = place("tri", [P, EXPERTS, EXPERTS], at=f)
        tris = place("tris", [P, TOK], at=f)
        sel1 = place("sel1", [P, TB, EXPERTS], at=f)
        sel2 = place("sel2", [P, TB, EXPERTS], at=f)
        mask = place("mask", [P, TB, EXPERTS], at=f)
        off = place("off", [P, TB + 1, EXPERTS], at=f)
        pos = place("pos", [P, TB, EXPERTS], at=f)
        qq = place("qq", [P, TB, EXPERTS], at=f)
        big = place("big", [P, TB, EXPERTS], at=f)
        slot = place("slot", [P, TB, EXPERTS], at=f)
        ev, oneE, extra, incl, ebase, xtmp = (place(n, [P, EXPERTS], at=f) for n in
                                              ("ev", "oneE", "extra", "incl", "ebase", "xtmp"))
        iv = place("iv", [P, EXTRA], at=f)
        oneI = place("oneI", [P, EXTRA], at=f)
        in1 = place("in1", [P, EXTRA, EXPERTS], at=f)
        in2 = place("in2", [P, EXTRA, EXPERTS], at=f)
        tabf = place("tabf", [P, EXTRA + 1 + EXPERTS], at=f)
        sf = place("sf", [P, 2, TB], at=f)
        f = [LR()[0] + 4 * 3 * T, LR()[1]]
        gs, gx, us, fx = (place(n, [P, SLOT3, S], at=f) for n in ("gs", "gx", "us", "fx"))
        xt = place("xt", [SH, 2, D], at=f)
        f = H()
        f[0] += 4 * DK * T
        y_t = place("y_t", [P, DK, S], at=f)
        ytok = place("ytok", [SH, 2, D], at=f)
        f = H()
        ya = place("ya", [TOK, 2, D], at=f)
        yb = place("yb", [TOK, 2, D], at=f)
        f = [xh_at, xh_at + 4 * 2 * DK * T]
        ot = place("ot", [TOK, 2, D], at=f)
        sqt = place("sqt", [TOK, D], at=f)
        assert cursor[0] <= nc.sbuf_usable_end

        acc = ctx.enter_context(nc.psum_tensor("acc", [P, 2, 2, 512], F32))
        side = ctx.enter_context(nc.psum_tensor("side", [P, 4, 512], F32))

        raw_landed = [sem(f"raw_landed{i}") for i in range(RING)]
        hi_ready = [sem(f"hi_ready{i}") for i in range(RING)]
        lo_ready = [sem(f"lo_ready{i}") for i in range(RING)]
        unit_done = [sem(f"unit_done{i}") for i in range(RING)]
        acc_free = [sem(f"acc_free{i}") for i in range(2)]
        x_landed, small_landed = sem("x_landed"), sem("small_landed")
        const_ready = sem("const_ready")
        hs_ready, sq_ready, ss_ready, rms_ready = sem("hs_ready"), sem("sq_ready"), sem("ss_ready"), sem("rms_ready")
        hn_ready, xh_ready, xl_ready = sem("hn_ready"), sem("xh_ready"), sem("xl_ready")
        hs_saved, hs_back = sem("hs_saved"), sem("hs_back")
        prep_act, prep_dve, prep_pool = sem("prep_act"), sem("prep_dve"), sem("prep_pool")
        up_ready, u_out, u_in = sem("up_ready"), sem("u_out"), sem("u_in")
        xp_ready, xc_ready, gg_ready = sem("xp_ready"), sem("xc_ready"), sem("gg_ready")
        gm_done, ri_ready = sem("gm_done"), sem("ri_ready")
        lru_a, lru_t, lru_m, lru_r = sem("lru_a"), sem("lru_t"), sem("lru_m"), sem("lru_r")
        yb_ready, ybh_ready, ybl_ready = sem("yb_ready"), sem("ybh_ready"), sem("ybl_ready")
        gates_ready = sem("gates_ready")
        pb_landed = [sem("pb_landed0"), sem("pb_landed1")]
        wg_landed = sem("wg_landed")
        m1t_ready, tab_ready, c_ready = sem("m1t_ready"), sem("tab_ready"), sem("c_ready")
        p1_done, p2_done, p3_done = sem("p1_done"), sem("p2_done"), sem("p3_done")
        m_act, m_dve, m2_ready, rot_ready = sem("m_act"), sem("m_dve"), sem("m2_ready"), sem("rot_ready")
        ys_ready, y_out, y_in = sem("ys_ready"), [sem("y_out0"), sem("y_out1")], sem("y_in")
        y1_ready, y1h_ready, y1l_ready = sem("y1_ready"), sem("y1h_ready"), sem("y1l_ready")
        sg_ready, y2_ready, y2h_ready, y2l_ready = sem("sg_ready"), sem("y2_ready"), sem("y2h_ready"), sem("y2l_ready")
        mg_ready = sem("mg_ready")
        g_ready, f_ready, fh_ready, fl_ready = sem("g_ready"), sem("f_ready"), sem("fh_ready"), sem("fl_ready")
        lg_done, ex_ready, d_ready, mask_ready, pos_done, slot_ready, tab_ready2 = (
            sem(n) for n in ("lg_done", "ex_ready", "d_ready", "mask_ready", "pos_done", "slot_ready", "table_ready"))
        acc_set = sem("acc_set")
        zero_set, zeroed, tok_done, hn_tok_ready, hs_tok_ready, scattered, gm_landed = (
            sem(n) for n in ("zero_set", "zeroed", "tok_done", "hn_tok_ready", "hs_tok_ready", "scattered", "gm_landed"))
        xt_landed, xt_read, xgh_ready, xgl_ready = (sem(n) for n in ("xt_landed", "xt_read", "xgh_ready", "xgl_ready"))
        half_ready = [sem("half_ready0"), sem("half_ready1")]
        gx_ready, fx_ready, fgh_ready, fgl_ready = sem("gx_ready"), sem("fx_ready"), sem("fgh_ready"), sem("fgl_ready")
        y_tr, ytok_ready, y_stored, all_stored = sem("y_tr"), sem("ytok_ready"), sem("y_stored"), sem("all_stored")
        ya_in, sum_ready, rms2_ready, sq2_ready, ot_ready = (
            [sem("ya_in0"), sem("ya_in1")], sem("sum_ready"), sem("rms2_ready"), sem("sq2_ready"), sem("ot_ready"))
        out_done = [sem("out_done0"), sem("out_done1")]
        act_chain, dve_chain, pool_chain = sem("act_chain"), sem("dve_chain"), sem("pool_chain")

        block = ctx.enter_context(nc.Block())
        ZDMAS = -(-SLOTS // P) - (-EXTRA * S // P)

        def col(name, layer, tile):
            at, n = COLS[name]
            return cols[:, at + layer * n + tile:at + layer * n + tile + 1]

        def use(u, more=0):
            return u % RING, u // RING + more

        def halves(x):
            return x.rearrange("p (b c) -> p b c", b=2)

        def perm(x):
            return x.rearrange("p j c -> p c j")

        def chunked(x):
            return x.rearrange("p (c j) -> p c j", j=L)

        mix_u = [0, U_MIX + 2 * U_FF]
        mix_acc = [0, ACC_MIX + 2 * ACC_FF]
        ff_u = [U_MIX, 2 * U_MIX + 2 * U_FF]
        ff_acc = [ACC_MIX, 2 * ACC_MIX + 2 * ACC_FF]
        ff_e0 = [0, 2]
        ff_n = [2, EXPERTS]
        hs_at_norm = [0, 8, 24, 32, 96]

        def slot_of(k):
            return divmod(k - 4, 3) if k >= 4 else (None, None)

        KIND = [("u", m) for m in range(MT)]
        for m in range(MT):
            KIND += [("x", m), ("g", m)]
        KIND += [("gate", q) for q in range(2 * DK)]

        @block.sync
        def _(sp):
            sp.dma_start(cols[:, :], cols_d).then_inc(small_landed, 16)
            for m in range(DK):
                sp.dma_start(hs[:, m, :], xT[:, m, :]).then_inc(x_landed, 16)
            for u in range(RING):
                sp.dma_start(raw[u][:, :], W[u, :, :]).then_inc(raw_landed[u], 16)
            with sp.Fori(1, UNITS // RING) as it:
                for s in range(RING):
                    sp.wait_ge(lo_ready[s], it)
                    sp.dma_start(raw[s][:, :], W[it * RING + s, :, :]).then_inc(raw_landed[s], 16)
            for u in range(UNITS // RING * RING, UNITS):
                s, n = use(u)
                sp.wait_ge(lo_ready[s], n)
                sp.dma_start(raw[s][:, :], W[u, :, :]).then_inc(raw_landed[s], 16)
            sp.wait_ge(tab_ready2, 1)
            n_extra = sp.value_load(tab[0:1, 0:1], min_val=0, max_val=EXTRA)
            with sp.If(n_extra > 0):
                with sp.Fori(0, n_extra) as i:
                    e = sp.value_load(tab[0:1, bass.ds(i + 1, 1)], min_val=0, max_val=EXPERTS - 1)
                    with sp.Fori(0, U_FF // RING) as it:
                        for j in range(RING):
                            s, n = use(UNITS + j, i * (U_FF // RING) + it)
                            sp.wait_ge(lo_ready[s], n)
                            sp.dma_start(raw[s][:, :], W[e * U_FF + it * RING + (ff_u[1] + j), :, :])\
                              .then_inc(raw_landed[s], 16)
            for t in range(TB):
                sp.wait_ge(ot_ready, t + 1)
                sp.dma_start(out[t * TOK:(t + 1) * TOK, :], ot[:, t % 2, :]).then_inc(out_done[t % 2], 16)
            for i in range(2):
                sp.wait_ge(out_done[i], 16 * TB // 2)

        @block.gpsimd
        def _(pool):
            g = nc.gpsimd
            chain = [0]

            def link(ins):
                chain[0] += 1
                ins.then_inc(pool_chain, 1)
                pool.wait_ge(pool_chain, chain[0])

            def tt(out, a, b, op):
                link(g.tensor_tensor(out, a, b, op))

            for n, i in (("lr", 0), ("li", 1), ("ldt", 2)):
                pool.dma_start(pp[n][:, :], s5p[:, i, :]).then_inc(prep_pool, 16)
            g.memset(ones[:, :], 1.0).then_inc(const_ready, 1)
            link(g.memset(ident[:, :], 0.0))
            g.affine_select(out=ident[:, :], in_=ident[:, :], compare_op=ALU.not_equal, fill=1.0, base=0,
                            pattern=[[-1, P]], channel_multiplier=1).then_inc(const_ready, 1)
            pool.wait_ge(const_ready, 2)
            link(g.memset(apr[:, 0, :], 1.0))
            link(g.memset(api[:, 0, :], 0.0))
            g.memset(xpad[:, 0:3], 0.0).then_inc(const_ready, 1)
            pool.dma_start(rws[:, :, :], rw).then_inc(prep_pool, 16)
            pool.dma_start(rbs[:, :], rb).then_inc(prep_pool, 16)
            pool.wait_ge(prep_act, 4)
            t1, t2 = pp["t1"][:, :], pp["t2"][:, :]
            c, s = pp["cos"][:, :], pp["sin"][:, :]
            tt(apr[:, 1, :], pp["mag"][:, :], c, ALU.mult)
            tt(api[:, 1, :], pp["mag"][:, :], s, ALU.mult)

            def product(outr, outi, ar, ai, br, bi, x1=t1, x2=t2):
                tt(x1, ar, br, ALU.mult)
                tt(x2, ai, bi, ALU.mult)
                tt(x1, x1, x2, ALU.subtract)
                tt(x2, ar, bi, ALU.mult)
                tt(outi, ai, br, ALU.mult)
                tt(outi, outi, x2, ALU.add)
                link(g.tensor_copy(outr, x1))

            pool.wait_ge(prep_dve, 2)
            link(g.tensor_scalar(pp["num"][:, :], apr[:, 1, :], 1.0, 0.0, ALU.subtract, ALU.add))
            num, lr, li = pp["num"][:, :], pp["lr"][:, :], pp["li"][:, :]
            tt(t1, num, lr, ALU.mult)
            tt(t2, api[:, 1, :], li, ALU.mult)
            tt(t1, t1, t2, ALU.add)
            tt(cfr[:, :], t1, pp["rden"][:, :], ALU.mult)
            tt(t1, api[:, 1, :], lr, ALU.mult)
            tt(t2, num, li, ALU.mult)
            tt(t1, t1, t2, ALU.subtract)
            tt(cfi[:, :], t1, pp["rden"][:, :], ALU.mult)
            for k in range(2, L + 1):
                product(apr[:, k, :], api[:, k, :], apr[:, k - 1, :], api[:, k - 1, :], apr[:, 1, :], api[:, 1, :])
            ur, ui = sqr[:, 0, :], sqi[:, 0, :]
            product(ur, ui, c, s, c, s)
            t3 = pp["t3"][:, :]
            n = 2
            while n < L:
                tt(t1, ur, ur, ALU.mult)
                tt(t2, ui, ui, ALU.mult)
                tt(t3, ur, ui, ALU.mult)
                tt(ur, t1, t2, ALU.subtract)
                tt(ui, t3, t3, ALU.add)
                n *= 2
            tt(t1, ur, ur, ALU.mult)
            tt(t2, ui, ui, ALU.mult)
            tt(t1, t1, t2, ALU.add)
            link(g.tensor_scalar(t1, t1, -0.5, 1.5, ALU.mult, ALU.add))
            tt(ur, ur, t1, ALU.mult)
            tt(ui, ui, t1, ALU.mult)
            for k in range(1, 7):
                ar, ai = sqr[:, k - 1, :], sqi[:, k - 1, :]
                tt(t1, ar, ar, ALU.mult)
                tt(t2, ai, ai, ALU.mult)
                tt(t3, ar, ai, ALU.mult)
                tt(sqr[:, k, :], t1, t2, ALU.subtract)
                tt(sqi[:, k, :], t3, t3, ALU.add)

            for l in range(LAYERS):
                if l:
                    pool.wait_ge(hs_ready, hs_at_norm[1])
                    link(g.memset(zero[:, :], 0.0))
                    for z in range(0, SLOTS, P):
                        n = min(P, SLOTS - z)
                        pool.dma_start(xg_d[z:z + n, :], zero[0:n, :]).then_inc(zeroed, 16)
                    for z in range(EXPERTS * S, SLOTS, P):
                        n = min(P, SLOTS - z)
                        pool.dma_start(yg_d[z:z + n, :], zero[0:n, :]).then_inc(zeroed, 16)
                    pool.wait_ge(zeroed, ZDMAS * 16)
                    pool.wait_ge(hs_ready, hs_at_norm[2])
                for r in range(2):
                    pool.dma_start(gw[:, r, :, :], wg[l, :, r, :, :]).then_inc(wg_landed, 16)
                for b in range(2):
                    pool.dma_start(pbuf[:, b, :, :], s5m[l, b, :, :, :]).then_inc(pb_landed[b], 16)
                link(g.memset(m1t[:, :, L * GC:PADW], 0.0))
                link(g.memset(cosT[:, :, 0:1], 1.0))
                link(g.memset(sinT[:, :, 0:1], 0.0))
                link(g.memset(decay[:, :, 0:1], 0.0))
                for b in range(NB):
                    done = l * NB + b
                    gs = slice(l * GROUPS + b * GB, l * GROUPS + (b + 1) * GB)
                    v = lambda x: x.rearrange("p (g h) -> p g h", g=GB)
                    b1, braw, craw1, craw2 = (v(pbuf[:, b % 2, i, :]) for i in range(4))
                    wide = [P, GB, GC]
                    cb = lambda x: x[:, gs].unsqueeze(2).to_broadcast(wide)
                    pool.wait_ge(pb_landed[b % 2], 16 * (l * NB // 2 + b // 2 + 1))
                    if done:
                        pool.wait_ge(p1_done, done)
                        pool.wait_ge(m2_ready, done)
                    link(g.tensor_scalar(b2s[:, :, :], braw, sgn[:, 0:1], 0.0, ALU.mult, ALU.add))
                    link(g.tensor_scalar(c1[:, :, :], craw1, sgn[:, 1:2], 0.0, ALU.mult, ALU.add))
                    g.tensor_scalar(c2[:, :, :], craw2, -1.0, 0.0, ALU.mult, ALU.add).then_inc(c_ready, 1)
                    x1, x2 = v(pt1[:, 0:GB * GC]), v(pt2[:, 0:GB * GC])
                    tt(x1, cb(cfr), b1, ALU.mult)
                    tt(x2, cb(cfi), b2s[:, :, :], ALU.mult)
                    tt(bx[:, :, :], x1, x2, ALU.add)
                    tt(x1, cb(cfr), b2s[:, :, :], ALU.mult)
                    tt(x2, cb(cfi), b1, ALU.mult)
                    tt(by[:, :, :], x1, x2, ALU.subtract)
                    pool.wait_ge(c_ready, done + 1)
                    if b + 2 < NB:
                        pool.dma_start(pbuf[:, b % 2, :, :], s5m[l, b + 2, :, :, :]).then_inc(pb_landed[b % 2], 16)
                    for j in range(L):
                        ab = lambda x: x[:, L - 1 - j, gs].unsqueeze(2).to_broadcast(wide)
                        y1, y2 = (v(x[:, j * 64:j * 64 + 64]) for x in (pt1, pt2))
                        g.tensor_tensor(y1, ab(apr), bx[:, :, :], ALU.mult)
                        last = g.tensor_tensor(y2, ab(api), by[:, :, :], ALU.mult)
                    link(last)
                    w4 = lambda x: x[:, :].rearrange("p (j g h) -> p g j h", g=GB, h=GC)
                    g.tensor_tensor(m1t[:, :, 0:L * GC].rearrange("p g (j h) -> p g j h", h=GC), w4(pt1), w4(pt2),
                                    ALU.add).then_inc(m1t_ready, 1)
                    if done:
                        pool.wait_ge(rot_ready, done)
                    pool.wait_ge(m1t_ready, done + 1)
                    col1 = lambda x: x[:, gs].unsqueeze(2).to_broadcast([P, GB, NC - 1])
                    link(g.tensor_copy(decay[:, :, 1:NC], col1(mag8)))
                    link(g.tensor_copy(cosT[:, :, 1:2], sqr[:, 0, gs].unsqueeze(2)))
                    link(g.tensor_copy(sinT[:, :, 1:2], sqi[:, 0, gs].unsqueeze(2)))
                    k = 1
                    for i in range(1, 7):
                        k *= 2
                        n = min(k, NC - k)
                        br = sqr[:, i, gs].unsqueeze(2).to_broadcast([P, GB, n])
                        bi = sqi[:, i, gs].unsqueeze(2).to_broadcast([P, GB, n])
                        z1, z2, z3, z4 = (x[:, o:o + GB * n].rearrange("p (g c) -> p g c", g=GB)
                                          for x in (pt1, pt2) for o in (0, 256))
                        g.tensor_tensor(z1, cosT[:, :, 0:n], br, ALU.mult)
                        g.tensor_tensor(z3, sinT[:, :, 0:n], bi, ALU.mult)
                        g.tensor_tensor(z2, cosT[:, :, 0:n], bi, ALU.mult)
                        tt(z4, sinT[:, :, 0:n], br, ALU.mult)
                        g.tensor_tensor(cosT[:, :, k:k + n], z1, z3, ALU.subtract)
                        last = g.tensor_tensor(sinT[:, :, k:k + n], z2, z4, ALU.add)
                        if i < 6:
                            link(last)
                    last.then_inc(tab_ready, 1)
                    pool.wait_ge(tab_ready, done + 1)
            pool.wait_ge(xl_ready, 5 * DK)
            pool.dma_start(gmb[:, :], fg).then_inc(gm_landed, 16)
            link(g.memset(tris[:, :], 1.0))
            link(g.affine_select(out=tris[:, :], in_=tris[:, :], compare_op=ALU.is_gt, fill=0.0, base=0,
                                 pattern=[[1, TOK]], channel_multiplier=-1))
            link(g.memset(tri[:, :, :], 1.0))
            g.affine_select(out=tri[:, :, :], in_=tri[:, :, :], compare_op=ALU.is_gt, fill=0.0, base=0,
                            pattern=[[1, EXPERTS], [-1, EXPERTS]], channel_multiplier=0).then_inc(const_ready, 1)

            pool.wait_ge(zeroed, ZDMAS * 16)
            pool.wait_ge(slot_ready, 1)
            for t in range(TB):
                pool.wait_ge(hn_tok_ready, t + 1)
                for k in range(2):
                    pool.indirect_dma_start(xg_d, bass.IndirectOffsetOnAxis(ap=idx[0:TOK, k, t:t + 1], axis=0),
                                            hn_tok[:, t, :], None).then_inc(scattered, 16)
            pool.wait_ge(scattered, 2 * TB * 16)

            def rows(d, b):
                return d[bass.ds(b * S, S), :].rearrange("(h p) c -> p h c", h=2)

            def lower_hidden(b):
                with pool.Fori(0, FT // BODY) as it:
                    for i in range(BODY):
                        m = it * BODY + i
                        pool.wait_ge(fgh_ready, b * FT + m + 1)
                        g.tensor_tensor(fg2[:, m, 1, :], fx[:, i % SLOT3, :], fg2[:, m, 0, :].bitcast(F32), ALU.subtract)\
                            .then_inc(fgl_ready, 1)

            pool.dma_start(xt[:, :, :], xg_d[0:S, :].rearrange("(h p) c -> p h c", h=2)).then_inc(xt_landed, 16)
            with pool.Fori(1, EXPERTS) as b:
                pool.wait_ge(xt_read, b)
                pool.dma_start(xt[:, :, :], rows(xg_d, b)).then_inc(xt_landed, 16)
                lower_hidden(b - 1)
            lower_hidden(EXPERTS - 1)
            pool.wait_ge(tab_ready2, 1)
            n_extra = pool.value_load(tab[0:1, 0:1], min_val=0, max_val=EXTRA)
            with pool.If(n_extra > 0):
                with pool.Fori(0, n_extra) as i:
                    pool.wait_ge(xt_read, i + EXPERTS)
                    pool.dma_start(xt[:, :, :], rows(xg_d, i + EXPERTS)).then_inc(xt_landed, 16)
                    lower_hidden(i + EXPERTS)
            pool.wait_ge(y_stored, (n_extra + (EXPERTS + 1)) * 16)
            pool.sem_inc(all_stored, 1)
            pool.wait_ge(all_stored, 1)
            for t in range(TB):
                if t >= 2:
                    pool.wait_ge(sum_ready, t - 1)
                for k, dst in ((0, ya), (1, yb)):
                    pool.indirect_dma_start(dst[:, t % 2, :], None, yg_d,
                                            bass.IndirectOffsetOnAxis(ap=idx[0:TOK, k, t:t + 1], axis=0))\
                        .then_inc(ya_in[t % 2], 16)

        @block.scalar
        def _(act):
            a = nc.scalar
            chain = [0]

            def link(ins):
                chain[0] += 1
                ins.then_inc(act_chain, 1)
                act.wait_ge(act_chain, chain[0])

            def split_hi(u, more=0):
                if isinstance(u, int) and isinstance(more, int) and u + RING * more >= UNITS:
                    return
                s, n = use(u, more)
                act.wait_ge(raw_landed[s], n * 16 + 16)
                if u >= RING:
                    act.wait_ge(unit_done[s], n)
                a.activation(wh[s][:, :], raw[s][:, :], ACT.Copy).then_inc(hi_ready[s], 1)

            def arrived(u, more=0):
                s, n = use(u, more)
                act.wait_ge(unit_done[s], n + 1)

            def norm(i):
                for m in range(DK):
                    if i == 0:
                        act.wait_ge(x_landed, 16 * DK)
                    else:
                        act.wait_ge(hs_ready, hs_at_norm[i] - DK + m + 1)
                    a.activation(hn[:, m, :], hs[:, m, :], ACT.Square).then_inc(sq_ready, 1)
                act.wait_ge(ss_ready, i + 1)
                link(a.activation(halves(rs[:, :]), side[:, 0:2, 0:TH], ACT.Copy, scale=1.0 / D))
                a.activation(rs[:, :], rs[:, :], ACT.Sqrt, bias=EPS).then_inc(rms_ready, 1)
                if i == 3:
                    return
                for m in range(DK):
                    act.wait_ge(hn_ready, i * DK + m + 1)
                    a.activation(xh[:, m, :], hn[:, m, :], ACT.Copy).then_inc(xh_ready, 1)

            def lru_pair(l, q):
                n = l * 2 + q
                act.wait_ge(ri_ready, 4 * n + 4)
                act.wait_ge(prep_dve, 4)
                if n:
                    act.wait_ge(yb_ready, 2 * n)
                for i in range(2):
                    t = l * MT + 2 * q + i
                    a.activation(th[:, i, :], ra[:, i, :], ACT.Tanh, scale=sp8[:, t:t + 1]).then_inc(lru_t, 1)
                act.wait_ge(lru_t, 2 * n + 2)
                for i in range(2):
                    t = l * MT + 2 * q + i
                    a.activation(ra[:, i, :], ra[:, i, :], ACT.Exp, scale=sp8n[:, t:t + 1]).then_inc(lru_a, 1)
                act.wait_ge(lru_m, n + 1)
                a.activation(th[:, :, :], th[:, :, :], ACT.Sqrt).then_inc(lru_r, 1)

            def lru_out(l, q):
                for t in (2 * q, 2 * q + 1):
                    act.wait_ge(yb_ready, l * MT + t + 1)
                    a.activation(ybh[:, t, :], gg[:, t, :], ACT.Copy).then_inc(ybh_ready, 1)

            def gate_sigmoid(l, q):
                t, r = q // 2, q % 2
                act.wait_ge(gm_done, l * 8 + q + 1)
                act.wait_ge(u_out, 64 * (l + 1))
                dst = (ra, ii)[r]
                if t >= 2:
                    act.wait_ge(yb_ready, l * MT + 2)
                a.activation(halves(dst[:, t % 2, :]), side[:, 2:4, 0:TH], ACT.Sigmoid,
                             bias=col(("b_r", "b_i")[r], l, t)).then_inc(ri_ready, 1)

            def mixer(l):
                u0, a0 = mix_u[l], mix_acc[l]
                for k in range(U_IN):
                    split_hi(u0 + k + 2)
                    kind, m = KIND[k]
                    arrived(u0 + k)
                    src = acc[:, k % 2, :, 0:TH]
                    if kind == "u":
                        if l and m == 0:
                            act.wait_ge(hs_ready, hs_at_norm[2])
                        a.activation(uperm[:, m, :, :].rearrange("p j (b c) -> p b c j", b=2),
                                     src.rearrange("p b (c j) -> p b c j", j=L), ACT.Copy).then_inc(acc_free[k % 2], 1)
                        act.wait_ge(acc_free[k % 2], a0 + k // 2 + 1)
                        act.dma_start(u_d[8 * m:8 * m + 8].rearrange("g h j c -> (g h) (j c)"),
                                      uperm[:, m, :, :].rearrange("p j c -> p (j c)")).then_inc(u_out, 16)
                    elif kind == "x":
                        if m or l:
                            act.wait_ge(xc_ready, l * MT + m)
                        if m == 0:
                            act.wait_ge(const_ready, 3)
                        a.activation(halves(xpad[:, 3:3 + T]), src, ACT.Copy).then_inc(acc_free[k % 2], 1)
                    elif kind == "g":
                        a.activation(halves(gg[:, m, :]), src, ACT.Gelu_apprx_tanh).then_inc(acc_free[k % 2], 1)
                    else:
                        if m == 0:
                            act.wait_ge(xl_ready, xl_at_norm(2 * l) + DK)
                            if l:
                                act.wait_ge(hs_saved, 16)
                        a.activation(halves(gates[:, m, :]), src, ACT.Sigmoid,
                                     bias=col("merge_bias", l, m)).then_inc(acc_free[k % 2], 1)
                    if k == 4:
                        act.wait_ge(u_out, 64 * (l + 1))
                        for j in range(L):
                            act.dma_start(uu[j * GC:(j + 1) * GC, :, :],
                                          u_d[:, :, j, :].rearrange("g h c -> h g c")).then_inc(u_in, 16)
                    b, part = slot_of(k)
                    if b is None:
                        continue
                    n = l * NB + b
                    if part == 0:
                        act.wait_ge(p1_done, n + 1)
                        mt = side[:, 0, :].rearrange("p (g s) -> p g s", g=GB)
                        a.activation(m1[:, :, :], mt, ACT.Copy)
                        a.activation(m1y[:, :, 0:GS], mt[:, :, GS:P], ACT.Copy)
                        a.activation(m1y[:, :, GS:P], mt[:, :, 0:GS], ACT.Copy, scale=-1.0).then_inc(m_act, 1)
                        if 1 <= b <= MT:
                            gate_sigmoid(l, 2 * b - 1)
                        if b in (2, 4):
                            lru_pair(l, b // 2 - 1)
                    elif part == 1 and b in (2, 4):
                        lru_out(l, b // 2 - 1)
                    elif part == 2:
                        act.wait_ge(p3_done, n + 1)
                        if n >= 2:
                            act.wait_ge(y_out[b % 2], 16 * L * (n // 2))
                        a.activation(ys[:, b % 2, :, :],
                                     side[:, 0, 0:GB * NC].rearrange("p (g c) -> p g c", g=GB),
                                     ACT.Copy).then_inc(ys_ready, 1)
                        act.wait_ge(ys_ready, n + 1)
                        for j in range(L):
                            act.dma_start(y_d[b * GB:(b + 1) * GB, :, j, :].rearrange("g h c -> h g c"),
                                          ys[j * GC:(j + 1) * GC, b % 2, :, :]).then_inc(y_out[b % 2], 16)
                        if b < MT:
                            gate_sigmoid(l, 2 * b)
                for i in range(2):
                    act.wait_ge(y_out[i], 16 * L * NB // 2 * (l + 1))
                act.dma_start(yt[:, :, :, :].rearrange("p m j c -> p m (j c)"),
                              y_d.rearrange("(m q) h j c -> (q h) m (j c)", m=MT)).then_inc(y_in, 16)
                act.wait_ge(y_in, 16 * (l + 1))
                for m in range(MT):
                    a.activation(yt[:, m, :, :], yt[:, m, :, :], ACT.Gelu_apprx_tanh).then_inc(y1_ready, 1)
                for m in range(MT):
                    act.wait_ge(y1_ready, l * MT + m + 1)
                    a.activation(chunked(y1h[:, m, :]), perm(yt[:, m, :, :]), ACT.Copy).then_inc(y1h_ready, 1)
                a1 = a0 + U_IN // 2
                for v in range(U_GLU):
                    u = u0 + U_IN + v
                    split_hi(u + 2)
                    arrived(u)
                    for i in range(2):
                        n = l * MT + 2 * v + i
                        if n >= 2:
                            act.wait_ge(y2_ready, n - 1)
                        if v == 0 and i == 0:
                            act.wait_ge(ybl_ready, (l + 1) * MT)
                        a.activation(halves(gt[:, i, :]), acc[:, i, :, 0:TH], ACT.Sigmoid,
                                     bias=col("b_glu", l, 2 * v + i)).then_inc(acc_free[i], 1)
                    for i in range(2):
                        act.wait_ge(y2_ready, l * MT + 2 * v + i + 1)
                        a.activation(y2h[:, 2 * v + i, :], ft[:, i, :], ACT.Copy).then_inc(y2h_ready, 1)
                for m in range(DK):
                    u = u0 + U_IN + U_GLU + m
                    split_hi(u + 2)
                    act.wait_ge(mg_ready, l * DK + m + 1)
                    a.activation(xh[:, m, :], ft[:, 0, :], ACT.Copy).then_inc(xh_ready, 1)
                for m in range(DK):
                    act.dma_start(hs[:, m, :], (hs_d if l else xT)[:, m, :]).then_inc(hs_back, 16)
                for m in range(DK):
                    split_hi(u0 + U_MIX - DK + m + 2)

            def expert(l, u0, e, e_all):
                with act.Fori(0, 2 * FT // STEP) as it:
                    more = e * (U_FF // RING) + it * (STEP // RING)
                    for i in range(STEP // 2):
                        m = it * (STEP // 2) + i
                        u = u0 + 2 * i
                        split_hi(u + 2, more)
                        arrived(u, more)
                        a.activation(halves(gt[:, 0, :]), acc[:, 0, :, 0:TH], ACT.Silu).then_inc(acc_free[0], 1)
                        split_hi(u + 3, more)
                        act.wait_ge(f_ready, e_all * FT + m + 1)
                        a.activation(fh[:, m, :], ft[:, 0, :], ACT.Copy).then_inc(fh_ready, 1)

            def down(u0, e, last):
                more = e * (U_FF // RING)
                for j in range(FT):
                    if not (last and j >= FT - 2):
                        split_hi(u0 + 2 * FT + j + 2, more)

            def silu_table():
                a.activation(warm[:, :], ones[:, 0:1], ACT.Silu)

            act.wait_ge(prep_pool, 16 * 5)
            link(a.activation(pp["dt"][:, :], pp["ldt"][:, :], ACT.Exp))
            a.activation(pp["t1"][:, :], pp["dt"][:, :], ACT.Copy).then_inc(prep_act, 1)
            act.wait_ge(prep_dve, 1)
            link(a.activation(pp["mag"][:, :], pp["num"][:, :], ACT.Exp))
            a.activation(mag8[:, :], pp["num"][:, :], ACT.Exp, scale=float(L)).then_inc(prep_act, 1)
            a.activation(pp["sin"][:, :], pp["red"][:, :], ACT.Sin).then_inc(prep_act, 1)
            a.activation(pp["cos"][:, :], pp["red2"][:, :], ACT.Sin).then_inc(prep_act, 1)
            act.wait_ge(prep_dve, 3)
            a.activation(spt[1][:, :], spt[0][:, :], ACT.Exp, scale=-1.0).then_inc(prep_act, 1)
            split_hi(0)
            split_hi(1)
            norm(0)
            mixer(0)
            norm(1)
            for l in range(LAYERS):
                if l:
                    for m in range(DK):
                        act.wait_ge(hs_ready, hs_at_norm[2] - DK + m + 1)
                    act.dma_start(hs_d, hs[:, :, :]).then_inc(hs_saved, 16)
                    norm(2)
                    mixer(1)
                    split_hi(ff_u[1] + 2)
                    norm(3)
                    continue
                silu_table()
                with act.Fori(0, ff_n[l] - 1) as e:
                    expert(l, ff_u[l], e, e + ff_e0[l])
                    down(ff_u[l], e, False)
                e = ff_n[l] - 1
                expert(l, ff_u[l], e, e + ff_e0[l])
                down(ff_u[l], e, False)

            act.wait_ge(mg_ready, 2 * DK)
            act.wait_ge(d_ready, 1)
            a.activation(ex[0:TOK, :], v2[0:TOK, :], ACT.Exp).then_inc(ex_ready, 1)
            for t in range(TB):
                act.wait_ge(tok_done, t + 1)
                a.activation(hn_tok[:, t, :].rearrange("p (b c) -> p b c", b=2), side[0:TOK, 0:2, :],
                             ACT.Copy).then_inc(hn_tok_ready, 1)
            a.nop().then_inc(y_stored, 16)

            def gather_hi(b, c):
                act.wait_ge(xt_read, b + 1)
                a.activation(xg[:, 2 * c:2 * c + 2, 0, :], side[:, c, 0:2 * S].rearrange("p (m s) -> p m s", m=2),
                             ACT.Copy).then_inc(xgh_ready, 1)

            def copy_half(out, a, bank):
                nc.scalar.activation(out, acc[:, a, bank, S:2 * S], ACT.Copy).then_inc(half_ready[a], 1)

            def moe_block(b, nxt, ahead):
                more, u0 = b * (U_FF // RING), ff_u[1]

                def upper(i):
                    act.wait_ge(fx_ready, b * FT + (i + 1))
                    a.activation(fg2[:, i, 0, :], fx[:, i % SLOT3, :], ACT.Copy).then_inc(fgh_ready, 1)

                for i in range(FT):
                    split_hi(u0 + 2 * i + 3, more)
                    arrived(u0 + 2 * i, more)
                    copy_half(gs[:, i % SLOT3, :], 0, i % 2)
                    if i:
                        upper(i - 1)
                    split_hi(u0 + 2 * i + 4, more)
                    arrived(u0 + 2 * i + 1, more)
                    copy_half(us[:, i % SLOT3, :], 1, i % 2)
                    act.wait_ge(acc_free[0], b * ACC_FF + (i + ff_acc[1] + 1))
                    a.activation(gx[:, i % SLOT3, :], gs[:, i % SLOT3, :], ACT.Silu).then_inc(gx_ready, 1)
                upper(FT - 1)
                for j in range(FT):
                    last = j == FT - 1
                    if not last and (ahead or j < FT - 3):
                        split_hi(u0 + 2 * FT + j + 3, more)
                    for m in moe_tiles_at(j):
                        arrived(u0 + 2 * FT + j, more)
                        copy_half(y_t[:, m, :], m % 2, m // 2 % 2)
                    if last and ahead:
                        split_hi(u0 + 2 * FT + j + 3, more)
                    if j in (2, 3, 4, 5) and nxt:
                        gather_hi(b + 1, j - 2)
                    if j in (7, FT - 1):
                        rows_back(b, 0 if j == 7 else 1)

            def rows_back(b, c):
                act.wait_ge(y_tr, 2 * b + c + 1)
                if c == 0:
                    act.wait_ge(y_stored, b * 16 + 16)
                a.activation(ytok[:, :, c * 512:(c + 1) * 512], side[0:SH, 2 * c:2 * c + 2, :],
                             ACT.Copy).then_inc(ytok_ready, 1)
                if c == 1:
                    act.wait_ge(ytok_ready, 2 * b + 2)
                    act.dma_start(yg_d[bass.ds(b * S, S), :].rearrange("(h p) c -> p h c", h=2),
                                  ytok[:, :, :]).then_inc(y_stored, 16)

            silu_table()
            for c in range(4):
                gather_hi(0, c)
            with act.Fori(0, EXPERTS - 1) as b:
                moe_block(b, True, True)
            moe_block(EXPERTS - 1, False, False)
            act.wait_ge(tab_ready2, 1)
            n_extra = act.value_load(tab[0:1, 0:1], min_val=0, max_val=EXTRA)
            with act.If(n_extra > 0):
                with act.Fori(0, n_extra) as i:
                    b = i + EXPERTS
                    for j in range(3):
                        split_hi(ff_u[1] + j, b * (U_FF // RING))
                    for c in range(4):
                        gather_hi(b, c)
                    moe_block(b, False, False)
            for t in range(TB):
                act.wait_ge(sum_ready, t + 1)
                a.activation(sqt[:, :], hs_tok[:, t, :], ACT.Square, accum_out=ssq[0:TOK, t:t + 1]).then_inc(sq2_ready, 1)
                act.wait_ge(sq2_ready, t + 1)
                a.activation(ssq[0:TOK, t:t + 1], ssq[0:TOK, t:t + 1], ACT.Sqrt, scale=1.0 / D, bias=EPS)\
                    .then_inc(rms2_ready, 1)

        @block.vector
        def _(dve):
            v = nc.vector
            chain = [0]

            def link(ins):
                chain[0] += 1
                ins.then_inc(dve_chain, 1)
                dve.wait_ge(dve_chain, chain[0])

            def tt(out, a, b, op):
                return v.tensor_tensor(out, a, b, op)

            def split_lo(u, more=0):
                if isinstance(u, int) and isinstance(more, int) and u + RING * more >= UNITS:
                    return
                s, n = use(u, more)
                dve.wait_ge(hi_ready[s], n + 1)
                tt(wl[s][:, :], raw[s][:, :], wh[s][:, :].bitcast(F32), ALU.subtract).then_inc(lo_ready[s], 1)

            def arrived(u, more=0):
                s, n = use(u, more)
                dve.wait_ge(unit_done[s], n + 1)

            def norm(i):
                name, layer = (("mix_norm", 0), ("ffn_norm", 0), ("mix_norm", 1), ("ffn_norm", 1))[i]
                dve.wait_ge(rms_ready, i + 1)
                link(v.reciprocal(rs[:, :], rs[:, :]))

                def lower(m):
                    dve.wait_ge(xh_ready, xh_at_norm(i) + m + 1)
                    tt(xl[:, m, :], hn[:, m, :], xh[:, m, :].bitcast(F32), ALU.subtract).then_inc(xl_ready, 1)

                for m in range(DK):
                    g = col(name, layer, m)
                    v.scalar_tensor_tensor(out=hn[:, m, :], in0=hs[:, m, :], scalar=g, in1=rs[:, :],
                                           op0=ALU.mult, op1=ALU.mult).then_inc(hn_ready, 1)
                    if m and i < 3:
                        lower(m - 1)
                if i < 3:
                    lower(DK - 1)

            def conv(l, m):
                n = l * MT + m
                w = lambda k: col("conv_w", l, 4 * k + m)
                if n == 0:
                    dve.wait_ge(c_ready, 1)
                dve.wait_ge(acc_free[0], mix_acc[l] + 2 + m + 1)
                link(v.tensor_scalar(xc[:, m, :], xpad[:, 0:T], w(0), col("conv_b", l, m), ALU.mult, ALU.add))
                for k in range(1, 4):
                    last = v.scalar_tensor_tensor(out=xc[:, m, :], in0=xpad[:, k:k + T], scalar=w(k),
                                                  in1=xc[:, m, :], op0=ALU.mult, op1=ALU.add)
                    if k < 3:
                        link(last)
                last.then_inc(xc_ready, 1)

            def lru_pair(l, q):
                n = l * 2 + q
                dve.wait_ge(lru_a, 2 * n + 2)
                dve.wait_ge(xc_ready, l * MT + 2 * q + 2)
                pair = slice(2 * q, 2 * q + 2)
                link(tt(ii[:, :, :], ii[:, :, :], xc[:, pair, :], ALU.mult))
                link(tt(xc[:, pair, :], ra[:, :, :], ra[:, :, :], ALU.mult))
                v.scalar_tensor_tensor(out=th[:, :, :].rearrange("p a b -> p (a b)"),
                                       in0=xc[:, pair, :].rearrange("p a b -> p (a b)"), scalar=1.0,
                                       in1=th[:, :, :].rearrange("p a b -> p (a b)"),
                                       op0=ALU.add, op1=ALU.mult).then_inc(lru_m, 1)

            def lru_scan(l, q):
                n = l * 2 + q
                dve.wait_ge(lru_r, n + 1)
                pair = slice(2 * q, 2 * q + 2)
                link(tt(ii[:, :, :], ii[:, :, :], th[:, :, :], ALU.mult))
                v.tensor_tensor_scan(th[:, 0, :], ra[:, 0, :], ii[:, 0, :], 0.0, ALU.mult, ALU.add)
                link(v.tensor_tensor_scan(th[:, 1, :], ra[:, 1, :], ii[:, 1, :], 0.0, ALU.mult, ALU.add))
                k = 4 + 2 * (2 * q + 1) + 1
                dve.wait_ge(acc_free[1], mix_acc[l] + k // 2 + 1)
                for i in range(2):
                    tt(gg[:, 2 * q + i, :], gg[:, 2 * q + i, :], th[:, i, :], ALU.mult).then_inc(yb_ready, 1)

            def lru_out(l, q):
                for t in (2 * q, 2 * q + 1):
                    dve.wait_ge(ybh_ready, l * MT + t + 1)
                    tt(ybl[:, t, :], gg[:, t, :], ybh[:, t, :].bitcast(F32), ALU.subtract).then_inc(ybl_ready, 1)

            def mixer(l):
                u0, a0 = mix_u[l], mix_acc[l]
                v.memset(cr[:, :, 0:1], 0.0)
                link(v.memset(sr[:, :, 0:1], 0.0))
                for k in range(U_IN):
                    split_lo(u0 + k + 2)
                    b, part = slot_of(k)
                    if b is None:
                        continue
                    n = l * NB + b
                    if part == 0:
                        dve.wait_ge(p1_done, n + 1)
                        for i in range(GB):
                            at = COLS["s5_d"][0] + l * GROUPS + b * GB + i
                            last = v.scalar_tensor_tensor(out=m3[:, i, :], in0=ident[:, :], scalar=cols[:, at:at + 1],
                                                          in1=side[:, 1, i * P:(i + 1) * P], op0=ALU.mult, op1=ALU.add)
                        last.then_inc(m_dve, 1)
                        dve.wait_ge(c_ready, n + 1)
                        if n:
                            dve.wait_ge(p3_done, n)
                        gs = slice(l * GROUPS + b * GB, l * GROUPS + (b + 1) * GB)
                        w4 = [P, GB, L, GC]
                        ab = lambda x: x[:, 1:L + 1, gs].rearrange("p j g -> p g j").unsqueeze(3).to_broadcast(w4)
                        cb = lambda x: x[:, :, :].unsqueeze(2).to_broadcast(w4)
                        q4 = lambda x: x[:, :, :].rearrange("p g (j h) -> p g j h", h=GC)
                        d4 = dt1[:, :].rearrange("p (g j h) -> p g j h", g=GB, h=GC)
                        tt(d4, ab(apr), cb(c1), ALU.mult)
                        link(tt(q4(m2), ab(api), cb(c2), ALU.mult))
                        link(tt(q4(m2), q4(m2), d4, ALU.add))
                        tt(d4, ab(apr), cb(c2), ALU.mult)
                        link(tt(q4(m2y), ab(api), cb(c1), ALU.mult))
                        tt(q4(m2y), d4, q4(m2y), ALU.subtract).then_inc(m2_ready, 1)
                        if b in (2, 4):
                            lru_pair(l, b // 2 - 1)
                    elif part == 1:
                        dve.wait_ge(p2_done, n + 1)
                        dve.wait_ge(tab_ready, n + 1)
                        w3 = lambda bank: side[:, bank, 0:GB * NC].rearrange("p (g c) -> p g c", g=GB)
                        tt(rot[:, :, :], w3(2), cosT[:, :, :], ALU.mult)
                        link(tt(rot2[:, :, :], w3(3), sinT[:, :, :], ALU.mult))
                        link(tt(rot[:, :, :], rot[:, :, :], rot2[:, :, :], ALU.add))
                        flat = lambda x: x[:, :, :].rearrange("p g c -> p (g c)")
                        link(v.tensor_tensor_scan(flat(turned), flat(decay), flat(rot), 0.0, ALU.mult, ALU.add))
                        tt(cr[:, :, 1:NC], turned[:, :, 0:NC - 1], cosT[:, :, 0:NC - 1], ALU.mult)
                        tt(sr[:, :, 1:NC], turned[:, :, 0:NC - 1], sinT[:, :, 0:NC - 1], ALU.mult).then_inc(rot_ready, 1)
                        if b in (2, 4):
                            lru_scan(l, b // 2 - 1)
                            lru_out(l, b // 2 - 1)
                    kind, m = KIND[k]
                    if kind == "x":
                        conv(l, m)
                for m in range(MT):
                    dve.wait_ge(y1h_ready, l * MT + m + 1)
                    tt(chunked(y1l[:, m, :]), perm(yt[:, m, :, :]), chunked(y1h[:, m, :].bitcast(F32)),
                       ALU.subtract).then_inc(y1l_ready, 1)
                a1 = a0 + U_IN // 2
                for g in range(U_GLU):
                    split_lo(u0 + U_IN + g + 2)
                    for i in range(2):
                        m = 2 * g + i
                        dve.wait_ge(acc_free[i], a1 + g + 1)
                        if m >= 2:
                            dve.wait_ge(y2l_ready, l * MT + m - 1)
                        tt(chunked(ft[:, i, :]), chunked(gt[:, i, :]), perm(yt[:, m, :, :]), ALU.mult).then_inc(y2_ready, 1)
                    for i in range(2):
                        m = 2 * g + i
                        dve.wait_ge(y2h_ready, l * MT + m + 1)
                        tt(y2l[:, m, :], ft[:, i, :], y2h[:, m, :].bitcast(F32), ALU.subtract).then_inc(y2l_ready, 1)
                for m in range(DK):
                    u = u0 + U_IN + U_GLU + m
                    split_lo(u + 2)
                    arrived(u)
                    if m == 0:
                        dve.wait_ge(acc_free[0], a0 + 14)
                        dve.wait_ge(acc_free[1], a0 + 14)
                        dve.wait_ge(y2l_ready, (l + 1) * MT)
                    else:
                        dve.wait_ge(xl_ready, xh_at_mix(l) + m)
                    tt(halves(ft[:, 0, :]), acc[:, 0, :, 0:TH], halves(gates[:, m, :]), ALU.mult).then_inc(acc_free[0], 1)
                    tt(halves(ft[:, 1, :]), acc[:, 1, :, 0:TH], halves(gates[:, DK + m, :]), ALU.mult).then_inc(acc_free[1], 1)
                    dve.wait_ge(acc_free[0], a0 + 16 + m + 1)
                    dve.wait_ge(acc_free[1], a0 + 16 + m + 1)
                    tt(ft[:, 0, :], ft[:, 0, :], ft[:, 1, :], ALU.add).then_inc(mg_ready, 1)
                    dve.wait_ge(xh_ready, xh_at_mix(l) + m + 1)
                    tt(xl[:, m, :], ft[:, 0, :], xh[:, m, :].bitcast(F32), ALU.subtract).then_inc(xl_ready, 1)
                for m in range(DK):
                    u = u0 + U_MIX - DK + m
                    split_lo(u + 2)
                    arrived(u)
                    dve.wait_ge(hs_back, 16 * DK * (l + 1))
                    v.tensor_tensor(halves(hs[:, m, :]), halves(hs[:, m, :]), acc[:, m % 2, :, 0:TH],
                                    ALU.add).then_inc(hs_ready, 1)
                    dve.wait_ge(hs_ready, hs_at_norm[2 * l + 1] - DK + m + 1)
                    v.nop().then_inc(acc_free[m % 2], 1)

            def expert(l, u0, e, e_all):
                with dve.Fori(0, 2 * FT // STEP) as it:
                    more = e * (U_FF // RING) + it * (STEP // RING)
                    for i in range(STEP // 2):
                        m = it * (STEP // 2) + i
                        u = u0 + 2 * i
                        split_lo(u + 2, more)
                        split_lo(u + 3, more)
                        arrived(u + 1, more)
                        uses = e * ACC_FF + it * (STEP // 2) + (i + ff_acc[l] + 1)
                        dve.wait_ge(acc_free[0], uses)
                        tt(halves(ft[:, 0, :]), halves(gt[:, 0, :]), acc[:, 1, :, 0:TH], ALU.mult).then_inc(acc_free[1], 1)
                        dve.wait_ge(acc_free[1], uses)
                        v.nop().then_inc(f_ready, 1)
                        dve.wait_ge(fh_ready, e_all * FT + m + 1)
                        tt(fl[:, m, :], ft[:, 0, :], fh[:, m, :].bitcast(F32), ALU.subtract).then_inc(fl_ready, 1)
                        dve.wait_ge(fl_ready, e_all * FT + m + 1)

            def down(l, u0, e, e_all, last):
                more = e * (U_FF // RING)
                for j in range(FT):
                    u = u0 + 2 * FT + j
                    if not (last and j >= FT - 2):
                        split_lo(u + 2, more)
                    if j % 3 == 0:
                        continue
                    m = 2 * (j // 3) + (j % 3 - 1)
                    arrived(u, more)
                    seen = hs_at_norm[2 * l + 1] + e * DK
                    if m == 0:
                        dve.wait_ge(hs_ready, seen)
                    v.tensor_tensor(halves(hs[:, m, :]), halves(hs[:, m, :]), acc[:, m % 2, :, 0:TH],
                                    ALU.add).then_inc(hs_ready, 1)
                    dve.wait_ge(hs_ready, seen + m + 1)
                    v.nop().then_inc(acc_free[m % 2], 1)

            v.memset(sgn[0:GS, 0:1], -1.0)
            v.memset(sgn[GS:P, 0:1], 1.0)
            v.memset(sgn[0:GS, 1:2], 1.0)
            link(v.memset(sgn[GS:P, 1:2], -1.0))
            dve.wait_ge(small_landed, 16)
            dve.wait_ge(prep_act, 1)
            ang, kk, red, red2 = (pp[n][:, :] for n in ("ang", "k", "red", "red2"))
            ROUND = 12582912.0
            C1, C2, C3 = 6.28125, 0.0019350051879882812, 3.019916e-07
            link(tt(ang, pp["li"][:, :], pp["dt"][:, :], ALU.mult))
            link(v.tensor_scalar(kk, ang, 0.15915494309189535, ROUND, ALU.mult, ALU.add))
            link(v.tensor_scalar(kk, kk, ROUND, 0.0, ALU.subtract, ALU.add))
            for c in (C1, C2, C3):
                link(v.scalar_tensor_tensor(out=ang, in0=kk, scalar=-c, in1=ang, op0=ALU.mult, op1=ALU.add))
            link(v.tensor_scalar(red, ang, 3.1415925, -3.1415925, ALU.min, ALU.max))
            link(v.tensor_scalar(kk, ang, 1.5707963267948966, -6.283185307179586, ALU.is_gt, ALU.mult))
            link(v.scalar_tensor_tensor(out=red2, in0=ang, scalar=1.5707963267948966, in1=kk, op0=ALU.add, op1=ALU.add))
            link(v.tensor_scalar(red2, red2, 3.1415925, -3.1415925, ALU.min, ALU.max))
            tt(pp["num"][:, :], pp["lr"][:, :], pp["dt"][:, :], ALU.mult).then_inc(prep_dve, 1)
            link(tt(pp["den"][:, :], pp["lr"][:, :], pp["lr"][:, :], ALU.mult))
            link(tt(pp["t3"][:, :], pp["li"][:, :], pp["li"][:, :], ALU.mult))
            link(tt(pp["den"][:, :], pp["den"][:, :], pp["t3"][:, :], ALU.add))
            v.reciprocal(pp["rden"][:, :], pp["den"][:, :]).then_inc(prep_dve, 1)
            at, n = COLS["lam"]
            lam = cols[:, at:at + LAYERS * n]
            s0, s1, s2, s3 = (x[:, :] for x in spt)
            link(v.tensor_scalar(s2, lam, -1.0, 0.0, ALU.mult, ALU.add))
            tt(s0, lam, s2, ALU.max).then_inc(prep_dve, 1)
            link(v.tensor_scalar(s3, s2, 0.0, 0.0, ALU.max, ALU.add))
            dve.wait_ge(prep_act, 5)
            link(v.tensor_scalar(s0, s1, 2.0, 0.0, ALU.add, ALU.add))
            link(v.reciprocal(s0, s0))
            link(tt(s1, s1, s0, ALU.mult))
            link(tt(s0, s1, s1, ALU.mult))
            link(v.tensor_scalar(s2, s0, 2.0 / 17, 2.0 / 15, ALU.mult, ALU.add))
            for d in (13, 11, 9, 7, 5, 3, 1):
                link(tt(s2, s2, s0, ALU.mult))
                link(v.tensor_scalar(s2, s2, 1.0, 2.0 / d, ALU.mult, ALU.add))
            link(tt(s2, s2, s1, ALU.mult))
            link(tt(s2, s2, s3, ALU.add))
            link(v.tensor_scalar(sp8[:, :], s2, LRU_C, 0.0, ALU.mult, ALU.add))
            v.tensor_scalar(sp8n[:, :], s2, -LRU_C, 0.0, ALU.mult, ALU.add).then_inc(prep_dve, 1)
            split_lo(0)
            split_lo(1)
            norm(0)
            mixer(0)
            norm(1)
            for l in range(LAYERS):
                if l:
                    norm(2)
                    mixer(1)
                    split_lo(ff_u[1] + 2)
                    norm(3)
                    k = slice(0, TOK)
                    dve.wait_ge(lg_done, 1)
                    dve.wait_ge(const_ready, 4)
                    w3, w4 = [TOK, TB, EXPERTS], [TOK, TB, EXPERTS, EXPERTS]
                    link(tt(lg[k, :, :], acc[k, 0, 0, 0:TB * EXPERTS].rearrange("p (t e) -> p t e", t=TB),
                            rbs[k, :].unsqueeze(1).to_broadcast(w3), ALU.add))
                    mine = lg[k, :, :].unsqueeze(3).to_broadcast(w4)
                    other = lg[k, :, :].unsqueeze(2).to_broadcast(w4)
                    tt(cmp1[k], other, mine, ALU.is_gt)
                    link(tt(cmp2[k], other, mine, ALU.is_equal))
                    link(tt(cmp2[k], cmp2[k], tri[k].unsqueeze(1).to_broadcast(w4), ALU.mult))
                    link(tt(cmp1[k], cmp1[k], cmp2[k], ALU.add))
                    link(v.reduce_sum(rank[k], cmp1[k], AX_X))
                    v.tensor_scalar(sel1[k], rank[k], 0.0, 0.0, ALU.is_equal, ALU.add)
                    link(v.tensor_scalar(sel2[k], rank[k], 1.0, 0.0, ALU.is_equal, ALU.add))
                    tt(mask[k], sel1[k], sel2[k], ALU.add).then_inc(mask_ready, 1)
                    v.reduce_max(v1[k], lg[k], AX_X)
                    link(v.tensor_scalar(gtmp[k], rank[k], 0.0, -1e30, ALU.is_equal, ALU.mult))
                    link(tt(gtmp[k], gtmp[k], lg[k], ALU.add))
                    link(v.reduce_max(v2[k], gtmp[k], AX_X))
                    tt(v2[k], v2[k], v1[k], ALU.subtract).then_inc(d_ready, 1)
                    dve.wait_ge(ex_ready, 1)
                    link(v.tensor_scalar(g1[k], ex[k], 1.0, 0.0, ALU.add, ALU.add))
                    link(v.reciprocal(g1[k], g1[k]))
                    link(tt(g2[k], g1[k], ex[k], ALU.mult))
                    continue
                with dve.Fori(0, ff_n[l] - 1) as e:
                    expert(l, ff_u[l], e, e + ff_e0[l])
                    down(l, ff_u[l], e, e + ff_e0[l], False)
                e = ff_n[l] - 1
                expert(l, ff_u[l], e, e + ff_e0[l])
                down(l, ff_u[l], e, e + ff_e0[l], False)

            for t in range(TB):
                dve.wait_ge(tok_done, t + 1)
                v.tensor_copy(hs_tok[:, t, :].rearrange("p (b c) -> p b c", b=2), side[0:TOK, 2:4, :])\
                    .then_inc(hs_tok_ready, 1)
            w8, wi = [TOK, TB, EXPERTS], [TOK, EXTRA, EXPERTS]
            v.memset(oneE[k], 1.0)
            v.memset(oneI[k], 1.0)
            link(v.memset(off[k, 0, :], 0.0))
            v.tensor_tensor_scan(ev[k], oneE[k], oneE[k], -1.0, ALU.mult, ALU.add)
            link(v.tensor_tensor_scan(iv[k], oneI[k], oneI[k], -1.0, ALU.mult, ALU.add))
            dve.wait_ge(pos_done, 1)
            counts = acc[k, 1, 1, 0:TB * EXPERTS].rearrange("p (t e) -> p t e", t=TB)
            for t in range(TB):
                link(tt(off[k, t + 1, :], off[k, t, :], counts[:, t, :], ALU.add))
            before = acc[k, 1, 0, 0:TB * EXPERTS].rearrange("p (t e) -> p t e", t=TB)
            link(tt(pos[k], before, off[k, 0:TB, :], ALU.add))

            def steps(out, tmp, x):
                link(v.tensor_scalar(out, x, float(S), 0.0, ALU.is_ge, ALU.add))
                for q in range(2, QMAX + 1):
                    link(v.tensor_scalar(tmp, x, float(q * S), 0.0, ALU.is_ge, ALU.add))
                    link(tt(out, out, tmp, ALU.add))

            link(v.tensor_scalar(xtmp[k], off[k, TB, :], 1.0, 0.0, ALU.subtract, ALU.add))
            steps(extra[k], ebase[k], xtmp[k])
            link(v.tensor_tensor_scan(incl[k], oneE[k], extra[k], 0.0, ALU.mult, ALU.add))
            link(tt(ebase[k], incl[k], extra[k], ALU.subtract))
            steps(qq[k], slot[k], pos[k])
            link(v.tensor_scalar(big[k], pos[k], float(S), 0.0, ALU.is_ge, ALU.add))
            link(tt(xtmp[k], ebase[k], ev[k], ALU.subtract))
            link(v.tensor_scalar(xtmp[k], xtmp[k], float(EXPERTS - 1), 0.0, ALU.add, ALU.add))
            link(tt(slot[k], qq[k], xtmp[k].unsqueeze(1).to_broadcast(w8), ALU.add))
            link(tt(slot[k], slot[k], big[k], ALU.mult))
            link(tt(slot[k], slot[k], ev[k].unsqueeze(1).to_broadcast(w8), ALU.add))
            link(tt(slot[k], slot[k], qq[k], ALU.subtract))
            link(v.scalar_tensor_tensor(out=slot[k].rearrange("p t e -> p (t e)"),
                                        in0=slot[k].rearrange("p t e -> p (t e)"), scalar=float(S),
                                        in1=pos[k].rearrange("p t e -> p (t e)"), op0=ALU.mult, op1=ALU.add))
            tt(qq[k], slot[k], sel1[k], ALU.mult)
            link(tt(big[k], slot[k], sel2[k], ALU.mult))
            v.reduce_sum(sf[k, 0, :], qq[k], AX_X)
            link(v.reduce_sum(sf[k, 1, :], big[k], AX_X))
            v.tensor_copy(idx[k], sf[k]).then_inc(slot_ready, 1)
            ib = iv[k].unsqueeze(2).to_broadcast(wi)
            tt(in1[k], ib, ebase[k].unsqueeze(1).to_broadcast(wi), ALU.is_ge)
            link(tt(in2[k], ib, incl[k].unsqueeze(1).to_broadcast(wi), ALU.is_lt))
            link(tt(in1[k], in1[k], in2[k], ALU.mult))
            link(tt(in1[k], in1[k], ev[k].unsqueeze(1).to_broadcast(wi), ALU.mult))
            v.tensor_copy(tabf[k, 0:1], incl[k, EXPERTS - 1:EXPERTS])
            link(v.reduce_sum(tabf[k, 1:EXTRA + 1], in1[k], AX_X))
            wider = tabf[k, EXTRA + 1:EXTRA + 1 + EXPERTS]
            link(v.tensor_scalar(wider, off[k, TB, :], float(WIDTHS[0]), 0.0, ALU.is_gt, ALU.add))
            for n in WIDTHS[1:-1]:
                link(v.tensor_scalar(xtmp[k], off[k, TB, :], float(n), 0.0, ALU.is_gt, ALU.add))
                link(tt(wider, wider, xtmp[k], ALU.add))
            v.tensor_copy(tab[k], tabf[k]).then_inc(tab_ready2, 1)

            def gather_lo(b, c):
                dve.wait_ge(xgh_ready, b * 4 + c + 1)
                tt(xg[:, 2 * c:2 * c + 2, 1, :], side[:, c, 0:2 * S].rearrange("p (m s) -> p m s", m=2),
                   xg[:, 2 * c:2 * c + 2, 0, :].bitcast(F32), ALU.subtract).then_inc(xgl_ready, 1)

            def add_halves(out, a, bank, b, n):
                dve.wait_ge(half_ready[a], b * ACC_FF + (n + 1))
                tt(out, out, acc[:, a, bank, 0:S], ALU.add).then_inc(acc_free[a], 1)

            def moe_block(b, nxt, ahead):
                more, u0 = b * (U_FF // RING), ff_u[1]
                for m in range(FT):
                    x = m % SLOT3
                    split_lo(u0 + 2 * m + 3, more)
                    add_halves(gs[:, x, :], 0, m % 2, b, m)
                    split_lo(u0 + 2 * m + 4, more)
                    add_halves(us[:, x, :], 1, m % 2, b, m)
                    dve.wait_ge(acc_free[1], b * ACC_FF + (m + ff_acc[1] + 1))
                    dve.wait_ge(gx_ready, b * FT + (m + 1))
                    if m >= SLOT3:
                        dve.wait_ge(fgl_ready, b * FT + (m - SLOT3 + 1))
                    tt(fx[:, x, :], gx[:, x, :], us[:, x, :], ALU.mult).then_inc(fx_ready, 1)
                for j in range(FT):
                    last = j == FT - 1
                    if not last and (ahead or j < FT - 3):
                        split_lo(u0 + 2 * FT + j + 3, more)
                    for m in moe_tiles_at(j):
                        add_halves(y_t[:, m, :], m % 2, m // 2 % 2, b, FT + m // 2)
                    if last and ahead:
                        split_lo(u0 + 2 * FT + j + 3, more)
                    if j in (2, 3, 4, 5) and nxt:
                        gather_lo(b + 1, j - 2)

            for c in range(4):
                gather_lo(0, c)
            dve.wait_ge(acc_free[1], ff_acc[1])
            v.memset(acc[:, :, :, :], 0.0).then_inc(acc_set, 1)
            with dve.Fori(0, EXPERTS - 1) as b:
                moe_block(b, True, True)
            moe_block(EXPERTS - 1, False, False)
            dve.wait_ge(tab_ready2, 1)
            n_extra = dve.value_load(tab[0:1, 0:1], min_val=0, max_val=EXTRA)
            with dve.If(n_extra > 0):
                with dve.Fori(0, n_extra) as i:
                    b = i + EXPERTS
                    for j in range(3):
                        split_lo(ff_u[1] + j, b * (U_FF // RING))
                    for c in range(4):
                        gather_lo(b, c)
                    moe_block(b, False, False)
            dve.wait_ge(gm_landed, 16)

            def normed(t):
                dve.wait_ge(rms2_ready, t + 1)
                link(v.reciprocal(ssq[k, t:t + 1], ssq[k, t:t + 1]))
                if t >= 2:
                    dve.wait_ge(out_done[t % 2], 16 * (t // 2))
                v.scalar_tensor_tensor(out=ot[:, t % 2, :], in0=hs_tok[:, t, :], scalar=ssq[k, t:t + 1],
                                       in1=gmb[:, :], op0=ALU.mult, op1=ALU.mult).then_inc(ot_ready, 1)

            for t in range(TB):
                dve.wait_ge(ya_in[t % 2], 32 * (t // 2 + 1))
                link(v.scalar_tensor_tensor(out=hs_tok[:, t, :], in0=ya[:, t % 2, :], scalar=g1[k, t:t + 1],
                                            in1=hs_tok[:, t, :], op0=ALU.mult, op1=ALU.add))
                v.scalar_tensor_tensor(out=hs_tok[:, t, :], in0=yb[:, t % 2, :], scalar=g2[k, t:t + 1],
                                       in1=hs_tok[:, t, :], op0=ALU.mult, op1=ALU.add).then_inc(sum_ready, 1)
                if t:
                    normed(t - 1)
            normed(TB - 1)

        @block.tensor
        def _(pe):
            mm = nc.tensor.matmul

            def free(s, n):
                if not isinstance(n, int) or n > 0:
                    pe.wait_ge(acc_free[s], n)

            def unit(u, jobs, more=0):
                s, n = use(u, more)
                pe.wait_ge(lo_ready[s], n + 1)
                for k, a, hi, lo, first, last in jobs:
                    w_hi, w_lo = (x[s][:, k * P:(k + 1) * P] for x in (wh, wl))
                    parts = [(w_hi, hi), (w_hi, lo), (w_lo, hi)]
                    for i, (w, x) in enumerate(parts):
                        for b in range(2):
                            ins = mm(acc[:, a, b, 0:TH], w, x[:, b * TH:(b + 1) * TH],
                                     start=first and i == 0, stop=last and i == 2)
                ins.then_inc(unit_done[s], 1)

            def norm(i):
                if i == 0:
                    pe.wait_ge(const_ready, 1)
                for m in range(DK):
                    pe.wait_ge(sq_ready, i * DK + m + 1)
                    for b in range(2):
                        ins = mm(side[:, b, 0:TH], ones[:, :], hn[:, m, b * TH:(b + 1) * TH],
                                 start=m == 0, stop=m == DK - 1)
                ins.then_inc(ss_ready, 1)

            def full(xs, m):
                return [(k, xs[0][:, k, :], xs[1][:, k, :]) for k in range(DK)]

            def gate_mm(l, q):
                t, r = q // 2, q % 2
                pe.wait_ge(xc_ready, l * MT + t + 1)
                pe.wait_ge(wg_landed, 32 * (l + 1))
                if l * 8 + q:
                    pe.wait_ge(ri_ready, l * 8 + q)
                pe.wait_ge(rot_ready, l * NB + q // 2 + 1)
                for hd in range(2):
                    rows = slice(hd * 64, hd * 64 + 64)
                    for b in range(2):
                        ins = mm(side[rows, 2 + b, 0:TH], gw[rows, r, t, :], xc[rows, t, b * TH:(b + 1) * TH],
                                 start=True, stop=True)
                ins.then_inc(gm_done, 1)

            def mixer(l):
                u0, a0 = mix_u[l], mix_acc[l]
                for k in range(U_IN):
                    if k == 0:
                        pe.wait_ge(xl_ready, xl_at_norm(2 * l) + DK)
                    free(k % 2, a0 + k // 2)
                    unit(u0 + k, [(j, k % 2, xh[:, j, :], xl[:, j, :], j == 0, j == DK - 1) for j in range(DK)])
                    b, part = slot_of(k)
                    if b is None:
                        continue
                    n = l * NB + b
                    if part == 0:
                        pe.wait_ge(const_ready, 2)
                        pe.wait_ge(m1t_ready, n + 1)
                        pe.wait_ge(c_ready, n + 1)
                        if n:
                            pe.wait_ge(ys_ready, n)
                            pe.wait_ge(m_dve, n)
                        for i in range(GB):
                            nc.tensor.transpose(side[:, 0, i * P:(i + 1) * P], m1t[:, i, 0:P], ident[:, :])
                        for i in range(GB):
                            for j in range(L):
                                at = (L - 1 - j) * GC
                                ins = mm(side[:, 1, i * P + j * GC:i * P + (j + 1) * GC], m1t[:, i, at:at + P],
                                         c1[:, i, :], start=True, stop=True)
                        ins.then_inc(p1_done, 1)
                        if 1 <= b <= MT:
                            gate_mm(l, 2 * b - 1)
                    elif part == 1:
                        pe.wait_ge(m_act, n + 1)
                        pe.wait_ge(m_dve, n + 1)
                        pe.wait_ge(u_in, 16 * L * (l + 1))
                        if b:
                            pe.wait_ge(ri_ready, l * 8 + min(2 * b, 8))
                        for i in range(GB):
                            c = slice(i * NC, (i + 1) * NC)
                            mm(side[:, 2, c], m1[:, i, :], uu[:, b * GB + i, :], start=True, stop=True)
                            ins = mm(side[:, 3, c], m1y[:, i, :], uu[:, b * GB + i, :], start=True, stop=True)
                        ins.then_inc(p2_done, 1)
                    else:
                        pe.wait_ge(rot_ready, n + 1)
                        pe.wait_ge(m2_ready, n + 1)
                        for i in range(GB):
                            c = slice(i * NC, (i + 1) * NC)
                            mm(side[:, 0, c], m3[:, i, :], uu[:, b * GB + i, :], start=True, stop=False)
                            mm(side[:, 0, c], m2[:, i, :], cr[:, i, :], start=False, stop=False)
                            ins = mm(side[:, 0, c], m2y[:, i, :], sr[:, i, :], start=False, stop=True)
                        ins.then_inc(p3_done, 1)
                        if b < MT:
                            gate_mm(l, 2 * b)
                a1 = a0 + U_IN // 2
                pe.wait_ge(y1l_ready, (l + 1) * MT)
                for g in range(U_GLU):
                    free(0, a1 + g)
                    free(1, a1 + g)
                    unit(u0 + U_IN + g, [(4 * i + k, i, y1h[:, k, :], y1l[:, k, :], k == 0, k == MT - 1)
                                         for i in range(2) for k in range(MT)])
                pe.wait_ge(y2l_ready, (l + 1) * MT)
                pe.wait_ge(ybl_ready, (l + 1) * MT)
                for m in range(DK):
                    free(0, a0 + 16 + m)
                    free(1, a0 + 16 + m)
                    unit(u0 + U_IN + U_GLU + m,
                         [(k, 0, y2h[:, k, :], y2l[:, k, :], k == 0, k == MT - 1) for k in range(MT)]
                         + [(MT + k, 1, ybh[:, k, :], ybl[:, k, :], k == 0, k == MT - 1) for k in range(MT)])
                pe.wait_ge(xl_ready, xl_mix_end(l))
                for m in range(DK):
                    free(m % 2, a0 + 24 + m // 2)
                    unit(u0 + U_MIX - DK + m,
                         [(k, m % 2, xh[:, k, :], xl[:, k, :], k == 0, k == DK - 1) for k in range(DK)])

            def expert(l, u0, e, e_all):
                with pe.Fori(0, 2 * FT // STEP) as it:
                    more = e * (U_FF // RING) + it * (STEP // RING)
                    for i in range(STEP):
                        free(i % 2, e * ACC_FF + it * (STEP // 2) + (i // 2 + ff_acc[l]))
                        unit(u0 + i, [(k, i % 2, xh[:, k, :], xl[:, k, :], k == 0, k == DK - 1) for k in range(DK)], more)

            def down(l, u0, e, e_all):
                more = e * (U_FF // RING)
                for q in range(FT // 3):
                    tiles = [(2 * q + i, k) for i in range(2) for k in range(FT)]
                    for j in range(3):
                        jobs = []
                        for p, (m, k) in enumerate(tiles[8 * j:8 * j + 8]):
                            jobs.append((p, m % 2, fh[:, k, :], fl[:, k, :], k == 0, k == FT - 1))
                        pe.wait_ge(fl_ready, e_all * FT + (8 if q == 0 and j == 0 else FT))
                        for m, k in tiles[8 * j:8 * j + 8]:
                            if k == 0:
                                free(m % 2, e * ACC_FF + (ff_acc[l] + FT + q))
                        unit(u0 + 2 * FT + 3 * q + j, jobs, more)

            norm(0)
            mixer(0)
            norm(1)
            for l in range(LAYERS):
                if l:
                    norm(2)
                    mixer(1)
                    norm(3)
                    pe.wait_ge(hn_ready, 4 * DK)
                    pe.wait_ge(prep_pool, 16 * 5)
                    for t in range(TB):
                        for k in range(DK):
                            ins = mm(acc[0:TOK, 0, 0, t * EXPERTS:(t + 1) * EXPERTS], hn[:, k, t * TOK:(t + 1) * TOK],
                                     rws[:, k, :], start=k == 0, stop=k == DK - 1)
                    ins.then_inc(lg_done, 1)
                    for t in range(TB):
                        if t:
                            pe.wait_ge(hn_tok_ready, t)
                            pe.wait_ge(hs_tok_ready, t)
                        if t == 1:
                            pe.wait_ge(mask_ready, 1)
                            sel = mask[0:TOK, :, :].rearrange("p t e -> p (t e)")
                            mm(acc[0:TOK, 1, 0, 0:TB * EXPERTS], tris[0:TOK, :], sel, start=True, stop=True)
                            mm(acc[0:TOK, 1, 1, 0:TB * EXPERTS], ones[0:TOK, 0:TOK], sel, start=True, stop=True)\
                                .then_inc(pos_done, 1)
                        for src, bank in ((hn, 0), (hs, 2)):
                            for m in range(DK):
                                ins = nc.tensor.transpose(side[0:TOK, bank + m // 4, m % 4 * P:(m % 4 + 1) * P],
                                                          src[:, m, t * TOK:(t + 1) * TOK], ident[:, :])
                        ins.then_inc(tok_done, 1)
                    continue
                pe.wait_ge(xl_ready, xl_at_norm(2 * l + 1) + DK)
                with pe.Fori(0, ff_n[l] - 1) as e:
                    expert(l, ff_u[l], e, e + ff_e0[l])
                    down(l, ff_u[l], e, e + ff_e0[l])
                e = ff_n[l] - 1
                expert(l, ff_u[l], e, e + ff_e0[l])
                down(l, ff_u[l], e, e + ff_e0[l])

            def slot_unit(u, jobs, more, width):
                s, n = use(u, more)
                pe.wait_ge(lo_ready[s], n + 1)
                for k, a, bank, x, first, last in jobs:
                    w_hi, w_lo = (w[s][:, k * P:(k + 1) * P] for w in (wh, wl))
                    halves2 = acc[:, a, bank, 0:2 * S].rearrange("p (h s) -> p h s", h=2)
                    mm(halves2[:, :, 0:width], w_hi, x[:, :, 0:width], start=first, stop=False)
                    ins = mm(halves2[:, 0, 0:width], w_lo, x[:, 0, 0:width], start=False, stop=last)
                ins.then_inc(unit_done[s], 1)

            def turn_rows(b):
                pe.wait_ge(xt_landed, b * 16 + 16)
                for m in range(DK):
                    for h in range(2):
                        at = m % 2 * S + h * SH
                        ins = nc.tensor.transpose(side[:, m // 2, at:at + SH], xt[:, h, m * P:(m + 1) * P],
                                                  ident[0:SH, 0:SH])
                ins.then_inc(xt_read, 1)

            def moe_block(b, nxt, n=S):
                more, u0 = b * (U_FF // RING), ff_u[1]

                def free(a, n):
                    pe.wait_ge(acc_free[a], b * ACC_FF + (ff_acc[1] + n - 1))

                with pe.Fori(0, FT // BODY) as it:
                    inner = it * (2 * BODY // RING)
                    for i in range(BODY):
                        if i == 0:
                            pe.wait_ge(xgl_ready, b * 4 + 4)
                        for a in range(2):
                            pe.wait_ge(acc_free[a], b * ACC_FF + it * BODY + (i + ff_acc[1] - 1))
                            slot_unit(u0 + 2 * i + a, [(k, a, i % 2, xg[:, k, :, :], k == 0, k == DK - 1)
                                                       for k in range(DK)], more + inner, n)
                for q in range(FT // 3):
                    tiles = [(m, k) for m, k in moe_down_order() if m // 2 == q]
                    for j in range(3):
                        pe.wait_ge(fgl_ready, b * FT + (8 if q == 0 and j < 2 else FT))
                        here = tiles[8 * j:8 * j + 8]
                        for m, k in here:
                            if k == 0:
                                free(m % 2, FT + q)
                        slot_unit(u0 + 2 * FT + 3 * q + j,
                                  [(p, m % 2, m // 2 % 2, fg2[:, k, :, :], k == 0, k == FT - 1)
                                   for p, (m, k) in enumerate(here)], more, n)
                        if q == 0 and j == 1 and nxt:
                            turn_rows(b + 1)
                        if 3 * q + j in (7, 10, FT - 1):
                            first, end = {7: (0, 4), 10: (4, 6), FT - 1: (6, 8)}[3 * q + j]
                            pe.wait_ge(xgl_ready, b * 4 + (8 if nxt else 4))
                            for i in range(2):
                                pe.wait_ge(acc_free[i], b * ACC_FF + (ff_acc[1] + FT + end // 2))
                            for h in range(2):
                                for m in range(first, end):
                                    ins = nc.tensor.transpose(side[0:SH, 2 * (m // 4) + h, m % 4 * P:(m % 4 + 1) * P],
                                                              y_t[:, m, h * SH:(h + 1) * SH], ident[:, :])
                            if end != 6:
                                ins.then_inc(y_tr, 1)

            turn_rows_first = lambda: (pe.wait_ge(hn_tok_ready, TB), pe.wait_ge(hs_tok_ready, TB), turn_rows(0))
            turn_rows_first()
            pe.wait_ge(tab_ready2, 1)
            pe.wait_ge(acc_set, 1)

            def by_width(b, nxt):
                wider = pe.value_load(tab[0:1, bass.ds(b + (EXTRA + 1), 1)], min_val=0, max_val=len(WIDTHS) - 1)
                for i, n in enumerate(WIDTHS):
                    with pe.If(wider == i):
                        moe_block(b, nxt, n)

            with pe.Fori(0, EXPERTS - 1) as b:
                by_width(b, True)
            by_width(EXPERTS - 1, False)
            n_extra = pe.value_load(tab[0:1, 0:1], min_val=0, max_val=EXTRA)
            with pe.If(n_extra > 0):
                with pe.Fori(0, n_extra) as i:
                    b = i + EXPERTS
                    pe.wait_ge(ytok_ready, b * 2)
                    turn_rows(b)
                    moe_block(b, False)


LRU_WB = 64


def xh_at_norm(i):
    return DK * (0, 2, 3)[i]


def xl_at_norm(i):
    return xh_at_norm(i)


def xh_at_mix(l):
    return DK * (1, 4)[l]


def xl_mix_end(l):
    return xh_at_mix(l) + DK


def moe_down_order():
    order = [(m, k) for m in range(2) for k in range(8)] + [(m, k) for m in range(2) for k in range(8, FT)]
    return order + [(m, k) for m in range(2, DK) for k in range(FT)]


def moe_tiles_at(j):
    done = moe_down_order()[8 * j:8 * j + 8]
    return [m for m, k in done if k == FT - 1]


def layout(inputs):
    import numpy as np

    a = {k: np.asarray(v) for k, v in inputs.items()}
    arrays = {}
    x = np.concatenate([a["meta_tokens"], a["x"][0]], axis=0)
    tiles = lambda v: np.moveaxis(v.reshape(-1, P, *v.shape[1:]), 0, 1)
    arrays["xT"] = tiles(x.T)

    W = np.empty((UNITS, P, UNIT), np.float32)
    at = [0]

    def put(w):
        n = w.shape[0] // 8
        W[at[0]:at[0] + n] = np.moveaxis(w.reshape(n, 8, P, P), 1, 2).reshape(n, P, UNIT)
        at[0] += n

    def cut(w):
        k, m = w.shape
        return w.reshape(k // P, P, m // P, P).transpose(2, 0, 1, 3)

    def ffn(gate, up, down, order=None):
        g, u = cut(gate), cut(up)
        put(np.stack([g, u], axis=1).reshape(-1, P, P))
        d = cut(down)
        put(np.stack([d[m, k] for m, k in order]) if order else d.reshape(-1, P, P))

    for l in range(LAYERS):
        w = cut(a["w_in"][l])
        order = list(range(MT))
        for m in range(MT):
            order += [MT + m, 2 * MT + m]
        order += list(range(3 * MT, U_IN))
        put(w[order].reshape(-1, P, P))
        put(cut(a["s5_w_glu"][l]).reshape(-1, P, P))
        put(np.stack([cut(a["s5_w_proj"][l]), cut(a["lru_w_proj"][l])], axis=1).reshape(-1, P, P))
        put(cut(a["w_out"][l]).reshape(-1, P, P))
        if l == 0:
            for h in range(2):
                c = slice(h * FF, (h + 1) * FF)
                ffn(a["dense_w_gate"][0][:, c], a["dense_w_up"][0][:, c], a["dense_w_down"][0][c])
        else:
            for e in range(EXPERTS):
                ffn(a["moe_w_gate"][0, e], a["moe_w_up"][0, e], a["moe_w_down"][0, e], moe_down_order())
    assert at[0] == UNITS
    arrays["W"] = W

    cols = np.empty((P, NCOL), np.float32)
    for name, key in (("mix_norm", "mix_norm"), ("ffn_norm", "ffn_norm"), ("merge_bias", "merge_bias"),
                      ("conv_w", "lru_conv_w"), ("conv_b", "lru_conv_b"), ("b_r", "lru_b_rgate"),
                      ("b_i", "lru_b_igate"), ("lam", "lru_lambda"), ("b_glu", "s5_b_glu")):
        c, n = COLS[name]
        cols[:, c:c + LAYERS * n] = a[key].reshape(-1, P).T
    c, n = COLS["s5_d"]
    cols[:, c:c + LAYERS * n] = np.tile(a["s5_d"].reshape(SP2, GC).T, (L, 1))
    arrays["cols"] = cols

    lam = [np.tile(a[k].reshape(SP2, GS).T, (2, 1)) for k in ("s5_lambda_re", "s5_lambda_im")]
    dt = np.broadcast_to(a["s5_log_dt"].reshape(1, SP2), (P, SP2))
    arrays["s5p"] = np.stack([*lam, dt], axis=1)
    br, bi = (a[k].transpose(0, 2, 1, 3) for k in ("s5_b_re", "s5_b_im"))
    cr, ci = (a[k].transpose(0, 3, 1, 2) for k in ("s5_c_re", "s5_c_im"))
    both = [np.concatenate(p, axis=1) for p in ((br, bi), (bi, br), (cr, ci), (ci, cr))]
    m = np.stack(both, axis=2).reshape(LAYERS, P, 4, NB, GB * GC)
    arrays["s5m"] = m.transpose(0, 3, 1, 2, 4)

    wr, wi = (a[k].reshape(LAYERS, MT, P, LRU_WB).transpose(0, 2, 1, 3) for k in ("lru_w_rgate", "lru_w_igate"))
    arrays["wg"] = np.stack([wr, wi], axis=2)
    arrays["rw"] = tiles(a["router_w"][0])
    arrays["rb"] = np.broadcast_to(a["router_b"], (P, EXPERTS))
    arrays["fg"] = np.broadcast_to(a["final_norm"], (TOK, D))
    return {"in_" + k: np.ascontiguousarray(v) for k, v in arrays.items()}


def kernel(**inputs):
    import numpy as np
    from concourse import bacc
    from concourse.bass_utils import run_bass_kernel_spmd

    arrays = layout(inputs)
    nc = bacc.Bacc("TRN2", target_bir_lowering=False, num_devices=1)
    args = [nc.dram_tensor(k, v.shape, F32, kind="ExternalInput").ap() for k, v in arrays.items()]
    out = nc.dram_tensor("out_0", (T, D), F32, kind="ExternalOutput").ap()
    scratch = [nc.dram_tensor(n, s, F32).ap() for n, s in
               (("hs_d", (P, DK, T)), ("u_d", (GROUPS, GC, L, NC)), ("y_d", (GROUPS, GC, L, NC)),
                ("xg_d", (SLOTS, D)), ("yg_d", (SLOTS, D)))]
    build(nc, *args, out, *scratch)
    r = run_bass_kernel_spmd(nc, [arrays], core_ids=[0]).results[0]["out_0"]
    return np.ascontiguousarray(r[None, META:])
```

```python
from contextlib import ExitStack

import concourse.bass as bass
from concourse import mybir

F32 = mybir.dt.float32
F32R = mybir.dt.float32r
ALU = mybir.AluOpType
ACT = mybir.ActivationFunctionType
AX_X = mybir.AxisListType.X

P = 128
D = 1024
DK = D // P
META = 16
T = 512 + META
TH = T // 2
LAYERS = 2
W5 = 512
MT = W5 // P
GROUPS, GC, GS = 32, 16, 64
L = P // GC
NC = T // L
GB = 4
NB = GROUPS // GB
PADW = (2 * L - 1) * GC
TAPS = 400
SP2 = LAYERS * GROUPS
FF = 1536
FT = FF // P
EXPERTS = 8
TOK = 88
TB = T // TOK
S = 216
SH = S // 2
WIDTHS = (128, 160, 192, S)
QMAX = -(-T // S) - 1
EXTRA = 2 * T // S
SLOTS = (EXPERTS + EXTRA) * S
ZROWS = 8
U32 = mybir.dt.uint32
EPS = 1e-6
LRU_C = 8.0

UNIT = 8 * P
RING = 3
HALVES = ((0, slice(0, UNIT // 2)), (1, slice(UNIT // 2, UNIT)))
U_IN = 28
U_GLU = 2
U_MIX = U_IN + U_GLU + 8 + 8
U_FF = 3 * FT
STEP = 6
BODY = 6
SLOT3 = 3
UNITS = LAYERS * U_MIX + (2 + EXPERTS) * U_FF
ACC_MIX, ACC_FF = 24, 16

COLS, _at = {}, 0
for _name, _n in (("mix_norm", 8), ("ffn_norm", 8), ("merge_bias", 16), ("conv_w", 16), ("conv_b", 4),
                  ("b_r", 4), ("b_i", 4), ("lam", 4), ("b_glu", 4), ("s5_d", 32)):
    COLS[_name] = (_at, _n)
    _at += LAYERS * _n
NCOL = _at


def build(nc, xT, W, cols_d, s5p, s5m, wg, rw, rb, fg, out, hs_d, u_d, y_d, xg_d, yg_d):
    ctx = ExitStack()
    with ctx:
        cursor = [16512]

        def region(nbytes):
            start = cursor[0]
            cursor[0] += (nbytes + 31) // 32 * 32
            return start

        def place(name, shape, dt=F32, at=None):
            n = 4
            for s in shape[1:]:
                n *= s
            if at is None:
                start = region(n)
            else:
                start = at[0]
                at[0] += (n + 31) // 32 * 32
                assert at[0] <= at[1], name
            return nc.alloc_sbuf_tensor_at(name, shape, dt, offset=start)

        def shared(nbytes):
            start = region(nbytes)
            return lambda: [start, start + nbytes]

        def sem(name):
            return ctx.enter_context(nc.semaphore(name))

        H = shared(4 * 2 * DK * T)
        h = H()
        hs = place("hs", [P, DK, T], at=h)
        hn = place("hn", [P, DK, T], at=h)
        gates = place("gates", [P, 2 * DK, T], at=H())
        xh_at = cursor[0]
        xh = place("xh", [P, DK, T], F32R)
        xl = place("xl", [P, DK, T], F32R)
        raw = [place(f"raw{i}", [P, UNIT]) for i in range(RING)]
        wh = [place(f"wh{i}", [P, UNIT], F32R) for i in range(RING)]
        wl = [place(f"wl{i}", [P, UNIT], F32R) for i in range(RING)]
        FFR = shared(4 * 2 * FT * T)
        f = FFR()
        fh = place("fh", [P, FT, T], F32R, at=f)
        fl = place("fl", [P, FT, T], F32R, at=f)
        f = FFR()
        y1h = place("y1h", [P, MT, T], F32R, at=f)
        y1l = place("y1l", [P, MT, T], F32R, at=f)
        y2h = place("y2h", [P, MT, T], F32R, at=f)
        y2l = place("y2l", [P, MT, T], F32R, at=f)
        ybh = place("ybh", [P, MT, T], F32R, at=f)
        ybl = place("ybl", [P, MT, T], F32R, at=f)
        start = FFR()[0]
        f = [start, start + 4 * 4 * MT * T]
        m1 = place("m1", [P, GB, P], at=f)
        m1y = place("m1y", [P, GB, P], at=f)
        m2 = place("m2", [P, GB, P], at=f)
        m2y = place("m2y", [P, GB, P], at=f)
        m3 = place("m3", [P, GB, P], at=f)
        m1t = place("m1t", [P, GB, P], at=f)
        taps = place("taps", [P, GB * GC], at=f)
        cosT = place("cosT", [P, GB, NC], at=f)
        sinT = place("sinT", [P, GB, NC], at=f)
        decay = place("decay", [P, GB, NC], at=f)
        rot = place("rot", [P, GB, NC], at=f)
        rot2 = place("rot2", [P, GB, NC], at=f)
        turned = place("turned", [P, GB, NC], at=f)
        cr = place("cr", [P, GB, NC], at=f)
        sr = place("sr", [P, GB, NC], at=f)
        pbuf = place("pbuf", [P, 2, 4, GB * GC], at=f)
        b2s = place("b2s", [P, GB, GC], at=f)
        bx = place("bx", [P, GB, GC], at=f)
        by = place("by", [P, GB, GC], at=f)
        c1 = place("c1", [P, GB, GC], at=f)
        c2 = place("c2", [P, GB, GC], at=f)
        pt1 = place("pt1", [P, GB * P], at=f)
        pt2 = place("pt2", [P, GB * P], at=f)
        dt1 = place("dt1", [P, GB * P], at=f)
        LR = shared(4 * (14 * T + T + 3 + 8))
        f = LR()
        xc = place("xc", [P, MT, T], at=f)
        gg = place("gg", [P, MT, T], at=f)
        ra = place("ra", [P, 2, T], at=f)
        ii = place("ii", [P, 2, T], at=f)
        th = place("th", [P, 2, T], at=f)
        xpad = place("xpad", [P, T + 3], at=f)
        uperm = place("uperm", [P, MT, L, NC], at=[LR()[0] + 4 * 8 * T, LR()[1]])
        f = LR()
        gt = place("gt", [P, 2, T], at=f)
        ft = place("ft", [P, 2, T], at=f)
        f = [LR()[0] + 4 * 12 * T, LR()[1]]
        zero = place("zero", [P, D], at=f)
        f = LR()
        pp = {n: place("p_" + n, [P, SP2], at=f) for n in
              ("lr", "li", "ldt", "dt", "ang", "k", "red", "red2", "sin", "cos", "mag", "num", "den",
               "rden", "t1", "t2", "t3")}

        UU = shared(4 * GROUPS * NC)
        uu = place("uu", [P, GROUPS, NC], at=UU())
        yt = place("yt", [P, MT, L, NC], at=UU())
        ys = place("ys", [P, 2, GB, NC])
        rs = place("rs", [P, T], at=[LR()[0] + 4 * 8 * T, LR()[1]])
        cols = place("cols", [P, NCOL])
        apr = place("apr", [P, L + 1, SP2])
        api = place("api", [P, L + 1, SP2])
        sqr = place("sqr", [P, 7, SP2])
        sqi = place("sqi", [P, 7, SP2])
        mag8 = place("mag8", [P, SP2])
        cfr = place("cfr", [P, SP2])
        cfi = place("cfi", [P, SP2])
        sp8 = place("sp8", [P, LAYERS * MT])
        sp8n = place("sp8n", [P, LAYERS * MT])
        spt = [place(f"spt{i}", [P, LAYERS * MT]) for i in range(4)]
        sgn = place("sgn", [P, 2])
        warm = place("warm", [P, 1])
        ones = place("ones", [P, P])
        ident = place("ident", [P, PADW])
        gw = place("gw", [P, 2, MT, LRU_WB])
        rws = place("rws", [P, DK, EXPERTS])
        rbs = place("rbs", [P, EXPERTS])
        lg = place("lg", [P, TB, EXPERTS])
        cmp1 = place("cmp1", [P, TB, EXPERTS, EXPERTS], at=[UU()[0], UU()[1]])
        cmp2 = place("cmp2", [P, TB, EXPERTS, EXPERTS], at=[UU()[0] + 4 * TB * 64, UU()[1]])
        lgt = place("lgt", [P, T], at=[UU()[0] + 4 * 2 * TB * 64, UU()[1]])
        rank = place("rank", [P, TB, EXPERTS])
        gate = place("gate", [P, TB, EXPERTS])
        gtmp = place("gtmp", [P, TB, EXPERTS])
        v1, v2, ex, g1, g2 = (place(n, [P, TB]) for n in ("v1", "v2", "ex", "g1", "g2"))
        idx = place("idx", [P, 2, TB], U32)
        tab = place("tab", [P, EXTRA + 1 + EXPERTS], U32)
        ssq = place("ssq", [P, TB])

        f = [xh_at, xh_at + 4 * 2 * DK * T]
        hn_tok = place("hn_tok", [TOK, TB, D], at=f)
        f = [xh_at, xh_at + 4 * 2 * DK * T]
        xg = place("xg", [P, DK, 2, S], F32R, at=f)
        f = FFR()
        fg2 = place("fg2", [P, FT, 2, S], F32R, at=f)
        hs_tok = place("hs_tok", [TOK, TB, D], at=f)
        gmb = place("gmb", [TOK, D], at=f)
        f = LR()
        tri = place("tri", [P, EXPERTS, EXPERTS], at=f)
        tris = place("tris", [P, TOK], at=f)
        sel1 = place("sel1", [P, TB, EXPERTS], at=f)
        sel2 = place("sel2", [P, TB, EXPERTS], at=f)
        mask = place("mask", [P, TB, EXPERTS], at=f)
        off = place("off", [P, TB + 1, EXPERTS], at=f)
        pos = place("pos", [P, TB, EXPERTS], at=f)
        qq = place("qq", [P, TB, EXPERTS], at=f)
        big = place("big", [P, TB, EXPERTS], at=f)
        slot = place("slot", [P, TB, EXPERTS], at=f)
        ev, oneE, extra, incl, ebase, xtmp = (place(n, [P, EXPERTS], at=f) for n in
                                              ("ev", "oneE", "extra", "incl", "ebase", "xtmp"))
        iv = place("iv", [P, EXTRA], at=f)
        oneI = place("oneI", [P, EXTRA], at=f)
        in1 = place("in1", [P, EXTRA, EXPERTS], at=f)
        in2 = place("in2", [P, EXTRA, EXPERTS], at=f)
        tabf = place("tabf", [P, EXTRA + 1 + EXPERTS], at=f)
        sf = place("sf", [P, 2, TB], at=f)
        f = [LR()[0] + 4 * 3 * T, LR()[1]]
        gs, gx, us, fx = (place(n, [P, SLOT3, S], at=f) for n in ("gs", "gx", "us", "fx"))
        xt = place("xt", [SH, 2, D], at=f)
        f = H()
        f[0] += 4 * DK * T
        y_t = place("y_t", [P, DK, S], at=f)
        ytok = place("ytok", [SH, 2, D], at=f)
        f = H()
        ya = place("ya", [TOK, 2, D], at=f)
        yb = place("yb", [TOK, 2, D], at=f)
        f = [xh_at, xh_at + 4 * 2 * DK * T]
        ot = place("ot", [TOK, 2, D], at=f)
        sqt = place("sqt", [TOK, D], at=f)
        assert cursor[0] <= nc.sbuf_usable_end

        acc = ctx.enter_context(nc.psum_tensor("acc", [P, 2, 2, 512], F32))
        side = ctx.enter_context(nc.psum_tensor("side", [P, 4, 512], F32))

        def merge_sums(m):
            return (side[:, 0:2, :], side[:, 2:4, :]) if m % 2 else (acc[:, 0, :, :], acc[:, 1, :, :])

        side_free = [sem("side_free0"), sem("side_free1")]
        raw_landed = [[sem(f"raw_landed{i}_{h}") for h in range(2)] for i in range(RING)]
        hi_ready = [sem(f"hi_ready{i}") for i in range(RING)]
        lo_ready = [sem(f"lo_ready{i}") for i in range(RING)]
        unit_done = [sem(f"unit_done{i}") for i in range(RING)]
        acc_free = [sem(f"acc_free{i}") for i in range(2)]
        x_landed, small_landed = sem("x_landed"), sem("small_landed")
        const_ready = sem("const_ready")
        hs_ready, sq_ready, ss_ready, rms_ready = sem("hs_ready"), sem("sq_ready"), sem("ss_ready"), sem("rms_ready")
        hn_ready, xh_ready, xl_ready = sem("hn_ready"), sem("xh_ready"), sem("xl_ready")
        hs_saved, hs_back = sem("hs_saved"), sem("hs_back")
        prep_in = sem("prep_in")
        prep_act, prep_dve, prep_pool = sem("prep_act"), sem("prep_dve"), sem("prep_pool")
        up_ready, u_out, u_in = sem("up_ready"), sem("u_out"), sem("u_in")
        xp_ready, xc_ready, gg_ready = sem("xp_ready"), sem("xc_ready"), sem("gg_ready")
        gm_done, ri_ready = sem("gm_done"), sem("ri_ready")
        lru_a, lru_t, lru_m, lru_r = sem("lru_a"), sem("lru_t"), sem("lru_m"), sem("lru_r")
        yb_ready, ybh_ready, ybl_ready = sem("yb_ready"), sem("ybh_ready"), sem("ybl_ready")
        gates_ready = sem("gates_ready")
        pb_landed = [sem("pb_landed0"), sem("pb_landed1")]
        wg_landed = sem("wg_landed")
        m1t_ready, tab_ready, c_ready = sem("m1t_ready"), sem("tab_ready"), sem("c_ready")
        taps_done, taps_ready, turn_ready = sem("taps_done"), sem("taps_ready"), sem("turn_ready")
        p1_done, p2_done, p3_done = sem("p1_done"), sem("p2_done"), sem("p3_done")
        m_act, m_dve, m2_ready, rot_ready = sem("m_act"), sem("m_dve"), sem("m2_ready"), sem("rot_ready")
        ys_ready, y_out, y_in = sem("ys_ready"), [sem("y_out0"), sem("y_out1")], [sem("y_in0"), sem("y_in1")]
        y1_ready, y1h_ready, y1l_ready = sem("y1_ready"), sem("y1h_ready"), sem("y1l_ready")
        sg_ready, y2_ready, y2h_ready, y2l_ready = sem("sg_ready"), sem("y2_ready"), sem("y2h_ready"), sem("y2l_ready")
        mg_ready = sem("mg_ready")
        g_ready, f_ready, fh_ready, fl_ready = sem("g_ready"), sem("f_ready"), sem("fh_ready"), sem("fl_ready")
        lgt_ready, lgt_done = sem("lgt_ready"), sem("lgt_done")
        lg_done, ex_ready, d_ready, mask_ready, pos_done, slot_ready, tab_ready2 = (
            sem(n) for n in ("lg_done", "ex_ready", "d_ready", "mask_ready", "pos_done", "slot_ready", "table_ready"))
        acc_set = sem("acc_set")
        zero_set, zeroed, tok_done, hn_tok_ready, hs_tok_ready, scattered, gm_landed = (
            sem(n) for n in ("zero_set", "zeroed", "tok_done", "hn_tok_ready", "hs_tok_ready", "scattered", "gm_landed"))
        xt_landed, xt_read, xgh_ready, xgl_ready = (sem(n) for n in ("xt_landed", "xt_read", "xgh_ready", "xgl_ready"))
        half_ready = [sem("half_ready0"), sem("half_ready1")]
        gx_ready, fx_ready, fgh_ready, fgl_ready = sem("gx_ready"), sem("fx_ready"), sem("fgh_ready"), sem("fgl_ready")
        y_tr, ytok_ready, all_stored = sem("y_tr"), sem("ytok_ready"), sem("all_stored")
        y_stored = [sem("y_stored0"), sem("y_stored1")]
        ya_in, sum_ready, rms2_ready, sq2_ready, ot_ready = (
            [sem("ya_in0"), sem("ya_in1")], sem("sum_ready"), sem("rms2_ready"), sem("sq2_ready"), sem("ot_ready"))
        out_done = [sem("out_done0"), sem("out_done1")]
        act_chain, dve_chain, pool_chain = sem("act_chain"), sem("dve_chain"), sem("pool_chain")

        block = ctx.enter_context(nc.Block())
        ZDMAS = -(-SLOTS // P) - (-EXTRA * S // P)

        def col(name, layer, tile):
            at, n = COLS[name]
            return cols[:, at + layer * n + tile:at + layer * n + tile + 1]

        def use(u, more=0):
            return u % RING, u // RING + more

        def halves(x):
            return x.rearrange("p (b c) -> p b c", b=2)

        def perm(x):
            return x.rearrange("p j c -> p c j")

        def chunked(x):
            return x.rearrange("p (c j) -> p c j", j=L)

        mix_u = [0, U_MIX + 2 * U_FF]
        mix_acc = [0, ACC_MIX + 2 * ACC_FF]
        ff_u = [U_MIX, 2 * U_MIX + 2 * U_FF]
        ff_acc = [ACC_MIX, 2 * ACC_MIX + 2 * ACC_FF]
        ff_e0 = [0, 2]
        ff_n = [2, EXPERTS]
        hs_at_norm = [0, 8, 24, 32, 96]

        def slot_of(k):
            return divmod(k - 3, 3) if 3 <= k < 3 + 3 * NB else (None, None)

        KIND = [("u", m) for m in range(MT)]
        for m in range(MT):
            KIND += [("x", m), ("g", m)]
        KIND += [("gate", q) for q in range(2 * DK)]

        @block.sync
        def _(sp):
            sp.dma_start(cols[:, :], cols_d).then_inc(small_landed, 16)
            for m in range(DK):
                sp.dma_start(hs[:, m, :], xT[:, m, :]).then_inc(x_landed, 16)
            for u in range(RING):
                for h, cs in HALVES:
                    sp.dma_start(raw[u][:, cs], W[u, :, cs]).then_inc(raw_landed[u][h], 16)
            with sp.Fori(1, UNITS // RING) as it:
                for s in range(RING):
                    for h, cs in HALVES:
                        sp.wait_ge(lo_ready[s], it * 2 + (h - 1))
                        sp.dma_start(raw[s][:, cs], W[it * RING + s, :, cs]).then_inc(raw_landed[s][h], 16)
            for u in range(UNITS // RING * RING, UNITS):
                s, n = use(u)
                for h, cs in HALVES:
                    sp.wait_ge(lo_ready[s], 2 * n + h - 1)
                    sp.dma_start(raw[s][:, cs], W[u, :, cs]).then_inc(raw_landed[s][h], 16)
            sp.wait_ge(tab_ready2, 1)
            n_extra = sp.value_load(tab[0:1, 0:1], min_val=0, max_val=EXTRA)
            with sp.If(n_extra > 0):
                with sp.Fori(0, n_extra) as i:
                    e = sp.value_load(tab[0:1, bass.ds(i + 1, 1)], min_val=0, max_val=EXPERTS - 1)
                    with sp.Fori(0, U_FF // RING) as it:
                        for j in range(RING):
                            s, n = use(UNITS + j, i * (U_FF // RING) + it)
                            for h, cs in HALVES:
                                sp.wait_ge(lo_ready[s], n * 2 + (h - 1))
                                sp.dma_start(raw[s][:, cs], W[e * U_FF + it * RING + (ff_u[1] + j), :, cs])\
                                  .then_inc(raw_landed[s][h], 16)
            for t in range(TB):
                sp.wait_ge(ot_ready, t + 1)
                sp.dma_start(out[t * TOK:(t + 1) * TOK, :], ot[:, t % 2, :]).then_inc(out_done[t % 2], 16)
            for i in range(2):
                sp.wait_ge(out_done[i], 16 * TB // 2)

        @block.gpsimd
        def _(pool):
            g = nc.gpsimd
            chain = [0]

            def link(ins):
                chain[0] += 1
                ins.then_inc(pool_chain, 1)
                pool.wait_ge(pool_chain, chain[0])

            def tt(out, a, b, op):
                link(g.tensor_tensor(out, a, b, op))

            g.memset(ones[:, :], 1.0).then_inc(const_ready, 1)
            link(g.memset(ident[:, :], 0.0))
            g.affine_select(out=ident[:, 0:P], in_=ident[:, 0:P], compare_op=ALU.not_equal, fill=1.0, base=0,
                            pattern=[[-1, P]], channel_multiplier=1).then_inc(const_ready, 1)
            pool.wait_ge(const_ready, 2)
            link(g.memset(apr[:, 0, :], 1.0))
            link(g.memset(api[:, 0, :], 0.0))
            g.memset(xpad[:, 0:3], 0.0).then_inc(const_ready, 1)
            pool.dma_start(rws[:, :, :], rw).then_inc(prep_pool, 16)
            pool.dma_start(rbs[:, :], rb).then_inc(prep_pool, 16)
            pool.wait_ge(prep_act, 4)
            t1, t2 = pp["t1"][:, :], pp["t2"][:, :]
            c, s = pp["cos"][:, :], pp["sin"][:, :]
            tt(apr[:, 1, :], pp["mag"][:, :], c, ALU.mult)
            tt(api[:, 1, :], pp["mag"][:, :], s, ALU.mult)

            def product(outr, outi, ar, ai, br, bi, x1=t1, x2=t2):
                tt(x1, ar, br, ALU.mult)
                tt(x2, ai, bi, ALU.mult)
                tt(x1, x1, x2, ALU.subtract)
                tt(x2, ar, bi, ALU.mult)
                tt(outi, ai, br, ALU.mult)
                tt(outi, outi, x2, ALU.add)
                link(g.tensor_copy(outr, x1))

            pool.wait_ge(prep_dve, 2)
            link(g.tensor_scalar(pp["num"][:, :], apr[:, 1, :], 1.0, 0.0, ALU.subtract, ALU.add))
            num, lr, li = pp["num"][:, :], pp["lr"][:, :], pp["li"][:, :]
            tt(t1, num, lr, ALU.mult)
            tt(t2, api[:, 1, :], li, ALU.mult)
            tt(t1, t1, t2, ALU.add)
            tt(cfr[:, :], t1, pp["rden"][:, :], ALU.mult)
            tt(t1, api[:, 1, :], lr, ALU.mult)
            tt(t2, num, li, ALU.mult)
            tt(t1, t1, t2, ALU.subtract)
            tt(cfi[:, :], t1, pp["rden"][:, :], ALU.mult)
            for k in range(2, L + 1):
                product(apr[:, k, :], api[:, k, :], apr[:, k - 1, :], api[:, k - 1, :], apr[:, 1, :], api[:, 1, :])
            for l in range(LAYERS):
                if l:
                    pool.wait_ge(hs_ready, hs_at_norm[1])
                    link(g.memset(zero[:, :], 0.0))
                    for z in range(0, SLOTS, P):
                        n = min(P, SLOTS - z)
                        pool.dma_start(xg_d[z:z + n, :], zero[0:n, :]).then_inc(zeroed, 16)
                    for z in range(EXPERTS * S, SLOTS, P):
                        n = min(P, SLOTS - z)
                        pool.dma_start(yg_d[z:z + n, :], zero[0:n, :]).then_inc(zeroed, 16)
                    pool.wait_ge(zeroed, ZDMAS * 16)
                    pool.wait_ge(hs_ready, hs_at_norm[2])
                for r in range(2):
                    pool.dma_start(gw[:, r, :, :], wg[l, :, r, :, :]).then_inc(wg_landed, 16)
                for b in range(2):
                    pool.dma_start(pbuf[:, b, :, :], s5m[l, b, :, :, :]).then_inc(pb_landed[b], 16)
                link(g.memset(cosT[:, :, 0:1], 1.0))
                link(g.memset(sinT[:, :, 0:1], 0.0))
                link(g.memset(decay[:, :, 0:1], 0.0))
                for b in range(NB):
                    done = l * NB + b
                    gs = slice(l * GROUPS + b * GB, l * GROUPS + (b + 1) * GB)
                    v = lambda x: x.rearrange("p (g h) -> p g h", g=GB)
                    b1, braw, craw1, craw2 = (v(pbuf[:, b % 2, i, :]) for i in range(4))
                    wide = [P, GB, GC]
                    cb = lambda x: x[:, gs].unsqueeze(2).to_broadcast(wide)
                    pool.wait_ge(pb_landed[b % 2], 16 * (l * NB // 2 + b // 2 + 1))
                    if done:
                        pool.wait_ge(p1_done, done)
                        pool.wait_ge(m2_ready, done)
                    link(g.tensor_scalar(b2s[:, :, :], braw, sgn[:, 0:1], 0.0, ALU.mult, ALU.add))
                    link(g.tensor_scalar(c1[:, :, :], craw1, sgn[:, 1:2], 0.0, ALU.mult, ALU.add))
                    g.tensor_scalar(c2[:, :, :], craw2, -1.0, 0.0, ALU.mult, ALU.add).then_inc(c_ready, 1)
                    x1, x2 = v(pt1[:, 0:GB * GC]), v(pt2[:, 0:GB * GC])
                    tt(x1, cb(cfr), b1, ALU.mult)
                    tt(x2, cb(cfi), b2s[:, :, :], ALU.mult)
                    tt(bx[:, :, :], x1, x2, ALU.add)
                    tt(x1, cb(cfr), b2s[:, :, :], ALU.mult)
                    tt(x2, cb(cfi), b1, ALU.mult)
                    tt(by[:, :, :], x1, x2, ALU.subtract)
                    pool.wait_ge(c_ready, done + 1)
                    if b + 2 < NB:
                        pool.dma_start(pbuf[:, b % 2, :, :], s5m[l, b + 2, :, :, :]).then_inc(pb_landed[b % 2], 16)
                    for j in range(L):
                        ab = lambda x: x[:, L - 1 - j, gs].unsqueeze(2).to_broadcast(wide)
                        y1, y2 = (v(x[:, j * 64:j * 64 + 64]) for x in (pt1, pt2))
                        g.tensor_tensor(y1, ab(apr), bx[:, :, :], ALU.mult)
                        last = g.tensor_tensor(y2, ab(api), by[:, :, :], ALU.mult)
                    link(last)
                    w4 = lambda x: x[:, :].rearrange("p (j g h) -> p g j h", g=GB, h=GC)
                    g.tensor_tensor(m1t[:, :, 0:L * GC].rearrange("p g (j h) -> p g j h", h=GC), w4(pt1), w4(pt2),
                                    ALU.add).then_inc(m1t_ready, 1)
                    if done:
                        pool.wait_ge(rot_ready, done)
                    else:
                        pool.wait_ge(turn_ready, 1)
                    pool.wait_ge(m1t_ready, done + 1)
                    col1 = lambda x: x[:, gs].unsqueeze(2).to_broadcast([P, GB, NC - 1])
                    link(g.tensor_copy(decay[:, :, 1:NC], col1(mag8)))
                    link(g.tensor_copy(cosT[:, :, 1:2], sqr[:, 0, gs].unsqueeze(2)))
                    link(g.tensor_copy(sinT[:, :, 1:2], sqi[:, 0, gs].unsqueeze(2)))
                    k = 1
                    for i in range(1, 7):
                        k *= 2
                        n = min(k, NC - k)
                        br = sqr[:, i, gs].unsqueeze(2).to_broadcast([P, GB, n])
                        bi = sqi[:, i, gs].unsqueeze(2).to_broadcast([P, GB, n])
                        z1, z2, z3, z4 = (x[:, o:o + GB * n].rearrange("p (g c) -> p g c", g=GB)
                                          for x in (pt1, pt2) for o in (0, 256))
                        g.tensor_tensor(z1, cosT[:, :, 0:n], br, ALU.mult)
                        g.tensor_tensor(z3, sinT[:, :, 0:n], bi, ALU.mult)
                        g.tensor_tensor(z2, cosT[:, :, 0:n], bi, ALU.mult)
                        tt(z4, sinT[:, :, 0:n], br, ALU.mult)
                        g.tensor_tensor(cosT[:, :, k:k + n], z1, z3, ALU.subtract)
                        last = g.tensor_tensor(sinT[:, :, k:k + n], z2, z4, ALU.add)
                        if i < 6:
                            link(last)
                    last.then_inc(tab_ready, 1)
                    pool.wait_ge(tab_ready, done + 1)
            pool.wait_ge(xl_ready, 5 * DK)
            pool.dma_start(gmb[:, :], fg).then_inc(gm_landed, 16)
            link(g.memset(tris[:, :], 1.0))
            link(g.affine_select(out=tris[:, :], in_=tris[:, :], compare_op=ALU.is_gt, fill=0.0, base=0,
                                 pattern=[[1, TOK]], channel_multiplier=-1))
            link(g.memset(tri[:, :, :], 1.0))
            g.affine_select(out=tri[:, :, :], in_=tri[:, :, :], compare_op=ALU.is_gt, fill=0.0, base=0,
                            pattern=[[1, EXPERTS], [-1, EXPERTS]], channel_multiplier=0).then_inc(const_ready, 1)

            pool.wait_ge(zeroed, ZDMAS * 16)
            pool.wait_ge(slot_ready, 1)
            for t in range(TB):
                pool.wait_ge(hn_tok_ready, t + 1)
                for k in range(2):
                    pool.indirect_dma_start(xg_d, bass.IndirectOffsetOnAxis(ap=idx[0:TOK, k, t:t + 1], axis=0),
                                            hn_tok[:, t, :], None).then_inc(scattered, 16)
            pool.wait_ge(scattered, 2 * TB * 16)

            def rows(d, b):
                return d[bass.ds(b * S, S), :].rearrange("(h p) c -> p h c", h=2)

            def lower_hidden(b):
                with pool.Fori(0, FT // BODY) as it:
                    for i in range(BODY):
                        m = it * BODY + i
                        pool.wait_ge(fgh_ready, b * FT + m + 1)
                        g.tensor_tensor(fg2[:, m, 1, :], fx[:, i % SLOT3, :], fg2[:, m, 0, :].bitcast(F32), ALU.subtract)\
                            .then_inc(fgl_ready, 1)

            pool.dma_start(xt[:, :, :], xg_d[0:S, :].rearrange("(h p) c -> p h c", h=2)).then_inc(xt_landed, 16)
            with pool.Fori(1, EXPERTS) as b:
                pool.wait_ge(xt_read, b)
                pool.dma_start(xt[:, :, :], rows(xg_d, b)).then_inc(xt_landed, 16)
                lower_hidden(b - 1)
            lower_hidden(EXPERTS - 1)
            pool.wait_ge(tab_ready2, 1)
            n_extra = pool.value_load(tab[0:1, 0:1], min_val=0, max_val=EXTRA)
            with pool.If(n_extra > 0):
                with pool.Fori(0, n_extra) as i:
                    pool.wait_ge(xt_read, i + EXPERTS)
                    pool.dma_start(xt[:, :, :], rows(xg_d, i + EXPERTS)).then_inc(xt_landed, 16)
                    lower_hidden(i + EXPERTS)
            for c in range(2):
                pool.wait_ge(y_stored[c], (n_extra + (EXPERTS + 1)) * 16)
            pool.sem_inc(all_stored, 1)
            pool.wait_ge(all_stored, 1)
            for t in range(TB):
                if t >= 2:
                    pool.wait_ge(sum_ready, t - 1)
                for k, dst in ((0, ya), (1, yb)):
                    pool.indirect_dma_start(dst[:, t % 2, :], None, yg_d,
                                            bass.IndirectOffsetOnAxis(ap=idx[0:TOK, k, t:t + 1], axis=0))\
                        .then_inc(ya_in[t % 2], 16)

        @block.scalar
        def _(act):
            a = nc.scalar
            chain = [0]

            def link(ins):
                chain[0] += 1
                ins.then_inc(act_chain, 1)
                act.wait_ge(act_chain, chain[0])

            def split_hi(u, more=0):
                if isinstance(u, int) and isinstance(more, int) and u + RING * more >= UNITS:
                    return
                s, n = use(u, more)
                if u >= RING:
                    act.wait_ge(unit_done[s], n)
                for h, cs in HALVES:
                    act.wait_ge(raw_landed[s][h], n * 16 + 16)
                    a.activation(wh[s][:, cs], raw[s][:, cs], ACT.Copy).then_inc(hi_ready[s], 1)

            def arrived(u, more=0):
                s, n = use(u, more)
                act.wait_ge(unit_done[s], n + 1)

            def square(i, m):
                if i == 0:
                    act.wait_ge(x_landed, 16 * DK)
                else:
                    act.wait_ge(hs_ready, hs_at_norm[i] - DK + m + 1)
                a.activation(hn[:, m, :], hs[:, m, :], ACT.Square).then_inc(sq_ready, 1)

            def norm(i):
                act.wait_ge(const_ready, 1)
                a.activation(warm[:, :], ones[:, 0:1], ACT.Sqrt)
                act.wait_ge(ss_ready, i + 1)
                a.activation(halves(rs[:, :]), side[:, 0:2, 0:TH], ACT.Sqrt, scale=1.0 / D, bias=EPS)\
                    .then_inc(rms_ready, 1)
                if i == 3:
                    return
                for m in range(DK):
                    act.wait_ge(hn_ready, i * DK + m + 1)
                    a.activation(xh[:, m, :], hn[:, m, :], ACT.Copy).then_inc(xh_ready, 1)

            def lru_pair(l, q):
                n = l * 2 + q
                act.wait_ge(ri_ready, 4 * n + 4)
                act.wait_ge(prep_dve, 4)
                if n:
                    act.wait_ge(yb_ready, 2 * n)
                for i in range(2):
                    t = l * MT + 2 * q + i
                    a.activation(th[:, i, :], ra[:, i, :], ACT.Tanh, scale=sp8[:, t:t + 1]).then_inc(lru_t, 1)
                act.wait_ge(lru_t, 2 * n + 2)
                for i in range(2):
                    t = l * MT + 2 * q + i
                    a.activation(ra[:, i, :], ra[:, i, :], ACT.Exp, scale=sp8n[:, t:t + 1]).then_inc(lru_a, 1)
                act.wait_ge(lru_m, n + 1)
                a.activation(th[:, :, :], th[:, :, :], ACT.Sqrt).then_inc(lru_r, 1)

            def lru_out(l, q):
                for t in (2 * q, 2 * q + 1):
                    act.wait_ge(yb_ready, l * MT + t + 1)
                    a.activation(ybh[:, t, :], gg[:, t, :], ACT.Copy).then_inc(ybh_ready, 1)

            def gate_sigmoid(l, q):
                t, r = q // 2, q % 2
                act.wait_ge(gm_done, l * 8 + q + 1)
                act.wait_ge(u_out, 64 * (l + 1))
                dst = (ra, ii)[r]
                if t >= 2:
                    act.wait_ge(yb_ready, l * MT + 2)
                a.activation(halves(dst[:, t % 2, :]), side[:, 2:4, 0:TH], ACT.Sigmoid,
                             bias=col(("b_r", "b_i")[r], l, t)).then_inc(ri_ready, 1)

            def s5_back(l, t):
                for i in range(2):
                    act.wait_ge(y_out[i], 16 * L * (NB // 2 * l + t + 1))
                act.dma_start(yt[:, t, :, :].rearrange("p j c -> p (j c)"),
                              y_d[8 * t:8 * t + 8].rearrange("g h j c -> (g h) (j c)"))\
                   .then_inc(y_in[t == MT - 1], 16)

            def s5_out(l, tiles):
                act.wait_ge(y_in[tiles[0] == MT - 1], 16 * (l + 1) * len(tiles))
                for m in tiles:
                    a.activation(yt[:, m, :, :], yt[:, m, :, :], ACT.Gelu_apprx_tanh).then_inc(y1_ready, 1)
                for m in tiles:
                    act.wait_ge(y1_ready, l * MT + m + 1)
                    a.activation(chunked(y1h[:, m, :]), perm(yt[:, m, :, :]), ACT.Copy).then_inc(y1h_ready, 1)

            def mixer(l):
                u0, a0 = mix_u[l], mix_acc[l]
                for k in range(U_IN):
                    split_hi(u0 + k + 2)
                    kind, m = KIND[k]
                    if k == 4:
                        act.wait_ge(u_out, 64 * (l + 1))
                        for j in range(L):
                            act.dma_start(uu[j * GC:(j + 1) * GC, :, :],
                                          u_d[:, :, j, :].rearrange("g h c -> h g c")).then_inc(u_in, 16)
                    if k >= 9 and k % 6 == 3 and k < U_IN - 1:
                        s5_back(l, (k - 9) // 6)
                    arrived(u0 + k)
                    src = acc[:, k % 2, :, 0:TH]
                    if kind == "u":
                        if l and m == 0:
                            act.wait_ge(hs_ready, hs_at_norm[2])
                        a.activation(uperm[:, m, :, :].rearrange("p j (b c) -> p b c j", b=2),
                                     src.rearrange("p b (c j) -> p b c j", j=L), ACT.Copy).then_inc(acc_free[k % 2], 1)
                        act.wait_ge(acc_free[k % 2], a0 + k // 2 + 1)
                        act.dma_start(u_d[8 * m:8 * m + 8].rearrange("g h j c -> (g h) (j c)"),
                                      uperm[:, m, :, :].rearrange("p j c -> p (j c)")).then_inc(u_out, 16)
                    elif kind == "x":
                        if m or l:
                            act.wait_ge(xc_ready, l * MT + m)
                        if m == 0:
                            act.wait_ge(const_ready, 3)
                        a.activation(halves(xpad[:, 3:3 + T]), src, ACT.Copy).then_inc(acc_free[k % 2], 1)
                    elif kind == "g":
                        a.activation(halves(gg[:, m, :]), src, ACT.Gelu_apprx_tanh).then_inc(acc_free[k % 2], 1)
                    else:
                        if m == 0:
                            act.wait_ge(xl_ready, xl_at_norm(2 * l) + DK)
                            if l:
                                act.wait_ge(hs_saved, 32)
                        a.activation(halves(gates[:, m, :]), src, ACT.Sigmoid,
                                     bias=col("merge_bias", l, m)).then_inc(acc_free[k % 2], 1)
                    b, part = slot_of(k)
                    if b is None:
                        continue
                    n = l * NB + b
                    if part == 0:
                        act.wait_ge(taps_done, n + 1)
                        a.activation(taps[:, :], side[:, 2, TAPS:TAPS + GB * GC], ACT.Copy).then_inc(taps_ready, 1)
                        act.wait_ge(p1_done, n + 1)
                        mt = side[:, 0, :].rearrange("p (g s) -> p g s", g=GB)
                        a.activation(m1[:, :, :], mt, ACT.Copy)
                        a.activation(m1y[:, :, 0:GS], mt[:, :, GS:P], ACT.Copy)
                        a.activation(m1y[:, :, GS:P], mt[:, :, 0:GS], ACT.Copy, scale=-1.0).then_inc(m_act, 1)
                        if 1 <= b <= MT:
                            gate_sigmoid(l, 2 * b - 1)
                        if b in (2, 4):
                            lru_pair(l, b // 2 - 1)
                    elif part == 1 and b in (2, 4):
                        lru_out(l, b // 2 - 1)
                    elif part == 2:
                        act.wait_ge(p3_done, n + 1)
                        if n >= 2:
                            act.wait_ge(y_out[b % 2], 16 * L * (n // 2))
                        a.activation(ys[:, b % 2, :, :],
                                     side[:, 0, 0:GB * NC].rearrange("p (g c) -> p g c", g=GB),
                                     ACT.Copy).then_inc(ys_ready, 1)
                        act.wait_ge(ys_ready, n + 1)
                        for j in range(L):
                            act.dma_start(y_d[b * GB:(b + 1) * GB, :, j, :].rearrange("g h c -> h g c"),
                                          ys[j * GC:(j + 1) * GC, b % 2, :, :]).then_inc(y_out[b % 2], 16)
                        if b < MT:
                            gate_sigmoid(l, 2 * b)
                s5_back(l, MT - 1)
                s5_out(l, range(MT - 1))
                s5_out(l, (MT - 1,))
                a1 = a0 + U_IN // 2
                for v in range(U_GLU):
                    u = u0 + U_IN + v
                    split_hi(u + 2)
                    arrived(u)
                    for i in range(2):
                        n = l * MT + 2 * v + i
                        if n >= 2:
                            act.wait_ge(y2_ready, n - 1)
                        if v == 0 and i == 0:
                            act.wait_ge(ybl_ready, (l + 1) * MT)
                        a.activation(halves(gt[:, i, :]), acc[:, i, :, 0:TH], ACT.Sigmoid,
                                     bias=col("b_glu", l, 2 * v + i)).then_inc(acc_free[i], 1)
                    for i in range(2):
                        act.wait_ge(y2_ready, l * MT + 2 * v + i + 1)
                        a.activation(y2h[:, 2 * v + i, :], ft[:, i, :], ACT.Copy).then_inc(y2h_ready, 1)
                for m in range(DK):
                    u = u0 + U_IN + U_GLU + m
                    split_hi(u + 2)
                    act.wait_ge(mg_ready, l * DK + m + 1)
                    a.activation(xh[:, m, :], ft[:, 0, :], ACT.Copy).then_inc(xh_ready, 1)
                for m in range(DK):
                    act.dma_start(hs[:, m, :], (hs_d if l else xT)[:, m, :]).then_inc(hs_back, 16)
                for m in range(DK):
                    split_hi(u0 + U_MIX - DK + m + 2)
                    if m:
                        square(2 * l + 1, m - 1)
                square(2 * l + 1, DK - 1)

            def expert(l, u0, e, e_all):
                with act.Fori(0, 2 * FT // STEP) as it:
                    more = e * (U_FF // RING) + it * (STEP // RING)
                    for i in range(STEP // 2):
                        m = it * (STEP // 2) + i
                        u = u0 + 2 * i
                        split_hi(u + 2, more)
                        arrived(u, more)
                        a.activation(halves(gt[:, 0, :]), acc[:, 0, :, 0:TH], ACT.Silu).then_inc(acc_free[0], 1)
                        split_hi(u + 3, more)
                        act.wait_ge(f_ready, e_all * FT + m + 1)
                        a.activation(fh[:, m, :], ft[:, 0, :], ACT.Copy).then_inc(fh_ready, 1)

            def down(u0, e, last):
                more = e * (U_FF // RING)
                for j in range(FT):
                    split_hi(u0 + 2 * FT + j + 2, more)
                    if last and j and (j - 1) % 3:
                        square(2, down_tile(j - 1))
                if last:
                    act.dma_start(hs_d[:, 0:DK - 1, :], hs[:, 0:DK - 1, :]).then_inc(hs_saved, 16)
                    square(2, DK - 1)

            def silu_table():
                a.activation(warm[:, :], ones[:, 0:1], ACT.Silu)

            for n, i in (("lr", 0), ("li", 1), ("ldt", 2)):
                act.dma_start(pp[n][:, :], s5p[:, i, :]).then_inc(prep_in, 16)
            for m in range(DK):
                square(0, m)
            act.wait_ge(prep_in, 16 * 3)
            link(a.activation(pp["dt"][:, :], pp["ldt"][:, :], ACT.Exp))
            a.activation(pp["t1"][:, :], pp["dt"][:, :], ACT.Copy).then_inc(prep_act, 1)
            act.wait_ge(prep_dve, 1)
            link(a.activation(pp["mag"][:, :], pp["num"][:, :], ACT.Exp))
            a.activation(mag8[:, :], pp["num"][:, :], ACT.Exp, scale=float(L)).then_inc(prep_act, 1)
            a.activation(pp["sin"][:, :], pp["red"][:, :], ACT.Sin).then_inc(prep_act, 1)
            a.activation(pp["cos"][:, :], pp["red2"][:, :], ACT.Sin).then_inc(prep_act, 1)
            act.wait_ge(prep_dve, 3)
            a.activation(spt[1][:, :], spt[0][:, :], ACT.Exp, scale=-1.0).then_inc(prep_act, 1)
            split_hi(0)
            split_hi(1)
            norm(0)
            mixer(0)
            norm(1)
            for l in range(LAYERS):
                if l:
                    act.dma_start(hs_d[:, DK - 1:DK, :], hs[:, DK - 1:DK, :]).then_inc(hs_saved, 16)
                    norm(2)
                    mixer(1)
                    split_hi(ff_u[1] + 2)
                    norm(3)
                    continue
                silu_table()
                with act.Fori(0, ff_n[l] - 1) as e:
                    expert(l, ff_u[l], e, e + ff_e0[l])
                    down(ff_u[l], e, False)
                e = ff_n[l] - 1
                expert(l, ff_u[l], e, e + ff_e0[l])
                down(ff_u[l], e, True)

            act.wait_ge(mg_ready, 2 * DK)
            for t in range(TB):
                act.wait_ge(tok_done, t + 1)
                a.activation(hs_tok[:, t, :].rearrange("p (b c) -> p b c", b=2),
                             side[0:TOK, 2 - t % 2 * 2:4 - t % 2 * 2, :], ACT.Copy).then_inc(hs_tok_ready, 1)
            act.wait_ge(lg_done, 1)
            a.activation(halves(lgt[0:EXPERTS, :]), acc[0:EXPERTS, 0, :, 0:TH], ACT.Copy).then_inc(lgt_ready, 1)
            for t in range(TB):
                if t == 4:
                    act.wait_ge(d_ready, 1)
                    a.activation(ex[0:TOK, :], v2[0:TOK, :], ACT.Exp).then_inc(ex_ready, 1)
                act.wait_ge(tok_done, TB + t + 1)
                a.activation(hn_tok[:, t, :].rearrange("p (b c) -> p b c", b=2),
                             side[0:TOK, 2 - t % 2 * 2:4 - t % 2 * 2, :], ACT.Copy).then_inc(hn_tok_ready, 1)
            for c in range(2):
                a.nop().then_inc(y_stored[c], 16)

            def gather_hi(b, c):
                act.wait_ge(xt_read, b + 1)
                a.activation(xg[:, 2 * c:2 * c + 2, 0, :], side[:, c, 0:2 * S].rearrange("p (m s) -> p m s", m=2),
                             ACT.Copy).then_inc(xgh_ready, 1)

            def copy_half(out, a, bank):
                nc.scalar.activation(out, acc[:, a, bank, S:2 * S], ACT.Copy).then_inc(half_ready[a], 1)

            def moe_block(b, nxt, ahead):
                more, u0 = b * (U_FF // RING), ff_u[1]

                def upper(i):
                    act.wait_ge(fx_ready, b * FT + (i + 1))
                    a.activation(fg2[:, i, 0, :], fx[:, i % SLOT3, :], ACT.Copy).then_inc(fgh_ready, 1)

                for i in range(FT):
                    split_hi(u0 + 2 * i + 3, more)
                    arrived(u0 + 2 * i, more)
                    copy_half(gs[:, i % SLOT3, :], 0, i % 2)
                    if i:
                        upper(i - 1)
                    split_hi(u0 + 2 * i + 4, more)
                    arrived(u0 + 2 * i + 1, more)
                    copy_half(us[:, i % SLOT3, :], 1, i % 2)
                    act.wait_ge(acc_free[0], b * ACC_FF + (i + ff_acc[1] + 1))
                    a.activation(gx[:, i % SLOT3, :], gs[:, i % SLOT3, :], ACT.Silu).then_inc(gx_ready, 1)
                upper(FT - 1)
                for j in range(FT):
                    last = j == FT - 1
                    if not last and (ahead or j < FT - 3):
                        split_hi(u0 + 2 * FT + j + 3, more)
                    for m in moe_tiles_at(j):
                        arrived(u0 + 2 * FT + j, more)
                        copy_half(y_t[:, m, :], m % 2, m // 2 % 2)
                    if last and ahead:
                        split_hi(u0 + 2 * FT + j + 3, more)
                    if j in (2, 3, 4, 5) and nxt:
                        gather_hi(b + 1, j - 2)
                    if j in (7, FT - 1):
                        rows_back(b, 0 if j == 7 else 1)

            def rows_back(b, c):
                act.wait_ge(y_tr, 2 * b + c + 1)
                cs = slice(c * D // 2, (c + 1) * D // 2)
                act.wait_ge(y_stored[c], b * 16 + 16)
                a.activation(ytok[:, :, cs], side[0:SH, 2 * c:2 * c + 2, :], ACT.Copy).then_inc(ytok_ready, 1)
                act.wait_ge(ytok_ready, 2 * b + (c + 1))
                act.dma_start(yg_d[bass.ds(b * S, S), cs].rearrange("(h p) c -> p h c", h=2),
                              ytok[:, :, cs]).then_inc(y_stored[c], 16)

            silu_table()
            for c in range(4):
                gather_hi(0, c)
            with act.Fori(0, EXPERTS - 1) as b:
                moe_block(b, True, True)
            moe_block(EXPERTS - 1, False, False)
            act.wait_ge(tab_ready2, 1)
            n_extra = act.value_load(tab[0:1, 0:1], min_val=0, max_val=EXTRA)
            with act.If(n_extra > 0):
                with act.Fori(0, n_extra) as i:
                    b = i + EXPERTS
                    for j in range(3):
                        split_hi(ff_u[1] + j, b * (U_FF // RING))
                    for c in range(4):
                        gather_hi(b, c)
                    moe_block(b, False, False)
            for t in range(TB):
                act.wait_ge(sum_ready, t + 1)
                a.activation(sqt[:, :], hs_tok[:, t, :], ACT.Square, accum_out=ssq[0:TOK, t:t + 1]).then_inc(sq2_ready, 1)
                act.wait_ge(sq2_ready, t + 1)
                a.activation(ssq[0:TOK, t:t + 1], ssq[0:TOK, t:t + 1], ACT.Sqrt, scale=1.0 / D, bias=EPS)\
                    .then_inc(rms2_ready, 1)

        @block.vector
        def _(dve):
            v = nc.vector
            chain = [0]

            def link(ins):
                chain[0] += 1
                ins.then_inc(dve_chain, 1)
                dve.wait_ge(dve_chain, chain[0])

            def tt(out, a, b, op):
                return v.tensor_tensor(out, a, b, op)

            def split_lo(u, more=0):
                if isinstance(u, int) and isinstance(more, int) and u + RING * more >= UNITS:
                    return
                s, n = use(u, more)
                for h, cs in HALVES:
                    dve.wait_ge(hi_ready[s], n * 2 + (h + 1))
                    tt(wl[s][:, cs], raw[s][:, cs], wh[s][:, cs].bitcast(F32), ALU.subtract).then_inc(lo_ready[s], 1)

            def arrived(u, more=0):
                s, n = use(u, more)
                dve.wait_ge(unit_done[s], n + 1)

            def norm(i):
                name, layer = (("mix_norm", 0), ("ffn_norm", 0), ("mix_norm", 1), ("ffn_norm", 1))[i]
                dve.wait_ge(rms_ready, i + 1)
                link(v.reciprocal(rs[:, :], rs[:, :]))

                def lower(m):
                    dve.wait_ge(xh_ready, xh_at_norm(i) + m + 1)
                    tt(xl[:, m, :], hn[:, m, :], xh[:, m, :].bitcast(F32), ALU.subtract).then_inc(xl_ready, 1)

                for m in range(DK):
                    g = col(name, layer, m)
                    v.scalar_tensor_tensor(out=hn[:, m, :], in0=hs[:, m, :], scalar=g, in1=rs[:, :],
                                           op0=ALU.mult, op1=ALU.mult).then_inc(hn_ready, 1)
                    if m and i < 3:
                        lower(m - 1)
                if i < 3:
                    lower(DK - 1)

            def conv(l, m):
                n = l * MT + m
                w = lambda k: col("conv_w", l, 4 * k + m)
                if n == 0:
                    dve.wait_ge(c_ready, 1)
                dve.wait_ge(acc_free[0], mix_acc[l] + 2 + m + 1)
                link(v.tensor_scalar(xc[:, m, :], xpad[:, 0:T], w(0), col("conv_b", l, m), ALU.mult, ALU.add))
                for k in range(1, 4):
                    last = v.scalar_tensor_tensor(out=xc[:, m, :], in0=xpad[:, k:k + T], scalar=w(k),
                                                  in1=xc[:, m, :], op0=ALU.mult, op1=ALU.add)
                    if k < 3:
                        link(last)
                last.then_inc(xc_ready, 1)

            def lru_pair(l, q):
                n = l * 2 + q
                dve.wait_ge(lru_a, 2 * n + 2)
                dve.wait_ge(xc_ready, l * MT + 2 * q + 2)
                pair = slice(2 * q, 2 * q + 2)
                link(tt(ii[:, :, :], ii[:, :, :], xc[:, pair, :], ALU.mult))
                link(tt(xc[:, pair, :], ra[:, :, :], ra[:, :, :], ALU.mult))
                v.scalar_tensor_tensor(out=th[:, :, :].rearrange("p a b -> p (a b)"),
                                       in0=xc[:, pair, :].rearrange("p a b -> p (a b)"), scalar=1.0,
                                       in1=th[:, :, :].rearrange("p a b -> p (a b)"),
                                       op0=ALU.add, op1=ALU.mult).then_inc(lru_m, 1)

            def lru_scan(l, q):
                n = l * 2 + q
                dve.wait_ge(lru_r, n + 1)
                pair = slice(2 * q, 2 * q + 2)
                link(tt(ii[:, :, :], ii[:, :, :], th[:, :, :], ALU.mult))
                v.tensor_tensor_scan(th[:, 0, :], ra[:, 0, :], ii[:, 0, :], 0.0, ALU.mult, ALU.add)
                link(v.tensor_tensor_scan(th[:, 1, :], ra[:, 1, :], ii[:, 1, :], 0.0, ALU.mult, ALU.add))
                k = 4 + 2 * (2 * q + 1) + 1
                dve.wait_ge(acc_free[1], mix_acc[l] + k // 2 + 1)
                for i in range(2):
                    tt(gg[:, 2 * q + i, :], gg[:, 2 * q + i, :], th[:, i, :], ALU.mult).then_inc(yb_ready, 1)

            def lru_out(l, q):
                for t in (2 * q, 2 * q + 1):
                    dve.wait_ge(ybh_ready, l * MT + t + 1)
                    tt(ybl[:, t, :], gg[:, t, :], ybh[:, t, :].bitcast(F32), ALU.subtract).then_inc(ybl_ready, 1)

            def mixer(l, setup=()):
                u0, a0 = mix_u[l], mix_acc[l]
                v.memset(cr[:, :, 0:1], 0.0)
                link(v.memset(sr[:, :, 0:1], 0.0))
                for k in range(U_IN):
                    split_lo(u0 + k + 2)
                    if k < len(setup):
                        setup[k]()
                    b, part = slot_of(k)
                    if b is None:
                        continue
                    n = l * NB + b
                    if part == 0:
                        dve.wait_ge(p1_done, n + 1)
                        for i in range(GB):
                            at = COLS["s5_d"][0] + l * GROUPS + b * GB + i
                            last = v.scalar_tensor_tensor(out=m3[:, i, :], in0=ident[:, 0:P], scalar=cols[:, at:at + 1],
                                                          in1=side[:, 1, i * P:(i + 1) * P], op0=ALU.mult, op1=ALU.add)
                        last.then_inc(m_dve, 1)
                        dve.wait_ge(c_ready, n + 1)
                        if n:
                            dve.wait_ge(p3_done, n)
                        gs = slice(l * GROUPS + b * GB, l * GROUPS + (b + 1) * GB)
                        w4 = [P, GB, L, GC]
                        ab = lambda x: x[:, 1:L + 1, gs].rearrange("p j g -> p g j").unsqueeze(3).to_broadcast(w4)
                        cb = lambda x: x[:, :, :].unsqueeze(2).to_broadcast(w4)
                        q4 = lambda x: x[:, :, :].rearrange("p g (j h) -> p g j h", h=GC)
                        d4 = dt1[:, :].rearrange("p (g j h) -> p g j h", g=GB, h=GC)
                        tt(d4, ab(apr), cb(c1), ALU.mult)
                        link(tt(q4(m2), ab(api), cb(c2), ALU.mult))
                        link(tt(q4(m2), q4(m2), d4, ALU.add))
                        tt(d4, ab(apr), cb(c2), ALU.mult)
                        link(tt(q4(m2y), ab(api), cb(c1), ALU.mult))
                        tt(q4(m2y), d4, q4(m2y), ALU.subtract).then_inc(m2_ready, 1)
                        if b in (2, 4):
                            lru_pair(l, b // 2 - 1)
                    elif part == 1:
                        dve.wait_ge(p2_done, n + 1)
                        dve.wait_ge(tab_ready, n + 1)
                        w3 = lambda bank: side[:, bank, 0:GB * NC].rearrange("p (g c) -> p g c", g=GB)
                        tt(rot[:, :, :], w3(2), cosT[:, :, :], ALU.mult)
                        link(tt(rot2[:, :, :], w3(3), sinT[:, :, :], ALU.mult))
                        link(tt(rot[:, :, :], rot[:, :, :], rot2[:, :, :], ALU.add))
                        flat = lambda x: x[:, :, :].rearrange("p g c -> p (g c)")
                        link(v.tensor_tensor_scan(flat(turned), flat(decay), flat(rot), 0.0, ALU.mult, ALU.add))
                        tt(cr[:, :, 1:NC], turned[:, :, 0:NC - 1], cosT[:, :, 0:NC - 1], ALU.mult)
                        tt(sr[:, :, 1:NC], turned[:, :, 0:NC - 1], sinT[:, :, 0:NC - 1], ALU.mult).then_inc(rot_ready, 1)
                        if b in (2, 4):
                            lru_scan(l, b // 2 - 1)
                            lru_out(l, b // 2 - 1)
                    kind, m = KIND[k]
                    if kind == "x":
                        conv(l, m)
                for m in range(MT):
                    dve.wait_ge(y1h_ready, l * MT + m + 1)
                    tt(chunked(y1l[:, m, :]), perm(yt[:, m, :, :]), chunked(y1h[:, m, :].bitcast(F32)),
                       ALU.subtract).then_inc(y1l_ready, 1)
                a1 = a0 + U_IN // 2
                for g in range(U_GLU):
                    split_lo(u0 + U_IN + g + 2)
                    for i in range(2):
                        m = 2 * g + i
                        dve.wait_ge(acc_free[i], a1 + g + 1)
                        if m >= 2:
                            dve.wait_ge(y2l_ready, l * MT + m - 1)
                        tt(chunked(ft[:, i, :]), chunked(gt[:, i, :]), perm(yt[:, m, :, :]), ALU.mult).then_inc(y2_ready, 1)
                    for i in range(2):
                        m = 2 * g + i
                        dve.wait_ge(y2h_ready, l * MT + m + 1)
                        tt(y2l[:, m, :], ft[:, i, :], y2h[:, m, :].bitcast(F32), ALU.subtract).then_inc(y2l_ready, 1)
                for m in range(DK):
                    u = u0 + U_IN + U_GLU + m
                    split_lo(u + 2)
                    arrived(u)
                    if m == 0:
                        dve.wait_ge(acc_free[0], a0 + 14)
                        dve.wait_ge(acc_free[1], a0 + 14)
                        dve.wait_ge(y2l_ready, (l + 1) * MT)
                    else:
                        dve.wait_ge(xl_ready, xh_at_mix(l) + m)
                    freed, n = (side_free, l * DK // 2) if m % 2 else (acc_free, a0 + 16)
                    for i in range(2):
                        tt(halves(ft[:, i, :]), merge_sums(m)[i][:, :, 0:TH], halves(gates[:, i * DK + m, :]), ALU.mult)\
                            .then_inc(freed[i], 1)
                    for i in range(2):
                        dve.wait_ge(freed[i], n + m // 2 + 1)
                    tt(ft[:, 0, :], ft[:, 0, :], ft[:, 1, :], ALU.add).then_inc(mg_ready, 1)
                    dve.wait_ge(xh_ready, xh_at_mix(l) + m + 1)
                    tt(xl[:, m, :], ft[:, 0, :], xh[:, m, :].bitcast(F32), ALU.subtract).then_inc(xl_ready, 1)
                for m in range(DK):
                    u = u0 + U_MIX - DK + m
                    split_lo(u + 2)
                    arrived(u)
                    dve.wait_ge(hs_back, 16 * DK * (l + 1))
                    v.tensor_tensor(halves(hs[:, m, :]), halves(hs[:, m, :]), acc[:, m % 2, :, 0:TH],
                                    ALU.add).then_inc(hs_ready, 1)
                    dve.wait_ge(hs_ready, hs_at_norm[2 * l + 1] - DK + m + 1)
                    v.nop().then_inc(acc_free[m % 2], 1)

            def expert(l, u0, e, e_all):
                with dve.Fori(0, 2 * FT // STEP) as it:
                    more = e * (U_FF // RING) + it * (STEP // RING)
                    for i in range(STEP // 2):
                        m = it * (STEP // 2) + i
                        u = u0 + 2 * i
                        split_lo(u + 2, more)
                        split_lo(u + 3, more)
                        arrived(u + 1, more)
                        uses = e * ACC_FF + it * (STEP // 2) + (i + ff_acc[l] + 1)
                        dve.wait_ge(acc_free[0], uses)
                        tt(halves(ft[:, 0, :]), halves(gt[:, 0, :]), acc[:, 1, :, 0:TH], ALU.mult).then_inc(acc_free[1], 1)
                        dve.wait_ge(acc_free[1], uses)
                        v.nop().then_inc(f_ready, 1)
                        dve.wait_ge(fh_ready, e_all * FT + m + 1)
                        tt(fl[:, m, :], ft[:, 0, :], fh[:, m, :].bitcast(F32), ALU.subtract).then_inc(fl_ready, 1)
                        dve.wait_ge(fl_ready, e_all * FT + m + 1)

            def down(l, u0, e, e_all, last):
                more = e * (U_FF // RING)
                for j in range(FT):
                    u = u0 + 2 * FT + j
                    if not (last and j >= FT - 2):
                        split_lo(u + 2, more)
                    if j % 3 == 0:
                        continue
                    m = 2 * (j // 3) + (j % 3 - 1)
                    arrived(u, more)
                    seen = hs_at_norm[2 * l + 1] + e * DK
                    if m == 0:
                        dve.wait_ge(hs_ready, seen)
                    v.tensor_tensor(halves(hs[:, m, :]), halves(hs[:, m, :]), acc[:, m % 2, :, 0:TH],
                                    ALU.add).then_inc(hs_ready, 1)
                    dve.wait_ge(hs_ready, seen + m + 1)
                    v.nop().then_inc(acc_free[m % 2], 1)

            v.memset(sgn[0:GS, 0:1], -1.0)
            v.memset(sgn[GS:P, 0:1], 1.0)
            v.memset(sgn[0:GS, 1:2], 1.0)
            link(v.memset(sgn[GS:P, 1:2], -1.0))
            dve.wait_ge(small_landed, 16)
            dve.wait_ge(prep_act, 1)
            ang, kk, red, red2 = (pp[n][:, :] for n in ("ang", "k", "red", "red2"))
            ROUND = 12582912.0
            C1, C2, C3 = 6.28125, 0.0019350051879882812, 3.019916e-07
            link(tt(ang, pp["li"][:, :], pp["dt"][:, :], ALU.mult))
            link(v.tensor_scalar(kk, ang, 0.15915494309189535, ROUND, ALU.mult, ALU.add))
            link(v.tensor_scalar(kk, kk, ROUND, 0.0, ALU.subtract, ALU.add))
            for c in (C1, C2, C3):
                link(v.scalar_tensor_tensor(out=ang, in0=kk, scalar=-c, in1=ang, op0=ALU.mult, op1=ALU.add))
            link(v.tensor_scalar(red, ang, 3.1415925, -3.1415925, ALU.min, ALU.max))
            link(v.tensor_scalar(kk, ang, 1.5707963267948966, -6.283185307179586, ALU.is_gt, ALU.mult))
            link(v.scalar_tensor_tensor(out=red2, in0=ang, scalar=1.5707963267948966, in1=kk, op0=ALU.add, op1=ALU.add))
            link(v.tensor_scalar(red2, red2, 3.1415925, -3.1415925, ALU.min, ALU.max))
            tt(pp["num"][:, :], pp["lr"][:, :], pp["dt"][:, :], ALU.mult).then_inc(prep_dve, 1)
            link(tt(pp["den"][:, :], pp["lr"][:, :], pp["lr"][:, :], ALU.mult))
            link(tt(pp["t3"][:, :], pp["li"][:, :], pp["li"][:, :], ALU.mult))
            link(tt(pp["den"][:, :], pp["den"][:, :], pp["t3"][:, :], ALU.add))
            v.reciprocal(pp["rden"][:, :], pp["den"][:, :]).then_inc(prep_dve, 1)
            at, n = COLS["lam"]
            lam = cols[:, at:at + LAYERS * n]
            s0, s1, s2, s3 = (x[:, :] for x in spt)
            link(v.tensor_scalar(s2, lam, -1.0, 0.0, ALU.mult, ALU.add))
            tt(s0, lam, s2, ALU.max).then_inc(prep_dve, 1)
            link(v.tensor_scalar(s3, s2, 0.0, 0.0, ALU.max, ALU.add))
            split_lo(0)
            split_lo(1)
            def turns():
                def link_square(outr, outi, ar, ai):
                    tt(t1, ar, ar, ALU.mult)
                    tt(t2, ai, ai, ALU.mult)
                    link(tt(t3, ar, ai, ALU.mult))
                    tt(outr, t1, t2, ALU.subtract)
                    link(tt(outi, t3, t3, ALU.add))

                t1, t2, t3 = pp["ang"][:, :], pp["k"][:, :], pp["t3"][:, :]
                ur, ui = pp["cos"][:, :], pp["sin"][:, :]
                dve.wait_ge(prep_act, 4)
                n = 1
                while n < L:
                    link_square(sqr[:, 0, :], sqi[:, 0, :], ur, ui)
                    ur, ui = sqr[:, 0, :], sqi[:, 0, :]
                    n *= 2
                tt(t1, ur, ur, ALU.mult)
                link(tt(t2, ui, ui, ALU.mult))
                link(tt(t1, t1, t2, ALU.add))
                link(v.tensor_scalar(t1, t1, -0.5, 1.5, ALU.mult, ALU.add))
                tt(ur, ur, t1, ALU.mult)
                link(tt(ui, ui, t1, ALU.mult))
                for k in range(1, 7):
                    link_square(sqr[:, k, :], sqi[:, k, :], sqr[:, k - 1, :], sqi[:, k - 1, :])
                v.nop().then_inc(turn_ready, 1)

            def softplus():
                dve.wait_ge(prep_act, 5)
                link(v.tensor_scalar(s0, s1, 2.0, 0.0, ALU.add, ALU.add))
                link(v.reciprocal(s0, s0))
                link(tt(s1, s1, s0, ALU.mult))
                link(tt(s0, s1, s1, ALU.mult))
                link(v.tensor_scalar(s2, s0, 2.0 / 17, 2.0 / 15, ALU.mult, ALU.add))
                for d in (13, 11, 9, 7, 5, 3, 1):
                    link(tt(s2, s2, s0, ALU.mult))
                    link(v.tensor_scalar(s2, s2, 1.0, 2.0 / d, ALU.mult, ALU.add))
                link(tt(s2, s2, s1, ALU.mult))
                link(tt(s2, s2, s3, ALU.add))
                link(v.tensor_scalar(sp8[:, :], s2, LRU_C, 0.0, ALU.mult, ALU.add))
                v.tensor_scalar(sp8n[:, :], s2, -LRU_C, 0.0, ALU.mult, ALU.add).then_inc(prep_dve, 1)

            norm(0)
            mixer(0, (turns, softplus))
            norm(1)
            for l in range(LAYERS):
                if l:
                    norm(2)
                    mixer(1)
                    split_lo(ff_u[1] + 2)
                    norm(3)
                    k = slice(0, TOK)
                    dve.wait_ge(lgt_done, 1)
                    dve.wait_ge(const_ready, 4)
                    w3, w4 = [TOK, TB, EXPERTS], [TOK, TB, EXPERTS, EXPERTS]
                    link(tt(lg[k, :, :], acc[k, 1, 0, 0:TB * EXPERTS].rearrange("p (t e) -> p t e", t=TB),
                            rbs[k, :].unsqueeze(1).to_broadcast(w3), ALU.add))
                    mine = lg[k, :, :].unsqueeze(3).to_broadcast(w4)
                    other = lg[k, :, :].unsqueeze(2).to_broadcast(w4)
                    tt(cmp1[k], other, mine, ALU.is_gt)
                    link(tt(cmp2[k], other, mine, ALU.is_equal))
                    link(tt(cmp2[k], cmp2[k], tri[k].unsqueeze(1).to_broadcast(w4), ALU.mult))
                    link(tt(cmp1[k], cmp1[k], cmp2[k], ALU.add))
                    link(v.reduce_sum(rank[k], cmp1[k], AX_X))
                    v.tensor_scalar(sel1[k], rank[k], 0.0, 0.0, ALU.is_equal, ALU.add)
                    link(v.tensor_scalar(sel2[k], rank[k], 1.0, 0.0, ALU.is_equal, ALU.add))
                    tt(mask[k], sel1[k], sel2[k], ALU.add).then_inc(mask_ready, 1)
                    v.reduce_max(v1[k], lg[k], AX_X)
                    link(v.tensor_scalar(gtmp[k], rank[k], 0.0, -1e30, ALU.is_equal, ALU.mult))
                    link(tt(gtmp[k], gtmp[k], lg[k], ALU.add))
                    link(v.reduce_max(v2[k], gtmp[k], AX_X))
                    tt(v2[k], v2[k], v1[k], ALU.subtract).then_inc(d_ready, 1)
                    continue
                with dve.Fori(0, ff_n[l] - 1) as e:
                    expert(l, ff_u[l], e, e + ff_e0[l])
                    down(l, ff_u[l], e, e + ff_e0[l], False)
                e = ff_n[l] - 1
                expert(l, ff_u[l], e, e + ff_e0[l])
                down(l, ff_u[l], e, e + ff_e0[l], False)

            w8, wi = [TOK, TB, EXPERTS], [TOK, EXTRA, EXPERTS]
            v.memset(oneE[k], 1.0)
            v.memset(oneI[k], 1.0)
            link(v.memset(off[k, 0, :], 0.0))
            v.tensor_tensor_scan(ev[k], oneE[k], oneE[k], -1.0, ALU.mult, ALU.add)
            link(v.tensor_tensor_scan(iv[k], oneI[k], oneI[k], -1.0, ALU.mult, ALU.add))
            dve.wait_ge(pos_done, 1)
            counts = acc[k, 1, 1, 0:TB * EXPERTS].rearrange("p (t e) -> p t e", t=TB)
            for t in range(TB):
                link(tt(off[k, t + 1, :], off[k, t, :], counts[:, t, :], ALU.add))
            before = acc[k, 1, 0, 0:TB * EXPERTS].rearrange("p (t e) -> p t e", t=TB)
            link(tt(pos[k], before, off[k, 0:TB, :], ALU.add))

            def steps(out, tmp, x):
                link(v.tensor_scalar(out, x, float(S), 0.0, ALU.is_ge, ALU.add))
                for q in range(2, QMAX + 1):
                    link(v.tensor_scalar(tmp, x, float(q * S), 0.0, ALU.is_ge, ALU.add))
                    link(tt(out, out, tmp, ALU.add))

            link(v.tensor_scalar(xtmp[k], off[k, TB, :], 1.0, 0.0, ALU.subtract, ALU.add))
            steps(extra[k], ebase[k], xtmp[k])
            link(v.tensor_tensor_scan(incl[k], oneE[k], extra[k], 0.0, ALU.mult, ALU.add))
            link(tt(ebase[k], incl[k], extra[k], ALU.subtract))
            steps(qq[k], slot[k], pos[k])
            link(v.tensor_scalar(big[k], pos[k], float(S), 0.0, ALU.is_ge, ALU.add))
            link(tt(xtmp[k], ebase[k], ev[k], ALU.subtract))
            link(v.tensor_scalar(xtmp[k], xtmp[k], float(EXPERTS - 1), 0.0, ALU.add, ALU.add))
            link(tt(slot[k], qq[k], xtmp[k].unsqueeze(1).to_broadcast(w8), ALU.add))
            link(tt(slot[k], slot[k], big[k], ALU.mult))
            link(tt(slot[k], slot[k], ev[k].unsqueeze(1).to_broadcast(w8), ALU.add))
            link(tt(slot[k], slot[k], qq[k], ALU.subtract))
            link(v.scalar_tensor_tensor(out=slot[k].rearrange("p t e -> p (t e)"),
                                        in0=slot[k].rearrange("p t e -> p (t e)"), scalar=float(S),
                                        in1=pos[k].rearrange("p t e -> p (t e)"), op0=ALU.mult, op1=ALU.add))
            tt(qq[k], slot[k], sel1[k], ALU.mult)
            link(tt(big[k], slot[k], sel2[k], ALU.mult))
            v.reduce_sum(sf[k, 0, :], qq[k], AX_X)
            link(v.reduce_sum(sf[k, 1, :], big[k], AX_X))
            v.tensor_copy(idx[k], sf[k]).then_inc(slot_ready, 1)
            ib = iv[k].unsqueeze(2).to_broadcast(wi)
            tt(in1[k], ib, ebase[k].unsqueeze(1).to_broadcast(wi), ALU.is_ge)
            link(tt(in2[k], ib, incl[k].unsqueeze(1).to_broadcast(wi), ALU.is_lt))
            link(tt(in1[k], in1[k], in2[k], ALU.mult))
            link(tt(in1[k], in1[k], ev[k].unsqueeze(1).to_broadcast(wi), ALU.mult))
            v.tensor_copy(tabf[k, 0:1], incl[k, EXPERTS - 1:EXPERTS])
            link(v.reduce_sum(tabf[k, 1:EXTRA + 1], in1[k], AX_X))
            wider = tabf[k, EXTRA + 1:EXTRA + 1 + EXPERTS]
            link(v.tensor_scalar(wider, off[k, TB, :], float(WIDTHS[0]), 0.0, ALU.is_gt, ALU.add))
            for n in WIDTHS[1:-1]:
                link(v.tensor_scalar(xtmp[k], off[k, TB, :], float(n), 0.0, ALU.is_gt, ALU.add))
                link(tt(wider, wider, xtmp[k], ALU.add))
            v.tensor_copy(tab[k], tabf[k]).then_inc(tab_ready2, 1)
            dve.wait_ge(ex_ready, 1)
            link(v.tensor_scalar(g1[k], ex[k], 1.0, 0.0, ALU.add, ALU.add))
            link(v.reciprocal(g1[k], g1[k]))
            link(tt(g2[k], g1[k], ex[k], ALU.mult))
            v.memset(acc[:, :, :, :], 0.0).then_inc(acc_set, 1)

            def gather_lo(b, c):
                dve.wait_ge(xgh_ready, b * 4 + c + 1)
                tt(xg[:, 2 * c:2 * c + 2, 1, :], side[:, c, 0:2 * S].rearrange("p (m s) -> p m s", m=2),
                   xg[:, 2 * c:2 * c + 2, 0, :].bitcast(F32), ALU.subtract).then_inc(xgl_ready, 1)

            def add_halves(out, a, bank, b, n):
                dve.wait_ge(half_ready[a], b * ACC_FF + (n + 1))
                tt(out, out, acc[:, a, bank, 0:S], ALU.add).then_inc(acc_free[a], 1)

            def moe_block(b, nxt, ahead):
                more, u0 = b * (U_FF // RING), ff_u[1]
                for m in range(FT):
                    x = m % SLOT3
                    split_lo(u0 + 2 * m + 3, more)
                    add_halves(gs[:, x, :], 0, m % 2, b, m)
                    split_lo(u0 + 2 * m + 4, more)
                    add_halves(us[:, x, :], 1, m % 2, b, m)
                    dve.wait_ge(acc_free[1], b * ACC_FF + (m + ff_acc[1] + 1))
                    dve.wait_ge(gx_ready, b * FT + (m + 1))
                    if m >= SLOT3:
                        dve.wait_ge(fgl_ready, b * FT + (m - SLOT3 + 1))
                    tt(fx[:, x, :], gx[:, x, :], us[:, x, :], ALU.mult).then_inc(fx_ready, 1)
                for j in range(FT):
                    last = j == FT - 1
                    if not last and (ahead or j < FT - 3):
                        split_lo(u0 + 2 * FT + j + 3, more)
                    for m in moe_tiles_at(j):
                        add_halves(y_t[:, m, :], m % 2, m // 2 % 2, b, FT + m // 2)
                    if last and ahead:
                        split_lo(u0 + 2 * FT + j + 3, more)
                    if j in (2, 3, 4, 5) and nxt:
                        gather_lo(b + 1, j - 2)

            for c in range(4):
                gather_lo(0, c)
            with dve.Fori(0, EXPERTS - 1) as b:
                moe_block(b, True, True)
            moe_block(EXPERTS - 1, False, False)
            dve.wait_ge(tab_ready2, 1)
            n_extra = dve.value_load(tab[0:1, 0:1], min_val=0, max_val=EXTRA)
            with dve.If(n_extra > 0):
                with dve.Fori(0, n_extra) as i:
                    b = i + EXPERTS
                    for j in range(3):
                        split_lo(ff_u[1] + j, b * (U_FF // RING))
                    for c in range(4):
                        gather_lo(b, c)
                    moe_block(b, False, False)
            dve.wait_ge(gm_landed, 16)

            def normed(t):
                dve.wait_ge(rms2_ready, t + 1)
                link(v.reciprocal(ssq[k, t:t + 1], ssq[k, t:t + 1]))
                if t >= 2:
                    dve.wait_ge(out_done[t % 2], 16 * (t // 2))
                v.scalar_tensor_tensor(out=ot[:, t % 2, :], in0=hs_tok[:, t, :], scalar=ssq[k, t:t + 1],
                                       in1=gmb[:, :], op0=ALU.mult, op1=ALU.mult).then_inc(ot_ready, 1)

            for t in range(TB):
                dve.wait_ge(ya_in[t % 2], 32 * (t // 2 + 1))
                link(v.scalar_tensor_tensor(out=hs_tok[:, t, :], in0=ya[:, t % 2, :], scalar=g1[k, t:t + 1],
                                            in1=hs_tok[:, t, :], op0=ALU.mult, op1=ALU.add))
                v.scalar_tensor_tensor(out=hs_tok[:, t, :], in0=yb[:, t % 2, :], scalar=g2[k, t:t + 1],
                                       in1=hs_tok[:, t, :], op0=ALU.mult, op1=ALU.add).then_inc(sum_ready, 1)
                if t:
                    normed(t - 1)
            normed(TB - 1)

        @block.tensor
        def _(pe):
            mm = nc.tensor.matmul

            def free(s, n):
                if not isinstance(n, int) or n > 0:
                    pe.wait_ge(acc_free[s], n)

            def unit(u, jobs, more=0, before=None, sums=None):
                s, n = use(u, more)
                pe.wait_ge(lo_ready[s], n * 2 + 2)
                for n, (k, a, hi, lo, first, last) in enumerate(jobs):
                    if before and n in before:
                        pe.wait_ge(*before[n])
                    w_hi, w_lo = (x[s][:, k * P:(k + 1) * P] for x in (wh, wl))
                    parts = [(w_hi, hi), (w_hi, lo), (w_lo, hi)]
                    for i, (w, x) in enumerate(parts):
                        for b in range(2):
                            out = acc[:, a, b, 0:TH] if sums is None else sums[a][:, b, 0:TH]
                            ins = mm(out, w, x[:, b * TH:(b + 1) * TH],
                                     start=first and i == 0, stop=last and i == 2)
                ins.then_inc(unit_done[s], 1)

            def add_squares(i, m):
                pe.wait_ge(sq_ready, i * DK + m + 1)
                for b in range(2):
                    ins = mm(side[:, b, 0:TH], ones[:, :], hn[:, m, b * TH:(b + 1) * TH],
                             start=m == 0, stop=m == DK - 1)
                if m == DK - 1:
                    ins.then_inc(ss_ready, 1)

            def norm(i):
                if i == 0:
                    pe.wait_ge(const_ready, 1)
                    for m in range(DK):
                        add_squares(i, m)

            def first_units(u, split):
                slots = [use(u + a) for a in range(2)]
                for s, n in slots:
                    pe.wait_ge(lo_ready[s], n * 2 + 2)
                for k in range(DK):
                    pe.wait_ge(xl_ready, split + k + 1)
                    for a, (s, _) in enumerate(slots):
                        w_hi, w_lo = (w[s][:, k * P:(k + 1) * P] for w in (wh, wl))
                        for i, (w, x) in enumerate(((w_hi, xh), (w_hi, xl), (w_lo, xh))):
                            for b in range(2):
                                ins = mm(acc[:, a, b, 0:TH], w, x[:, k, b * TH:(b + 1) * TH],
                                         start=k == 0 and i == 0, stop=k == DK - 1 and i == 2)
                        if k == DK - 1:
                            ins.then_inc(unit_done[s], 1)

            def gate_mm(l, q):
                t, r = q // 2, q % 2
                pe.wait_ge(xc_ready, l * MT + t + 1)
                pe.wait_ge(wg_landed, 32 * (l + 1))
                if l * 8 + q:
                    pe.wait_ge(ri_ready, l * 8 + q)
                pe.wait_ge(rot_ready, l * NB + q // 2 + 1)
                for hd in range(2):
                    rows = slice(hd * 64, hd * 64 + 64)
                    for b in range(2):
                        ins = mm(side[rows, 2 + b, 0:TH], gw[rows, r, t, :], xc[rows, t, b * TH:(b + 1) * TH],
                                 start=True, stop=True)
                ins.then_inc(gm_done, 1)

            def mixer(l):
                u0, a0 = mix_u[l], mix_acc[l]
                free(0, a0)
                free(1, a0)
                first_units(u0, xl_at_norm(2 * l))
                for k in range(2, U_IN):
                    free(k % 2, a0 + k // 2)
                    unit(u0 + k, [(j, k % 2, xh[:, j, :], xl[:, j, :], j == 0, j == DK - 1) for j in range(DK)])
                    b, part = slot_of(k)
                    if b is None:
                        continue
                    n = l * NB + b
                    if part == 0:
                        pe.wait_ge(const_ready, 2)
                        pe.wait_ge(m1t_ready, n + 1)
                        pe.wait_ge(c_ready, n + 1)
                        if n:
                            pe.wait_ge(ys_ready, n)
                            pe.wait_ge(m_dve, n)
                        if b:
                            pe.wait_ge(ri_ready, l * 8 + min(2 * b - 1, 8))
                        for i in range(GB):
                            ins = mm(side[:, 2, TAPS + i * GC:TAPS + (i + 1) * GC], m1t[:, i, :], c1[:, i, :],
                                     start=True, stop=True)
                        ins.then_inc(taps_done, 1)
                        for i in range(GB):
                            nc.tensor.transpose(side[:, 0, i * P:(i + 1) * P], m1t[:, i, :], ident[:, 0:P])
                        pe.wait_ge(taps_ready, n + 1)
                        for j in range(L):
                            at = (L - 1 - j) * GC
                            out4 = side[:, 1, :].rearrange("p (g j h) -> p g j h", g=GB, h=GC)[:, :, j, :]
                            ins = mm(out4, ident[:, at:at + P], taps[:, :].rearrange("p (g h) -> p g h", g=GB),
                                     start=True, stop=True)
                        ins.then_inc(p1_done, 1)
                        if 1 <= b <= MT:
                            gate_mm(l, 2 * b - 1)
                    elif part == 1:
                        pe.wait_ge(m_act, n + 1)
                        pe.wait_ge(m_dve, n + 1)
                        pe.wait_ge(u_in, 16 * L * (l + 1))
                        if b:
                            pe.wait_ge(ri_ready, l * 8 + min(2 * b, 8))
                        for i in range(GB):
                            c = slice(i * NC, (i + 1) * NC)
                            mm(side[:, 2, c], m1[:, i, :], uu[:, b * GB + i, :], start=True, stop=True)
                            ins = mm(side[:, 3, c], m1y[:, i, :], uu[:, b * GB + i, :], start=True, stop=True)
                        ins.then_inc(p2_done, 1)
                    else:
                        pe.wait_ge(rot_ready, n + 1)
                        pe.wait_ge(m2_ready, n + 1)
                        for i in range(GB):
                            c = slice(i * NC, (i + 1) * NC)
                            mm(side[:, 0, c], m3[:, i, :], uu[:, b * GB + i, :], start=True, stop=False)
                            mm(side[:, 0, c], m2[:, i, :], cr[:, i, :], start=False, stop=False)
                            ins = mm(side[:, 0, c], m2y[:, i, :], sr[:, i, :], start=False, stop=True)
                        ins.then_inc(p3_done, 1)
                        if b < MT:
                            gate_mm(l, 2 * b)
                a1 = a0 + U_IN // 2
                for g in range(U_GLU):
                    free(0, a1 + g)
                    free(1, a1 + g)
                    unit(u0 + U_IN + g, [(4 * i + k, i, y1h[:, k, :], y1l[:, k, :], k == 0, k == MT - 1)
                                         for k in range(MT) for i in range(2)],
                         before={2 * k: (y1l_ready, l * MT + k + 1) for k in range(MT)} if g == 0 else None)
                pe.wait_ge(ybl_ready, (l + 1) * MT)
                for m in range(DK):
                    for i in range(2):
                        if m % 2 == 0:
                            free(i, a0 + 16 + m // 2)
                        elif l or m > 1:
                            pe.wait_ge(side_free[i], l * DK // 2 + m // 2)
                    unit(u0 + U_IN + U_GLU + m,
                         [(MT + k, 1, ybh[:, k, :], ybl[:, k, :], k == 0, k == MT - 1) for k in range(MT)]
                         + [(k, 0, y2h[:, k, :], y2l[:, k, :], k == 0, k == MT - 1) for k in range(MT)],
                         before={MT + k: (y2l_ready, l * MT + k + 1) for k in range(MT)} if m == 0 else None,
                         sums=merge_sums(m))
                for m in range(DK):
                    free(m % 2, a0 + 20 + m // 2)
                    if m == 0:
                        pe.wait_ge(xl_ready, xl_mix_end(l) - 1)
                    unit(u0 + U_MIX - DK + m,
                         [(k, m % 2, xh[:, k, :], xl[:, k, :], k == 0, k == DK - 1) for k in range(DK)],
                         before={DK - 1: (xl_ready, xl_mix_end(l))} if m == 0 else None)
                    if m >= 2:
                        add_squares(2 * l + 1, m - 2)
                add_squares(2 * l + 1, DK - 2)
                add_squares(2 * l + 1, DK - 1)

            def expert(l, u0, e, e_all):
                if e == 0:
                    free(0, ff_acc[l])
                    free(1, ff_acc[l])
                    first_units(u0, xl_at_norm(2 * l + 1))
                    for i in range(2, STEP):
                        free(i % 2, i // 2 + ff_acc[l])
                        unit(u0 + i, [(k, i % 2, xh[:, k, :], xl[:, k, :], k == 0, k == DK - 1) for k in range(DK)])
                with pe.Fori(1 if e == 0 else 0, 2 * FT // STEP) as it:
                    more = e * (U_FF // RING) + it * (STEP // RING)
                    for i in range(STEP):
                        free(i % 2, e * ACC_FF + it * (STEP // 2) + (i // 2 + ff_acc[l]))
                        unit(u0 + i, [(k, i % 2, xh[:, k, :], xl[:, k, :], k == 0, k == DK - 1) for k in range(DK)], more)

            def down(l, u0, e, e_all, last=False):
                more = e * (U_FF // RING)
                for q in range(FT // 3):
                    tiles = [(2 * q + i, k) for i in range(2) for k in range(FT)]
                    for j in range(3):
                        jobs = []
                        for p, (m, k) in enumerate(tiles[8 * j:8 * j + 8]):
                            jobs.append((p, m % 2, fh[:, k, :], fl[:, k, :], k == 0, k == FT - 1))
                        pe.wait_ge(fl_ready, e_all * FT + (8 if q == 0 and j == 0 else FT))
                        for m, k in tiles[8 * j:8 * j + 8]:
                            if k == 0:
                                free(m % 2, e * ACC_FF + (ff_acc[l] + FT + q))
                        unit(u0 + 2 * FT + 3 * q + j, jobs, more)
                        n = 3 * q + j - 2
                        if last and n >= 0 and n % 3:
                            add_squares(2, down_tile(n))
                if last:
                    add_squares(2, DK - 2)
                    add_squares(2, DK - 1)

            norm(0)
            mixer(0)
            norm(1)
            for l in range(LAYERS):
                if l:
                    norm(2)
                    mixer(1)
                    norm(3)
                    def rows_of(src, t, pair):
                        for m in range(DK):
                            ins = nc.tensor.transpose(side[0:TOK, 2 * pair + m // 4, m % 4 * P:(m % 4 + 1) * P],
                                                      src[:, m, t * TOK:(t + 1) * TOK], ident[:, 0:P])
                        ins.then_inc(tok_done, 1)

                    for t in range(TB):
                        if t == 1:
                            pe.wait_ge(rms_ready, 4)
                        if t >= 2:
                            pe.wait_ge(hs_tok_ready, t - 1)
                        rows_of(hs, t, 1 - t % 2)
                    pe.wait_ge(prep_pool, 16 * 2)
                    for m in range(DK):
                        pe.wait_ge(hn_ready, 3 * DK + m + 1)
                        for b in range(2):
                            ins = mm(acc[0:EXPERTS, 0, b, 0:TH], rws[:, m, :], hn[:, m, b * TH:(b + 1) * TH],
                                     start=m == 0, stop=m == DK - 1)
                    ins.then_inc(lg_done, 1)
                    pe.wait_ge(lgt_ready, 1)
                    for t in range(TB):
                        ins = nc.tensor.transpose(acc[0:TOK, 1, 0, t * EXPERTS:(t + 1) * EXPERTS],
                                                  lgt[0:EXPERTS, t * TOK:(t + 1) * TOK], ident[0:EXPERTS, 0:EXPERTS])
                    ins.then_inc(lgt_done, 1)
                    for t in range(TB):
                        pe.wait_ge(*((hn_tok_ready, t - 1) if t >= 2 else (hs_tok_ready, TB - 1 + t)))
                        if t == 2:
                            pe.wait_ge(mask_ready, 1)
                            sel = mask[0:TOK, :, :].rearrange("p t e -> p (t e)")
                            mm(acc[0:TOK, 1, 0, 0:TB * EXPERTS], tris[0:TOK, :], sel, start=True, stop=True)
                            mm(acc[0:TOK, 1, 1, 0:TB * EXPERTS], ones[0:TOK, 0:TOK], sel, start=True, stop=True)\
                                .then_inc(pos_done, 1)
                        rows_of(hn, t, 1 - t % 2)
                    continue
                for e in range(ff_n[l]):
                    expert(l, ff_u[l], e, e + ff_e0[l])
                    down(l, ff_u[l], e, e + ff_e0[l], e == ff_n[l] - 1)

            def slot_unit(u, jobs, more, width):
                s, n = use(u, more)
                pe.wait_ge(lo_ready[s], n * 2 + 2)
                for k, a, bank, x, first, last in jobs:
                    w_hi, w_lo = (w[s][:, k * P:(k + 1) * P] for w in (wh, wl))
                    halves2 = acc[:, a, bank, 0:2 * S].rearrange("p (h s) -> p h s", h=2)
                    mm(halves2[:, :, 0:width], w_hi, x[:, :, 0:width], start=first, stop=False)
                    ins = mm(halves2[:, 0, 0:width], w_lo, x[:, 0, 0:width], start=False, stop=last)
                ins.then_inc(unit_done[s], 1)

            def turn_rows(b):
                pe.wait_ge(xt_landed, b * 16 + 16)
                for m in range(DK):
                    for h in range(2):
                        at = m % 2 * S + h * SH
                        ins = nc.tensor.transpose(side[:, m // 2, at:at + SH], xt[:, h, m * P:(m + 1) * P],
                                                  ident[0:SH, 0:SH])
                ins.then_inc(xt_read, 1)

            def moe_block(b, nxt, n=S):
                more, u0 = b * (U_FF // RING), ff_u[1]

                def free(a, n):
                    pe.wait_ge(acc_free[a], b * ACC_FF + (ff_acc[1] + n - 1))

                with pe.Fori(0, FT // BODY) as it:
                    inner = it * (2 * BODY // RING)
                    for i in range(BODY):
                        if i == 0:
                            pe.wait_ge(xgl_ready, b * 4 + 4)
                        for a in range(2):
                            pe.wait_ge(acc_free[a], b * ACC_FF + it * BODY + (i + ff_acc[1] - 1))
                            slot_unit(u0 + 2 * i + a, [(k, a, i % 2, xg[:, k, :, :], k == 0, k == DK - 1)
                                                       for k in range(DK)], more + inner, n)
                for q in range(FT // 3):
                    tiles = [(m, k) for m, k in moe_down_order() if m // 2 == q]
                    for j in range(3):
                        pe.wait_ge(fgl_ready, b * FT + (8 if q == 0 and j < 2 else FT))
                        here = tiles[8 * j:8 * j + 8]
                        for m, k in here:
                            if k == 0:
                                free(m % 2, FT + q)
                        slot_unit(u0 + 2 * FT + 3 * q + j,
                                  [(p, m % 2, m // 2 % 2, fg2[:, k, :, :], k == 0, k == FT - 1)
                                   for p, (m, k) in enumerate(here)], more, n)
                        if q == 0 and j == 1 and nxt:
                            turn_rows(b + 1)
                        if 3 * q + j in (7, 10, FT - 1):
                            first, end = {7: (0, 4), 10: (4, 6), FT - 1: (6, 8)}[3 * q + j]
                            pe.wait_ge(xgl_ready, b * 4 + (8 if nxt else 4))
                            for i in range(2):
                                pe.wait_ge(acc_free[i], b * ACC_FF + (ff_acc[1] + FT + end // 2))
                            for h in range(2):
                                for m in range(first, end):
                                    ins = nc.tensor.transpose(side[0:SH, 2 * (m // 4) + h, m % 4 * P:(m % 4 + 1) * P],
                                                              y_t[:, m, h * SH:(h + 1) * SH], ident[:, 0:P])
                            if end != 6:
                                ins.then_inc(y_tr, 1)

            turn_rows_first = lambda: (pe.wait_ge(hn_tok_ready, TB), pe.wait_ge(hs_tok_ready, TB), turn_rows(0))
            turn_rows_first()
            pe.wait_ge(tab_ready2, 1)
            pe.wait_ge(acc_set, 1)

            def by_width(b, nxt):
                wider = pe.value_load(tab[0:1, bass.ds(b + (EXTRA + 1), 1)], min_val=0, max_val=len(WIDTHS) - 1)
                for i, n in enumerate(WIDTHS):
                    with pe.If(wider == i):
                        moe_block(b, nxt, n)

            with pe.Fori(0, EXPERTS - 1) as b:
                by_width(b, True)
            by_width(EXPERTS - 1, False)
            n_extra = pe.value_load(tab[0:1, 0:1], min_val=0, max_val=EXTRA)
            with pe.If(n_extra > 0):
                with pe.Fori(0, n_extra) as i:
                    b = i + EXPERTS
                    pe.wait_ge(ytok_ready, b * 2)
                    turn_rows(b)
                    moe_block(b, False)


LRU_WB = 64


def xh_at_norm(i):
    return DK * (0, 2, 3)[i]


def xl_at_norm(i):
    return xh_at_norm(i)


def xh_at_mix(l):
    return DK * (1, 4)[l]


def xl_mix_end(l):
    return xh_at_mix(l) + DK


def moe_down_order():
    order = [(m, k) for m in range(2) for k in range(8)] + [(m, k) for m in range(2) for k in range(8, FT)]
    return order + [(m, k) for m in range(2, DK) for k in range(FT)]


def moe_tiles_at(j):
    done = moe_down_order()[8 * j:8 * j + 8]
    return [m for m, k in done if k == FT - 1]


def down_tile(j):
    return 2 * (j // 3) + (j % 3 - 1)


def layout(inputs):
    import numpy as np

    a = {k: np.asarray(v) for k, v in inputs.items()}
    arrays = {}
    x = np.concatenate([a["meta_tokens"], a["x"][0]], axis=0)
    tiles = lambda v: np.moveaxis(v.reshape(-1, P, *v.shape[1:]), 0, 1)
    arrays["xT"] = tiles(x.T)

    W = np.empty((UNITS, P, UNIT), np.float32)
    at = [0]

    def put(w):
        n = w.shape[0] // 8
        W[at[0]:at[0] + n] = np.moveaxis(w.reshape(n, 8, P, P), 1, 2).reshape(n, P, UNIT)
        at[0] += n

    def cut(w):
        k, m = w.shape
        return w.reshape(k // P, P, m // P, P).transpose(2, 0, 1, 3)

    def ffn(gate, up, down, order=None):
        g, u = cut(gate), cut(up)
        put(np.stack([g, u], axis=1).reshape(-1, P, P))
        d = cut(down)
        put(np.stack([d[m, k] for m, k in order]) if order else d.reshape(-1, P, P))

    for l in range(LAYERS):
        w = cut(a["w_in"][l])
        order = list(range(MT))
        for m in range(MT):
            order += [MT + m, 2 * MT + m]
        order += list(range(3 * MT, U_IN))
        put(w[order].reshape(-1, P, P))
        put(cut(a["s5_w_glu"][l]).reshape(-1, P, P))
        put(np.stack([cut(a["s5_w_proj"][l]), cut(a["lru_w_proj"][l])], axis=1).reshape(-1, P, P))
        put(cut(a["w_out"][l]).reshape(-1, P, P))
        if l == 0:
            for h in range(2):
                c = slice(h * FF, (h + 1) * FF)
                ffn(a["dense_w_gate"][0][:, c], a["dense_w_up"][0][:, c], a["dense_w_down"][0][c])
        else:
            for e in range(EXPERTS):
                ffn(a["moe_w_gate"][0, e], a["moe_w_up"][0, e], a["moe_w_down"][0, e], moe_down_order())
    assert at[0] == UNITS
    arrays["W"] = W

    cols = np.empty((P, NCOL), np.float32)
    for name, key in (("mix_norm", "mix_norm"), ("ffn_norm", "ffn_norm"), ("merge_bias", "merge_bias"),
                      ("conv_w", "lru_conv_w"), ("conv_b", "lru_conv_b"), ("b_r", "lru_b_rgate"),
                      ("b_i", "lru_b_igate"), ("lam", "lru_lambda"), ("b_glu", "s5_b_glu")):
        c, n = COLS[name]
        cols[:, c:c + LAYERS * n] = a[key].reshape(-1, P).T
    c, n = COLS["s5_d"]
    cols[:, c:c + LAYERS * n] = np.tile(a["s5_d"].reshape(SP2, GC).T, (L, 1))
    arrays["cols"] = cols

    lam = [np.tile(a[k].reshape(SP2, GS).T, (2, 1)) for k in ("s5_lambda_re", "s5_lambda_im")]
    dt = np.broadcast_to(a["s5_log_dt"].reshape(1, SP2), (P, SP2))
    arrays["s5p"] = np.stack([*lam, dt], axis=1)
    br, bi = (a[k].transpose(0, 2, 1, 3) for k in ("s5_b_re", "s5_b_im"))
    cr, ci = (a[k].transpose(0, 3, 1, 2) for k in ("s5_c_re", "s5_c_im"))
    both = [np.concatenate(p, axis=1) for p in ((br, bi), (bi, br), (cr, ci), (ci, cr))]
    m = np.stack(both, axis=2).reshape(LAYERS, P, 4, NB, GB * GC)
    arrays["s5m"] = m.transpose(0, 3, 1, 2, 4)

    wr, wi = (a[k].reshape(LAYERS, MT, P, LRU_WB).transpose(0, 2, 1, 3) for k in ("lru_w_rgate", "lru_w_igate"))
    arrays["wg"] = np.stack([wr, wi], axis=2)
    arrays["rw"] = tiles(a["router_w"][0])
    arrays["rb"] = np.broadcast_to(a["router_b"], (P, EXPERTS))
    arrays["fg"] = np.broadcast_to(a["final_norm"], (TOK, D))
    return {"in_" + k: np.ascontiguousarray(v) for k, v in arrays.items()}


def kernel(**inputs):
    import numpy as np
    from concourse import bacc
    from concourse.bass_utils import run_bass_kernel_spmd

    arrays = layout(inputs)
    nc = bacc.Bacc("TRN2", target_bir_lowering=False, num_devices=1)
    args = [nc.dram_tensor(k, v.shape, F32, kind="ExternalInput").ap() for k, v in arrays.items()]
    out = nc.dram_tensor("out_0", (T, D), F32, kind="ExternalOutput").ap()
    scratch = [nc.dram_tensor(n, s, F32).ap() for n, s in
               (("hs_d", (P, DK, T)), ("u_d", (GROUPS, GC, L, NC)), ("y_d", (GROUPS, GC, L, NC)),
                ("xg_d", (SLOTS, D)), ("yg_d", (SLOTS, D)))]
    build(nc, *args, out, *scratch)
    r = run_bass_kernel_spmd(nc, [arrays], core_ids=[0]).results[0]["out_0"]
    return np.ascontiguousarray(r[None, META:])
```
